# Optimizing a Trainium2 kernel written in Bass

```python
import jax, jax.numpy as jnp
from jax import lax
import numpy as np
import math
import jax
import jax.numpy as jnp

D_MODEL = 1024
BATCH = 1
SEQ = 512
DEPTH = 2

N_EVEN = (DEPTH + 1) // 2
N_ODD = DEPTH // 2

LRU_WIDTH = D_MODEL // 2
LRU_HEADS = 8
LRU_HEAD_DIM = LRU_WIDTH // LRU_HEADS
LRU_CONV = 4
LRU_C = 8.0
LRU_MIN_RAD = 0.9
LRU_MAX_RAD = 0.999
SC_WIDTH = D_MODEL // 2
SC_CONV = 3
EVEN_IN = 2 * LRU_WIDTH + 3 * SC_WIDTH

SGU_WIDTH = D_MODEL // 2
SGU_HEADS = 8
SGU_HEAD_DIM = SGU_WIDTH // SGU_HEADS
CHUNK = 128
FOX_HEADS = 8
FOX_HEAD_DIM = 64
FOX_WIDTH = FOX_HEADS * FOX_HEAD_DIM
Q_BLOCK = 128
ODD_IN = 2 * SGU_WIDTH + 3 * FOX_WIDTH + FOX_HEADS

D_FF = 2816
FFN_CONV = 3
EPS = 1e-6


def rmsnorm(x, g):
    xf = x.astype(jnp.float32)
    y = xf * lax.rsqrt(jnp.mean(xf * xf, axis=-1, keepdims=True) + EPS)
    return (y * g.astype(jnp.float32)).astype(x.dtype)

def causal_depthwise_conv(x, w, b):
    k_width, ch = w.shape
    out = lax.conv_general_dilated(
        x, w[:, None, :].astype(x.dtype), window_strides=(1,),
        padding=[(k_width - 1, 0)], dimension_numbers=('NWC', 'WIO', 'NWC'),
        feature_group_count=ch)
    return out + b.astype(x.dtype)

def rg_lru(x, w_a, b_a, w_x, b_x, lam):
    bsz, s, w = x.shape
    xh = x.reshape(bsz, s, LRU_HEADS, LRU_HEAD_DIM)
    r = jax.nn.sigmoid((jnp.einsum('bshi,hij->bshj', xh, w_a).reshape(bsz, s, w) + b_a).astype(jnp.float32))
    i = jax.nn.sigmoid((jnp.einsum('bshi,hij->bshj', xh, w_x).reshape(bsz, s, w) + b_x).astype(jnp.float32))
    log_a = -LRU_C * r * jax.nn.softplus(-lam.astype(jnp.float32))
    a = jnp.exp(log_a)
    u = jnp.sqrt(-jnp.expm1(2.0 * log_a)) * (i * x.astype(jnp.float32))

    def combine(left, right):
        a_l, h_l = left
        a_r, h_r = right
        return a_l * a_r, a_r * h_l + h_r

    _, h = lax.associative_scan(combine, (a, u), axis=1)
    return h.astype(x.dtype)

def even_mixer(x, w_in, lru_conv_w, lru_conv_b, lru_wa, lru_ba, lru_wx, lru_bx, lru_lambda,
               sconv_w, sconv_b, w_out):
    p = x @ w_in
    W, C = LRU_WIDTH, SC_WIDTH
    xa, ga, c_pre, b_post, vb = jnp.split(p, [W, 2 * W, 2 * W + C, 2 * W + 2 * C], axis=-1)
    xa = causal_depthwise_conv(xa, lru_conv_w, lru_conv_b)
    ya = rg_lru(xa, lru_wa, lru_ba, lru_wx, lru_bx, lru_lambda) * jax.nn.gelu(ga)
    yb = b_post * causal_depthwise_conv(c_pre * vb, sconv_w, sconv_b)
    return jnp.concatenate([ya, yb], axis=-1) @ w_out

def chunked_spatial_gating(u, g, g_norm, w_s, b_s):
    bsz, s, _ = u.shape
    n_chunks = s // CHUNK
    gv = rmsnorm(g.reshape(bsz, s, SGU_HEADS, SGU_HEAD_DIM), g_norm.reshape(SGU_HEADS, SGU_HEAD_DIM))
    gv = gv.reshape(bsz, n_chunks, CHUNK, SGU_HEADS, SGU_HEAD_DIM)
    w_causal = jnp.tril(w_s)
    mixed = jnp.einsum('gts,bnsgc->bntgc', w_causal, gv) + b_s.T[:, :, None]
    return u * mixed.reshape(bsz, s, SGU_WIDTH)

def forgetting_attention(q, k, v, f_logit, b_f):
    bsz, s, _ = q.shape
    nb = s // Q_BLOCK

    def heads(t):
        return t.reshape(bsz, s, FOX_HEADS, FOX_HEAD_DIM).transpose(0, 2, 1, 3)

    q, k, v = heads(q), heads(k), heads(v)
    log_f = jax.nn.log_sigmoid(f_logit.astype(jnp.float32) + b_f.astype(jnp.float32))
    c = jnp.cumsum(log_f, axis=1).transpose(0, 2, 1)
    q_blocks = q.reshape(bsz, FOX_HEADS, nb, Q_BLOCK, FOX_HEAD_DIM).transpose(2, 0, 1, 3, 4)
    c_blocks = c.reshape(bsz, FOX_HEADS, nb, Q_BLOCK).transpose(2, 0, 1, 3)
    starts = jnp.arange(nb) * Q_BLOCK
    key_pos = jnp.arange(s)
    scale = FOX_HEAD_DIM ** -0.5

    def block(args):
        qb, cb, start = args
        logits = (jnp.einsum('bhqd,bhkd->bhqk', qb, k).astype(jnp.float32) * scale
                  + cb[..., None] - c[:, :, None, :])
        q_pos = start + jnp.arange(Q_BLOCK)
        logits = jnp.where(key_pos[None, :] <= q_pos[:, None], logits, -jnp.inf)
        p = jax.nn.softmax(logits, axis=-1)
        return jnp.einsum('bhqk,bhkd->bhqd', p.astype(v.dtype), v)

    out = lax.map(block, (q_blocks, c_blocks, starts))
    return out.transpose(1, 0, 3, 2, 4).reshape(bsz, s, FOX_WIDTH)

def odd_mixer(x, w_in, sgu_norm, sgu_w, sgu_b, fox_bf, w_out):
    p = x @ w_in
    Z, F = 2 * SGU_WIDTH, FOX_WIDTH
    z, q, k, v, f = jnp.split(p, [Z, Z + F, Z + 2 * F, Z + 3 * F], axis=-1)
    z = jax.nn.gelu(z)
    u, g = jnp.split(z, 2, axis=-1)
    yc = chunked_spatial_gating(u, g, sgu_norm, sgu_w, sgu_b)
    yd = forgetting_attention(q, k, v, f, fox_bf)
    return jnp.concatenate([yc, yd], axis=-1) @ w_out

def conv_glu_ffn(x, w_up, conv_w, conv_b, w_down):
    h = causal_depthwise_conv(x @ w_up, conv_w, conv_b)
    gate, val = jnp.split(h, 2, axis=-1)
    return (jax.nn.silu(gate) * val) @ w_down

def first_inputs(seed: int = 0) -> dict:
    key = jax.random.key(seed)
    ks = jax.random.split(key, 32)
    f32 = jnp.float32

    def dense(k, shape, fan_in):
        return jax.random.normal(k, shape, f32) * fan_in ** -0.5

    def gain(k, shape):
        return 1.0 + 0.05 * jax.random.normal(k, shape, f32)

    def bias(k, shape):
        return 0.1 * jax.random.normal(k, shape, f32)

    a_c = jax.random.uniform(ks[9], (N_EVEN, LRU_WIDTH), f32, LRU_MIN_RAD, LRU_MAX_RAD)
    s_base = a_c ** (1.0 / LRU_C)
    lru_lambda = jnp.log(s_base) - jnp.log1p(-s_base)

    return {
        "x": jax.random.normal(ks[0], (BATCH, SEQ, D_MODEL), f32),
        "mix0_norm": gain(ks[1], (N_EVEN, D_MODEL)),
        "mix0_w_in": dense(ks[2], (N_EVEN, D_MODEL, EVEN_IN), D_MODEL),
        "lru_conv_w": dense(ks[3], (N_EVEN, LRU_CONV, LRU_WIDTH), LRU_CONV),
        "lru_conv_b": bias(ks[4], (N_EVEN, LRU_WIDTH)),
        "lru_wa": dense(ks[5], (N_EVEN, LRU_HEADS, LRU_HEAD_DIM, LRU_HEAD_DIM), LRU_HEAD_DIM),
        "lru_ba": bias(ks[6], (N_EVEN, LRU_WIDTH)),
        "lru_wx": dense(ks[7], (N_EVEN, LRU_HEADS, LRU_HEAD_DIM, LRU_HEAD_DIM), LRU_HEAD_DIM),
        "lru_bx": bias(ks[8], (N_EVEN, LRU_WIDTH)),
        "lru_lambda": lru_lambda,
        "sconv_w": dense(ks[10], (N_EVEN, SC_CONV, SC_WIDTH), SC_CONV),
        "sconv_b": bias(ks[11], (N_EVEN, SC_WIDTH)),
        "mix0_w_out": dense(ks[12], (N_EVEN, LRU_WIDTH + SC_WIDTH, D_MODEL), LRU_WIDTH + SC_WIDTH),
        "mix1_norm": gain(ks[13], (N_ODD, D_MODEL)),
        "mix1_w_in": dense(ks[14], (N_ODD, D_MODEL, ODD_IN), D_MODEL),
        "sgu_norm": gain(ks[15], (N_ODD, SGU_WIDTH)),
        "sgu_w": dense(ks[16], (N_ODD, SGU_HEADS, CHUNK, CHUNK), CHUNK),
        "sgu_b": 1.0 + bias(ks[17], (N_ODD, SGU_HEADS, CHUNK)),
        "fox_bf": bias(ks[18], (N_ODD, FOX_HEADS)),
        "mix1_w_out": dense(ks[19], (N_ODD, SGU_WIDTH + FOX_WIDTH, D_MODEL), SGU_WIDTH + FOX_WIDTH),
        "ffn_norm": gain(ks[20], (DEPTH, D_MODEL)),
        "ffn_up": dense(ks[21], (DEPTH, D_MODEL, 2 * D_FF), D_MODEL),
        "ffn_conv_w": dense(ks[22], (DEPTH, FFN_CONV, 2 * D_FF), FFN_CONV),
        "ffn_conv_b": bias(ks[23], (DEPTH, 2 * D_FF)),
        "ffn_down": dense(ks[24], (DEPTH, D_FF, D_MODEL), D_FF),
        "final_norm": gain(ks[25], (D_MODEL,)),
    }

def first_block(x, mix0_norm, mix0_w_in, lru_conv_w, lru_conv_b, lru_wa, lru_ba, lru_wx, lru_bx,
              lru_lambda, sconv_w, sconv_b, mix0_w_out, mix1_norm, mix1_w_in, sgu_norm, sgu_w,
              sgu_b, fox_bf, mix1_w_out, ffn_norm, ffn_up, ffn_conv_w, ffn_conv_b, ffn_down,
              final_norm):
    h = x
    for layer in range(DEPTH):
        i = layer // 2
        if layer % 2 == 0:
            h = h + even_mixer(rmsnorm(h, mix0_norm[i]), mix0_w_in[i], lru_conv_w[i], lru_conv_b[i],
                               lru_wa[i], lru_ba[i], lru_wx[i], lru_bx[i], lru_lambda[i],
                               sconv_w[i], sconv_b[i], mix0_w_out[i])
        else:
            h = h + odd_mixer(rmsnorm(h, mix1_norm[i]), mix1_w_in[i], sgu_norm[i], sgu_w[i],
                              sgu_b[i], fox_bf[i], mix1_w_out[i])
        h = h + conv_glu_ffn(rmsnorm(h, ffn_norm[layer]), ffn_up[layer], ffn_conv_w[layer],
                             ffn_conv_b[layer], ffn_down[layer])
    return rmsnorm(h, final_norm)


DEPTH_2 = 1

GRID_W = 64
CTX_LEN = 256
N_MOD = 6

GDN_HEADS = 8
GDN_DK = 128
GDN_DV = 128
GDN_CONV = 5
GDN_CHUNK = 64
DT_MIN = 0.001
DT_MAX = 0.1
GDN_QKV_W = GDN_HEADS * (2 * GDN_DK + GDN_DV)

MLA_HEADS = 8
MLA_Q_LORA = 384
MLA_KV_LORA = 256
MLA_NOPE = 128
MLA_ROPE = 64
MLA_V = 128
MLA_QK = MLA_NOPE + MLA_ROPE
ROPE_THETA = 10000.0
ROPE_AXIS = MLA_ROPE // 2
ROPE_FREQS = ROPE_AXIS // 2

D_FF_2 = 4 * D_MODEL
N_BRANCH = 2

IN_SPLITS = (GDN_QKV_W, GDN_HEADS * GDN_DV, 2 * GDN_HEADS, 2 * GDN_HEADS,
             MLA_Q_LORA, MLA_KV_LORA, MLA_ROPE, N_BRANCH * D_MODEL)
IN_COLS = sum(IN_SPLITS)


def _rms(x, w):
    xf = x.astype(jnp.float32)
    y = xf * lax.rsqrt(jnp.mean(xf * xf, axis=-1, keepdims=True) + EPS)
    return y.astype(x.dtype) * w

def _l2norm(x):
    xf = x.astype(jnp.float32)
    return (xf * lax.rsqrt(jnp.sum(xf * xf, axis=-1, keepdims=True) + EPS)).astype(x.dtype)

def _modulate(xn, shift, scale):
    return xn * (1.0 + scale) + shift

def _split_in(proj):
    offsets = np.cumsum(IN_SPLITS)[:-1].tolist()
    return jnp.split(proj, offsets, axis=-1)

def _centred_conv(x, w):
    k_w = w.shape[0]
    t = x.shape[1]
    p = k_w // 2
    xp = jnp.pad(x, ((0, 0), (p, p), (0, 0)))
    return sum(xp[:, i:i + t] * w[i] for i in range(k_w))

def _gdn_inputs(qkv, beta_logit, decay_logit, conv_w, a_log, dt_bias):
    B, T, _ = qkv.shape
    qkv = jax.nn.silu(_centred_conv(qkv, conv_w))
    q, k, v = jnp.split(qkv, [GDN_HEADS * GDN_DK, 2 * GDN_HEADS * GDN_DK], axis=-1)
    q = _l2norm(q.reshape(B, T, GDN_HEADS, GDN_DK))
    k = _l2norm(k.reshape(B, T, GDN_HEADS, GDN_DK))
    v = v.reshape(B, T, GDN_HEADS, GDN_DV)
    beta = jax.nn.sigmoid(beta_logit.astype(jnp.float32)).reshape(B, T, 2, GDN_HEADS)
    g = -jnp.exp(a_log.astype(jnp.float32)) * jax.nn.softplus(
        decay_logit.astype(jnp.float32).reshape(B, T, 2, GDN_HEADS) + dt_bias.astype(jnp.float32))
    return q, k, v, g, beta

def _chunk_gated_delta(q, k, v, g, beta, state0):
    in_dtype = v.dtype
    B, T, H, DK = q.shape
    C = GDN_CHUNK
    n = T // C

    def chunks(t):
        return t.astype(jnp.float32).reshape(B, n, C, H, -1).transpose(0, 3, 1, 2, 4)

    q = chunks(q) * (DK ** -0.5)
    k = chunks(k)
    v = chunks(v)
    gc = jnp.cumsum(chunks(g[..., None])[..., 0], axis=-1)
    beta = chunks(beta[..., None])
    tri = jnp.tril(jnp.ones((C, C), dtype=bool))
    strict = jnp.tril(jnp.ones((C, C), dtype=bool), -1)
    diff = gc[..., :, None] - gc[..., None, :]
    decay = jnp.where(tri, jnp.exp(jnp.where(tri, diff, 0.0)), 0.0)
    kb = k * beta
    vb = v * beta
    a_mat = jnp.where(strict, jnp.einsum('bhnid,bhnjd->bhnij', kb, k) * decay, 0.0)
    eye = jnp.eye(C, dtype=jnp.float32)
    t_mat = lax.linalg.triangular_solve(eye + a_mat, jnp.broadcast_to(eye, a_mat.shape),
                                        left_side=True, lower=True, unit_diagonal=True)
    u = jnp.einsum('bhnij,bhnjd->bhnid', t_mat, vb)
    w = jnp.einsum('bhnij,bhnjd->bhnid', t_mat, kb * jnp.exp(gc)[..., None])
    qk = jnp.where(tri, jnp.einsum('bhnid,bhnjd->bhnij', q, k) * decay, 0.0)
    q_dec = q * jnp.exp(gc)[..., None]
    k_dec = k * jnp.exp(gc[..., -1:] - gc)[..., None]
    g_last = jnp.exp(gc[..., -1])
    xs = tuple(jnp.moveaxis(t, 2, 0) for t in (u, w, qk, q_dec, k_dec, g_last))

    def step(s, inp):
        u_i, w_i, qk_i, qd_i, kd_i, gl_i = inp
        v_new = u_i - jnp.einsum('bhcd,bhde->bhce', w_i, s)
        o_i = jnp.einsum('bhcd,bhde->bhce', qd_i, s) + jnp.einsum('bhcj,bhje->bhce', qk_i, v_new)
        s = s * gl_i[..., None, None] + jnp.einsum('bhcd,bhce->bhde', kd_i, v_new)
        return s, o_i

    s_final, o = lax.scan(step, state0.astype(jnp.float32), xs)
    o = jnp.moveaxis(o, 0, 2).transpose(0, 2, 3, 1, 4).reshape(B, T, H, -1)
    return o.astype(in_dtype), s_final

def _bidirectional_gdn(q, k, v, g, beta, s0_fwd, s0_bwd):
    o_f, s_f = _chunk_gated_delta(q, k, v, g[:, :, 0], beta[:, :, 0], s0_fwd)
    rev = lambda t: jnp.flip(t, axis=1)
    o_b, s_b = _chunk_gated_delta(rev(q), rev(k), rev(v), rev(g[:, :, 1]), rev(beta[:, :, 1]), s0_bwd)
    return o_f + rev(o_b), s_f, s_b

def _gdn_out(o, z, w_norm):
    B, T = o.shape[:2]
    y = _rms(o, w_norm) * jax.nn.silu(z.reshape(B, T, GDN_HEADS, GDN_DV))
    return y.reshape(B, T, GDN_HEADS * GDN_DV)

def _axial_rope(x, row, col):
    inv = ROPE_THETA ** (-jnp.arange(ROPE_FREQS, dtype=jnp.float32) / ROPE_FREQS)

    def rotate(seg, pos):
        ang = pos[:, None] * inv
        cos = jnp.cos(ang)[None, :, None, :].astype(seg.dtype)
        sin = jnp.sin(ang)[None, :, None, :].astype(seg.dtype)
        x1, x2 = seg[..., :ROPE_FREQS], seg[..., ROPE_FREQS:]
        return jnp.concatenate([x1 * cos - x2 * sin, x2 * cos + x1 * sin], axis=-1)

    return jnp.concatenate([rotate(x[..., :ROPE_AXIS], row), rotate(x[..., ROPE_AXIS:], col)], axis=-1)

def _mla_qkv(cq, ckv, k_rope, q_a_norm, kv_a_norm, w_uq, w_ukv, q_norm, k_norm, pos):
    B, T, _ = cq.shape
    q = (_rms(cq, q_a_norm) @ w_uq).reshape(B, T, MLA_HEADS, MLA_QK)
    kv = (_rms(ckv, kv_a_norm) @ w_ukv).reshape(B, T, MLA_HEADS, MLA_NOPE + MLA_V)
    k_nope, v = kv[..., :MLA_NOPE], kv[..., MLA_NOPE:]
    k = jnp.concatenate([k_nope, jnp.broadcast_to(k_rope[:, :, None, :], (B, T, MLA_HEADS, MLA_ROPE))], axis=-1)
    q = _rms(q, q_norm)
    k = _rms(k, k_norm)
    if pos is not None:
        row, col = pos
        q = jnp.concatenate([q[..., :MLA_NOPE], _axial_rope(q[..., MLA_NOPE:], row, col)], axis=-1)
        k = jnp.concatenate([k[..., :MLA_NOPE], _axial_rope(k[..., MLA_NOPE:], row, col)], axis=-1)
    return q, k, v

def _softmax_attend(q, k, v):
    s = jnp.einsum('bqhd,bkhd->bhqk', q, k).astype(jnp.float32) * (MLA_QK ** -0.5)
    p = jax.nn.softmax(s, axis=-1).astype(v.dtype)
    return jnp.einsum('bhqk,bkhd->bqhd', p, v)

def _blockwise_attention(q, k, v):
    B, T, H, _ = q.shape
    nb = T // Q_BLOCK
    qb = jnp.moveaxis(q.reshape(B, nb, Q_BLOCK, H, -1), 1, 0)
    o = lax.map(lambda qq: _softmax_attend(qq, k, v), qb)
    return jnp.moveaxis(o, 0, 1).reshape(B, T, H * v.shape[-1])

def _merge(o_gdn, o_mla, gate_logits, w_branch_gdn, w_branch_mla, w_out):
    g_gdn, g_mla = jnp.split(gate_logits, N_BRANCH, axis=-1)
    y = jax.nn.sigmoid(g_gdn) * (o_gdn @ w_branch_gdn) + jax.nn.sigmoid(g_mla) * (o_mla @ w_branch_mla)
    return y @ w_out

def _sq_relu_mlp(h, w1, w2):
    return jnp.square(jax.nn.relu(h @ w1)) @ w2

def second_inputs(seed: int = 0) -> dict:
    key = jax.random.key(seed)
    ks = jax.random.split(key, 24)
    D = D_MODEL

    def nrm(k, shape, scale):
        return jax.random.normal(k, shape, jnp.float32) * scale

    def gain(k, n):
        return 1.0 + nrm(k, (DEPTH_2, n), 0.02)

    dt = jnp.exp(jax.random.uniform(ks[9], (DEPTH_2, 2, GDN_HEADS), jnp.float32,
                                    minval=math.log(DT_MIN), maxval=math.log(DT_MAX)))
    return {
        'x': nrm(ks[0], (BATCH, SEQ, D), 1.0),
        'c': nrm(ks[1], (BATCH, D), 1.0),
        'ctx': nrm(ks[2], (BATCH, CTX_LEN, D), 1.0),
        'c_ctx': nrm(ks[3], (D,), 1.0),
        'w_mod': nrm(ks[4], (DEPTH_2, D, N_MOD * D), D ** -0.5),
        'b_mod': nrm(ks[5], (DEPTH_2, N_MOD * D), 0.01),
        'norm_attn': gain(ks[6], D),
        'norm_mlp': gain(ks[7], D),
        'w_in': nrm(ks[8], (DEPTH_2, D, IN_COLS), D ** -0.5),
        'conv_qkv': nrm(ks[10], (DEPTH_2, GDN_CONV, GDN_QKV_W), GDN_CONV ** -0.5),
        'gdn_a_log': jnp.log(jax.random.uniform(ks[11], (DEPTH_2, 2, GDN_HEADS), jnp.float32, minval=1.0, maxval=16.0)),
        'gdn_dt_bias': dt + jnp.log(-jnp.expm1(-dt)),
        'gdn_out_norm': gain(ks[12], GDN_DV),
        'mla_q_a_norm': gain(ks[13], MLA_Q_LORA),
        'mla_kv_a_norm': gain(ks[14], MLA_KV_LORA),
        'w_uq': nrm(ks[15], (DEPTH_2, MLA_Q_LORA, MLA_HEADS * MLA_QK), MLA_Q_LORA ** -0.5),
        'w_ukv': nrm(ks[16], (DEPTH_2, MLA_KV_LORA, MLA_HEADS * (MLA_NOPE + MLA_V)), MLA_KV_LORA ** -0.5),
        'q_norm': gain(ks[17], MLA_QK),
        'k_norm': gain(ks[18], MLA_QK),
        'w_branch_gdn': nrm(ks[19], (DEPTH_2, GDN_HEADS * GDN_DV, D), (GDN_HEADS * GDN_DV) ** -0.5),
        'w_branch_mla': nrm(ks[20], (DEPTH_2, MLA_HEADS * MLA_V, D), (MLA_HEADS * MLA_V) ** -0.5),
        'w_out': nrm(ks[21], (DEPTH_2, D, D), D ** -0.5),
        'w_mlp_in': nrm(ks[22], (DEPTH_2, D, D_FF_2), D ** -0.5),
        'w_mlp_out': nrm(ks[23], (DEPTH_2, D_FF_2, D), 0.5 * D_FF_2 ** -0.5),
    }

def second_block(x, c, ctx, c_ctx, w_mod, b_mod, norm_attn, norm_mlp, w_in, conv_qkv, gdn_a_log, gdn_dt_bias,
              gdn_out_norm, mla_q_a_norm, mla_kv_a_norm, w_uq, w_ukv, q_norm, k_norm, w_branch_gdn,
              w_branch_mla, w_out, w_mlp_in, w_mlp_out):
    B, L, _ = x.shape
    lc = ctx.shape[1]
    rows = L // GRID_W
    row = jnp.repeat(jnp.arange(rows, dtype=jnp.float32), GRID_W)
    col = jnp.tile(jnp.arange(GRID_W, dtype=jnp.float32), rows)
    silu_c = jax.nn.silu(c)[:, None, :]
    silu_cc = jax.nn.silu(c_ctx)
    zero_state = jnp.zeros((B, GDN_HEADS, GDN_DK, GDN_DV), jnp.float32)

    for l in range(DEPTH_2):
        mod_x = jnp.split(silu_c @ w_mod[l] + b_mod[l], N_MOD, axis=-1)
        mod_c = jnp.split(silu_cc @ w_mod[l] + b_mod[l], N_MOD, axis=-1)

        h = _modulate(_rms(x, norm_attn[l]), mod_x[0], mod_x[1])
        hc = _modulate(_rms(ctx, norm_attn[l]), mod_c[0], mod_c[1])
        qkv, z, beta_lg, decay_lg, cq, ckv, k_rope, gates = _split_in(h @ w_in[l])
        qkv_c, z_c, beta_lg_c, decay_lg_c, cq_c, ckv_c, k_rope_c, gates_c = _split_in(hc @ w_in[l])

        qa_c, ka_c, va_c, g_c, beta_c = _gdn_inputs(qkv_c, beta_lg_c, decay_lg_c, conv_qkv[l], gdn_a_log[l], gdn_dt_bias[l])
        o_gdn_c, s_fwd, s_bwd = _bidirectional_gdn(qa_c, ka_c, va_c, g_c, beta_c, zero_state, zero_state)
        qa, ka, va, g, beta = _gdn_inputs(qkv, beta_lg, decay_lg, conv_qkv[l], gdn_a_log[l], gdn_dt_bias[l])
        o_gdn, _, _ = _bidirectional_gdn(qa, ka, va, g, beta, s_fwd, s_bwd)

        qb, kb, vb = _mla_qkv(cq, ckv, k_rope, mla_q_a_norm[l], mla_kv_a_norm[l], w_uq[l], w_ukv[l],
                              q_norm[l], k_norm[l], (row, col))
        qb_c, kb_c, vb_c = _mla_qkv(cq_c, ckv_c, k_rope_c, mla_q_a_norm[l], mla_kv_a_norm[l], w_uq[l], w_ukv[l],
                                    q_norm[l], k_norm[l], None)
        o_mla = _blockwise_attention(qb, jnp.concatenate([kb_c, kb], axis=1), jnp.concatenate([vb_c, vb], axis=1))

        x = x + mod_x[2] * _merge(_gdn_out(o_gdn, z, gdn_out_norm[l]), o_mla, gates,
                                  w_branch_gdn[l], w_branch_mla[l], w_out[l])
        x = x + mod_x[5] * _sq_relu_mlp(_modulate(_rms(x, norm_mlp[l]), mod_x[3], mod_x[4]), w_mlp_in[l], w_mlp_out[l])

        if l < DEPTH_2 - 1:
            o_mla_c = _softmax_attend(qb_c, kb_c, vb_c).reshape(B, lc, MLA_HEADS * MLA_V)
            ctx = ctx + mod_c[2] * _merge(_gdn_out(o_gdn_c, z_c, gdn_out_norm[l]), o_mla_c, gates_c,
                                          w_branch_gdn[l], w_branch_mla[l], w_out[l])
            ctx = ctx + mod_c[5] * _sq_relu_mlp(_modulate(_rms(ctx, norm_mlp[l]), mod_c[3], mod_c[4]),
                                                w_mlp_in[l], w_mlp_out[l])
    return x


def setup_inputs(seed=0):
    out = dict(first_inputs(seed))
    for name, value in second_inputs(seed + 1).items():
        if name != "x":
            out[name + "_2"] = value
    return out


def reference(
    x, mix0_norm, mix0_w_in, lru_conv_w, lru_conv_b, lru_wa, lru_ba, lru_wx, lru_bx, lru_lambda,
    sconv_w, sconv_b, mix0_w_out, mix1_norm, mix1_w_in, sgu_norm, sgu_w, sgu_b, fox_bf,
    mix1_w_out, ffn_norm, ffn_up, ffn_conv_w, ffn_conv_b, ffn_down, final_norm, c_2, ctx_2,
    c_ctx_2, w_mod_2, b_mod_2, norm_attn_2, norm_mlp_2, w_in_2, conv_qkv_2, gdn_a_log_2,
    gdn_dt_bias_2, gdn_out_norm_2, mla_q_a_norm_2, mla_kv_a_norm_2, w_uq_2, w_ukv_2, q_norm_2,
    k_norm_2, w_branch_gdn_2, w_branch_mla_2, w_out_2, w_mlp_in_2, w_mlp_out_2,
):
    x = first_block(
        x, mix0_norm, mix0_w_in, lru_conv_w, lru_conv_b, lru_wa, lru_ba, lru_wx, lru_bx,
        lru_lambda, sconv_w, sconv_b, mix0_w_out, mix1_norm, mix1_w_in, sgu_norm, sgu_w, sgu_b,
        fox_bf, mix1_w_out, ffn_norm, ffn_up, ffn_conv_w, ffn_conv_b, ffn_down, final_norm,
    )
    return second_block(
        x, c_2, ctx_2, c_ctx_2, w_mod_2, b_mod_2, norm_attn_2, norm_mlp_2, w_in_2, conv_qkv_2,
        gdn_a_log_2, gdn_dt_bias_2, gdn_out_norm_2, mla_q_a_norm_2, mla_kv_a_norm_2, w_uq_2,
        w_ukv_2, q_norm_2, k_norm_2, w_branch_gdn_2, w_branch_mla_2, w_out_2, w_mlp_in_2,
        w_mlp_out_2,
    )


_drawn_inputs = setup_inputs


def setup_inputs(seed=0):
    import zlib

    import numpy as np

    out = dict(_drawn_inputs(seed))
    spreads = {}
    factors = {'lru_ba': 7.205,
     'lru_bx': 4.539,
     'sgu_norm': 5.094,
     'fox_bf': 4.632,
     'ctx_2': 3.003,
     'b_mod_2': 4.4,
     'norm_attn_2': 8.0,
     'norm_mlp_2': 27.013,
     'gdn_out_norm_2': 21.507,
     'mla_q_a_norm_2': 22.512,
     'mla_kv_a_norm_2': 28.595,
     'q_norm_2': 8.0,
     'k_norm_2': 21.948}
    for name, (base, spread) in spreads.items():
        noise = np.random.default_rng([zlib.crc32(name.encode()), seed]).standard_normal(out[name].shape)
        drawn = base * np.exp(spread * noise) if base else spread * noise
        out[name] = jnp.asarray(drawn.astype(out[name].dtype))
    for name, factor in factors.items():
        out[name] = (out[name] * factor).astype(out[name].dtype)
    return out
```

```python
from contextlib import ExitStack

import numpy as np

import concourse.bass as bass
from concourse import mybir

F32, F32R, BF16, U32 = mybir.dt.float32, mybir.dt.float32r, mybir.dt.bfloat16, mybir.dt.uint32
ACT = mybir.ActivationFunctionType
ALU = mybir.AluOpType
AX = mybir.AxisListType

P = 128
T = 512
TC = 256
D = 1024
KD = D // P
EPS = 1e-6
FF_HALF = 11
SLOT = 2048
ARENA = 31744
SPLIT = 24576
TAIL = 1536


class Signal:

    def __init__(self, nc, ctx, name):
        self.sem = ctx.enter_context(nc.semaphore(name))
        self.base = 0
        self.total = 0

    def up(self, amount=1):
        self.total += amount
        return self.sem

    def count(self, n):
        return n + self.base


class Chain:

    def __init__(self, nc, ctx, name):
        self.sem = ctx.enter_context(nc.semaphore(name))
        self.n, self.loop, self.j = 0, None, 0

    def enter(self, i, per_turn):
        self.loop, self.j = (i, per_turn), 0

    def leave(self, turns):
        assert self.j == self.loop[1], (self.j, self.loop[1])
        self.n += turns * self.loop[1]
        self.loop, self.j = None, 0

    def up(self):
        if self.loop:
            self.j += 1
        else:
            self.n += 1
        return self.sem

    def now(self):
        return self.n if not self.loop else self.loop[0] * self.loop[1] + (self.n + self.j)


class Segment:

    def __init__(self, src, n, k, tiles, cols=None):
        self.src, self.n, self.k, self.tiles = src, n, k, tiles
        self.cols = cols or tiles * P
        self.size = k * self.cols
        self.g0 = None


class Unit:
    def __init__(self, seg, u, parity, i, turns):
        self.seg, self.u, self.turns = seg, u, turns
        self.slot = (seg.g0 + parity) % 2
        self.use = (seg.g0 + parity) // 2 + i
        self.g = u + seg.g0


class Machine:

    def __init__(self, nc, ctx):
        self.nc, self.ctx = nc, ctx
        self.signals = {}
        sb = lambda name, shape, dt=F32: ctx.enter_context(nc.sbuf_tensor(name, shape, dt))
        self.h = sb("h", [P, KD, T])
        self.rounded_names = {}
        for name, shape, split in (("ring", [P, 3, 2, SLOT], 6 * SLOT), ("arena", [P, ARENA], SPLIT)):
            with nc.sbuf_tensor(name, shape, F32) as plain:
                pass
            rounded = sb(name + "_rounded", [P, split], F32R)
            self.rounded_names[name] = rounded
            if name == "ring":
                self.ring = plain
            else:
                sb("arena_rest", [P, ARENA - SPLIT])
                self.arena = plain
        self.tail = sb("tail", [P, TAIL])
        self.ident = sb("ident", [P, P])
        self.ones = sb("ones", [P, 1])
        self.cum = sb("cum", [P, 2, P])
        self.bar = sb("bar", [P, 2, P])
        self.lev = sb("lev", [P, 2, 7, P], BF16)
        self.small = sb("small", [P, 288])
        self.gcols = sb("gcols", [P, 6, 96])
        self.mods = sb("mods", [P, 48, 2])
        self.psum = ctx.enter_context(nc.psum_tensor("psum", [P, 8, 512], F32))
        self.raw_full = [ctx.enter_context(nc.semaphore(f"raw_full{s}")) for s in range(2)]
        self.hi_done = ctx.enter_context(nc.semaphore("hi_done"))
        self.lo_done = ctx.enter_context(nc.semaphore("lo_done"))
        self.vchain = Chain(nc, ctx, "vector_order")
        self.achain = Chain(nc, ctx, "scalar_order")
        self.gchain = Chain(nc, ctx, "gpsimd_order")
        self.segments, self.units = [], []

    def sig(self, name):
        if name not in self.signals:
            self.signals[name] = Signal(self.nc, self.ctx, name)
        return self.signals[name]

    def sem(self, name):
        return self.sig(name).sem

    def count(self, name, n):
        return self.sig(name).count(n)

    def up(self, name, amount=1):
        return self.sig(name).up(amount)

    def end_stage(self):
        for s in self.signals.values():
            s.base += s.total
            s.total = 0

    def at(self, offset, *shape):
        n = int(np.prod(shape))
        v = self.arena[:, offset:offset + n] if offset < ARENA else self.tail[:, offset - ARENA:offset - ARENA + n]
        if len(shape) == 2:
            v = v.rearrange("p (a b) -> p a b", b=shape[1])
        if len(shape) == 3:
            v = v.rearrange("p (a b c) -> p a b c", b=shape[1], c=shape[2])
        return v

    def rounded(self, view):
        rounded = self.rounded_names[view.tensor.name]
        ap = [[rounded.shape[1], P]] + [list(x) for x in view.ap][1:]
        return bass.AP(tensor=rounded, offset=view.offset, ap=ap)

    def plan(self, segments):
        for seg in segments:
            seg.g0 = len(self.units)
            self.units += [(seg, u) for u in range(seg.n)]
        self.segments = segments

    def walk(self, eng, seg, body, chain=None, per_turn=0, head=2):
        pairs = max(0, (seg.n - 2 - head) // 2)
        if pairs < 2:
            pairs = 0
        for u in range(head if pairs else 0):
            body(Unit(seg, u, u % 2, u // 2, 1))
        if pairs:
            with eng.Fori(0, pairs) as i:
                if chain:
                    chain.enter(i, per_turn)
                for p in range(2):
                    body(Unit(seg, i * 2 + (head + p), p, i + head // 2, pairs))
                if chain:
                    chain.leave(pairs)
        for u in range(head + 2 * pairs if pairs else 0, seg.n):
            body(Unit(seg, u, u % 2, u // 2, 1))

    def ahead(self, unit):
        if not isinstance(unit.u, int):
            return unit.seg, unit.u + 2
        g = unit.g + 2
        return self.units[g] if g < len(self.units) else None

    def load(self, sp, seg, u, slot):
        src = seg.src[u] if isinstance(u, int) else \
            seg.src[bass.ds(u, 1), :, :].rearrange("a p f -> (a p) f")
        sp.dma_start(self.ring[:, 0, slot, 0:seg.size], src).then_inc(self.raw_full[slot], 16)

    def sp_unit(self, sp, unit):
        nxt = self.ahead(unit)
        if nxt:
            sp.wait_ge(self.lo_done, unit.g + 1)
            self.load(sp, nxt[0], nxt[1], unit.slot)

    def split_hi(self, dve, seg, slot, use):
        dve.wait_ge(self.raw_full[slot], (use + 1) * 16)
        dve.tensor_copy(self.rounded(self.ring[:, 1, slot, 0:seg.size]),
                        self.ring[:, 0, slot, 0:seg.size]).then_inc(self.hi_done, 1)

    def split_lo(self, pool, seg, slot, g):
        pool.wait_ge(self.hi_done, g + 1)
        pool.tensor_tensor(self.rounded(self.ring[:, 2, slot, 0:seg.size]), self.ring[:, 0, slot, 0:seg.size],
                           self.rounded(self.ring[:, 1, slot, 0:seg.size]).bitcast(F32),
                           ALU.subtract).then_inc(self.lo_done, 1)

    def dve_unit(self, dve, unit):
        nxt = self.ahead(unit)
        if nxt:
            self.split_hi(dve, nxt[0], unit.slot, unit.use + 1)

    def pool_unit(self, pool, unit):
        nxt = self.ahead(unit)
        if nxt:
            self.split_lo(pool, nxt[0], unit.slot, unit.g + 2)

    def product(self, pe, out, weights, moving, start, stop):
        (wh, wl), (xh, xl) = weights, moving
        r = self.rounded
        pe.matmul(out, r(wh), r(xh), start=start, stop=False)
        pe.matmul(out, r(wh), r(xl), start=False, stop=False)
        return pe.matmul(out, r(wl), r(xh), start=False, stop=stop)


class Dense:

    def __init__(self, m, seg, halves, ready=False):
        self.m, self.seg, self.halves, self.ready = m, seg, halves, ready

    def weights(self, unit, k, t):
        o = k * self.seg.cols + t * P
        return [self.m.ring[:, part, unit.slot, o:o + P] for part in (1, 2)]

    def pe_unit(self, pe, unit):
        m, seg = self.m, self.seg
        pe.wait_ge(m.lo_done, unit.g + 1)
        for t in range(seg.tiles):
            for k in range(seg.k):
                if self.ready and t == 0 and isinstance(unit.u, int) and unit.u == 0:
                    pe.wait_ge(m.sem("xready"), m.count("xready", k + 1))
                last = m.product(pe, m.psum[:, 2 * unit.slot + t, :], self.weights(unit, k, t),
                                 self.halves(k), k == 0, k == seg.k - 1)
            last.then_inc(m.up("done", unit.turns), 1)


def split_in_place(m, dve, hi, lo, ready, times=1):
    dve.tensor_copy(m.rounded(hi), lo).then_inc(m.vchain.up(), 1)
    dve.wait_ge(m.vchain.sem, m.vchain.now())
    dve.tensor_tensor(m.rounded(lo), lo, m.rounded(hi).bitcast(F32), ALU.subtract).then_inc(ready.up(times), 1)


def rstd_pe_sums(m, pe, acc, cols, bank, sig="ssq"):
    for i in range(cols):
        last = pe.matmul(m.psum[:, bank, i:i + 1], acc[:, i * P:(i + 1) * P], m.ones[:, 0:1],
                         start=True, stop=True)
    last.then_inc(m.up(sig), 1)


def rstd_dve_mean(m, dve, psum, mean, scale, eps=EPS):
    dve.tensor_scalar(mean, psum, scale, eps, ALU.mult, ALU.add).then_inc(m.up("mean"), 1)


def rstd_pool(m, pool, mean, half, out, count):
    pool.wait_ge(m.sem("mean"), m.count("mean", count))
    pool.tensor_tensor(out, mean, half, ALU.pow).then_inc(m.up("root"), 1)


def rstd_newton(m, dve, mean, root, tmp, sig):
    c = m.vchain
    dve.tensor_tensor(tmp, root, root, ALU.mult).then_inc(c.up(), 1)
    dve.wait_ge(c.sem, c.now())
    dve.tensor_tensor(tmp, tmp, mean, ALU.mult).then_inc(c.up(), 1)
    dve.wait_ge(c.sem, c.now())
    dve.tensor_scalar(tmp, tmp, -0.5, 1.5, ALU.mult, ALU.add).then_inc(c.up(), 1)
    dve.wait_ge(c.sem, c.now())
    dve.tensor_tensor(root, root, tmp, ALU.mult).then_inc(sig.up(), 1)


def rstd_pe_spread(m, pe, root, cols, out):
    for i in range(cols):
        last = pe.matmul(out(i), root[:, i:i + 1].broadcast_to([P, P]), m.ident[:, :],
                         start=True, stop=True)
    last.then_inc(m.up("spread"), 1)


S_MEAN, S_ROOT, S_TMP, S_HALF = 0, 6, 12, 18


def norm_stage_parts(m, acc, gain, xh, xl, final=None, shift=None):
    mean, root = m.small[:, S_MEAN:S_MEAN + 4], m.small[:, S_ROOT:S_ROOT + 4]
    tmp, half = m.small[:, S_TMP:S_TMP + 4], m.small[:, S_HALF:S_HALF + 4]

    def pe_part(pe):
        rstd_pe_sums(m, pe, acc, 4, 7)
        pe.wait_ge(m.sem("rstd"), m.count("rstd", 1))
        rstd_pe_spread(m, pe, root, 4, lambda i: m.psum[:, 6, i * P:(i + 1) * P])

    def dve_part(dve):
        dve.wait_ge(m.sem("ssq"), m.count("ssq", 1))
        rstd_dve_mean(m, dve, m.psum[:, 7, 0:4], mean, 1.0 / D)
        dve.wait_ge(m.sem("root"), m.count("root", 1))
        rstd_newton(m, dve, mean, root, tmp, m.sig("rstd"))
        dve.wait_ge(m.sem("spread"), m.count("spread", 1))
        for k in range(KD):
            norm = dve.scalar_tensor_tensor(xl[:, k, :], m.h[:, k, :], gain[:, k:k + 1],
                                            m.psum[:, 6, :], ALU.mult, ALU.mult)
            if final is not None:
                norm.then_inc(m.up("xready"), 1)
            else:
                norm.then_inc(m.vchain.up(), 1)
                dve.wait_ge(m.vchain.sem, m.vchain.now())
                if shift is not None:
                    dve.tensor_scalar(xl[:, k, :], xl[:, k, :], shift[:, k:k + 1], None, ALU.add).then_inc(m.vchain.up(), 1)
                    dve.wait_ge(m.vchain.sem, m.vchain.now())
                split_in_place(m, dve, xh[:, k, :], xl[:, k, :], m.sig("xready"))

    def pool_part(pool):
        rstd_pool(m, pool, mean, half, root, 1)

    return pe_part, dve_part, pool_part


ACC_AT = ARENA + TAIL - T


def pick(view, i):
    if isinstance(i, int):
        return view[:, i, :]
    return view[:, bass.ds(i, 1), :].rearrange("p a b -> p (a b)")


def col(view, i):
    return view[:, i:i + 1] if isinstance(i, int) else view[:, bass.ds(i, 1)]


class Residual:

    def __init__(self, m, seg, tile0, done0, freed0, squares, sq_at=None, scale=None, final_sum=False):
        self.m, self.seg, self.done0, self.freed0 = m, seg, done0, freed0
        self.squares, self.scale = squares, scale
        self.acc = m.at(ACC_AT, T)
        self.sq = m.at(sq_at, 2, T) if squares else None

    def tile(self, unit, t):
        return unit.u * self.seg.tiles + t

    def dve_unit(self, dve, unit):
        m, tiles = self.m, self.seg.tiles
        dve.wait_ge(m.sem("done"), m.count("done", self.done0 + (unit.u + 1) * tiles))
        m.dve_unit(dve, unit)
        for t in range(tiles):
            tile = self.tile(unit, t)
            h = pick(m.h, tile)
            bank = m.psum[:, 2 * unit.slot + t, :]
            if self.scale is None:
                ins = dve.tensor_tensor(h, bank, h, ALU.add)
            else:
                ins = dve.scalar_tensor_tensor(h, bank, col(self.scale, tile), h, ALU.mult, ALU.add)
            ins.then_inc(m.up("freed", unit.turns), 1)
            if self.squares and not (isinstance(tile, int) and tile < 2):
                self.add_square(dve, tile - 1, unit, t)

    def slot_of(self, tile, unit, t):
        if isinstance(tile, int):
            return tile % 2
        return (unit.seg.tiles * ((unit.slot - unit.seg.g0) % 2) + t) % 2

    def add_square(self, dve, tile, unit, t):
        m = self.m
        dve.wait_ge(m.sem("square"), m.count("square", tile + 1))
        dve.wait_ge(m.sem("summed"), m.count("summed", tile - 1))
        slot = tile % 2 if isinstance(tile, int) else 1 - self.slot_of(tile + 1, unit, t)
        ins = dve.tensor_tensor(self.acc, self.acc, self.sq[:, slot, :], ALU.add)
        ins.then_inc(m.up("summed", unit.turns), 1)

    def dve_end(self, dve):
        if self.squares:
            self.add_square(dve, KD - 1, Unit(self.seg, self.seg.n - 1, 0, 0, 1), 0)

    def act_unit(self, act, unit):
        if not self.squares:
            return
        m = self.m
        for t in range(self.seg.tiles):
            tile = self.tile(unit, t)
            act.wait_ge(m.sem("freed"), m.count("freed", self.freed0 + tile + 1))
            if not (isinstance(tile, int) and tile < 3):
                act.wait_ge(m.sem("summed"), m.count("summed", tile - 2))
            out = self.acc if isinstance(tile, int) and tile == 0 else \
                self.sq[:, self.slot_of(tile, unit, t), :]
            act.activation(out, pick(m.h, tile), ACT.Square).then_inc(m.up("square", unit.turns), 1)


def run_stage(m, parts):
    with m.nc.Block() as block:
        @block.sync
        def _(sp):
            parts["sp"](sp)

        @block.tensor
        def _(pe):
            parts["pe"](pe)

        @block.scalar
        def _(act):
            if "act" in parts:
                parts["act"](act)

        @block.vector
        def _(dve):
            parts["dve"](dve)

        @block.gpsimd
        def _(pool):
            parts["pool"](pool)
    m.end_stage()


def begin_stage(m):
    def sp(sp):
        for slot in range(2):
            m.load(sp, *m.units[slot], slot)

    def dve(dve):
        dve.memset(m.small[:, S_HALF:S_HALF + 6], -0.5).then_inc(m.vchain.up(), 1)
        dve.wait_ge(m.vchain.sem, m.vchain.now())
        for slot in range(2):
            m.split_hi(dve, m.units[slot][0], slot, 0)
        acc, sq = m.at(ACC_AT, T), m.at(0, T)
        dve.tensor_tensor(acc, m.h[:, 0, :], m.h[:, 0, :], ALU.mult).then_inc(m.vchain.up(), 1)
        dve.wait_ge(m.vchain.sem, m.vchain.now())
        for k in range(1, KD):
            dve.tensor_tensor(sq, m.h[:, k, :], m.h[:, k, :], ALU.mult).then_inc(m.vchain.up(), 1)
            dve.wait_ge(m.vchain.sem, m.vchain.now())
            dve.tensor_tensor(acc, acc, sq, ALU.add).then_inc(m.vchain.up(), 1)
            dve.wait_ge(m.vchain.sem, m.vchain.now())

    def pool(pool):
        for slot in range(2):
            m.split_lo(pool, m.units[slot][0], slot, slot)

    run_stage(m, dict(sp=sp, pe=lambda e: None, dve=dve, pool=pool))


def ffn_stage(m, segs, gain, taps):
    xh, xl = m.at(0, KD, T), m.at(4096, KD, T)
    ah, al = m.at(8192, FF_HALF, T), m.at(8192 + FF_HALF * T, FF_HALF, T)
    tmp = m.at(8192 + 2 * FF_HALF * T, 2, 2, T)
    sq_at = 8192 + 2 * FF_HALF * T + 4 * T
    npe, ndve, npool = norm_stage_parts(m, m.at(ACC_AT, T), gain, xh, xl)
    up = [Dense(m, s, lambda k: (xh[:, k, :], xl[:, k, :]), i == 0)
          for i, s in ((0, segs[0]), (2, segs[2]))]
    down = [Dense(m, s, lambda k: (ah[:, k, :], al[:, k, :]))
            for s in (segs[1], segs[3])]
    U, Dn = FF_HALF, KD
    per_half = 2 * U + Dn
    res = [Residual(m, segs[2 * i + 1], 0, i * per_half + 2 * U, i * per_half + 2 * U, i == 1, sq_at)
           for i in range(2)]

    def sp(sp):
        for seg in segs:
            m.walk(sp, seg, lambda unit: m.sp_unit(sp, unit))

    def pe(pe):
        npe(pe)
        for half in range(2):
            f0 = half * per_half

            def up_unit(unit):
                if not isinstance(unit.u, int) or unit.u >= 2:
                    pe.wait_ge(m.sem("freed"), m.count("freed", f0 + (unit.u - 1) * 2))
                elif half:
                    pe.wait_ge(m.sem("freed"), m.count("freed", f0 - 1 + unit.u))
                up[half].pe_unit(pe, unit)

            def down_unit(unit):
                if not isinstance(unit.u, int) or unit.u >= 2:
                    pe.wait_ge(m.sem("freed"), m.count("freed", f0 + 2 * U + unit.u - 1))
                else:
                    pe.wait_ge(m.sem("freed"), m.count("freed", f0 + 2 * U - 2 + 2 * unit.u))
                if isinstance(unit.u, int) and unit.u == 0:
                    pe.wait_ge(m.sem("actready"), m.count("actready", (half + 1) * U))
                down[half].pe_unit(pe, unit)

            m.walk(pe, segs[2 * half], up_unit)
            m.walk(pe, segs[2 * half + 1], down_unit)

    def act(act):
        for half in range(2):
            f0 = half * per_half

            def up_unit(unit):
                for t in range(2):
                    c = (unit.u * 2 + (half * 2 * U + t)) * 4
                    act.wait_ge(m.sem("done"), m.count("done", f0 + unit.u * 2 + (t + 1)))
                    if t == 0 and not (isinstance(unit.u, int) and half * U + unit.u < 2):
                        act.wait_ge(m.sem("actready"), m.count("actready", half * U + unit.u - 1))
                    act.activation(
                        tmp[:, unit.slot, t, :], m.psum[:, 2 * unit.slot + t, :], ACT.Identity,
                        bias=col(taps, c + 3), scale=col(taps, c + 2)).then_inc(m.up("tapped", unit.turns), 1)
                act.wait_ge(m.sem("freed"), m.count("freed", f0 + unit.u * 2 + 1))
                gate = tmp[:, unit.slot, 0, :]
                act.activation(gate, gate, ACT.Silu).then_inc(m.up("silu", unit.turns), 1)

            m.walk(act, segs[2 * half], up_unit)
            m.walk(act, segs[2 * half + 1], lambda unit: res[half].act_unit(act, unit))

    def dve(dve):
        ndve(dve)
        for half in range(2):
            f0 = half * per_half

            def up_unit(unit):
                dve.wait_ge(m.sem("done"), m.count("done", f0 + unit.u * 2 + 2))
                m.dve_unit(dve, unit)
                for t in range(2):
                    c = (unit.u * 2 + (half * 2 * U + t)) * 4
                    out, bank = tmp[:, unit.slot, t, :], m.psum[:, 2 * unit.slot + t, :]
                    dve.wait_ge(m.sem("tapped"), m.count("tapped", (half * U + unit.u) * 2 + (t + 1)))
                    dve.scalar_tensor_tensor(
                        out[:, 1:T], bank[:, 0:T - 1], col(taps, c + 1), out[:, 1:T], ALU.mult, ALU.add).then_inc(m.vchain.up(), 1)
                    dve.wait_ge(m.vchain.sem, m.vchain.now())
                    dve.scalar_tensor_tensor(
                        out[:, 2:T], bank[:, 0:T - 2], col(taps, c), out[:, 2:T], ALU.mult, ALU.add).then_inc(m.up("freed", unit.turns), 1)
                dve.wait_ge(m.sem("silu"), m.count("silu", half * U + unit.u + 1))
                dve.wait_ge(m.sem("freed"), m.count("freed", f0 + unit.u * 2 + 2))
                hi, lo = pick(ah, unit.u), pick(al, unit.u)
                dve.tensor_tensor(lo, tmp[:, unit.slot, 0, :], tmp[:, unit.slot, 1, :],
                                                     ALU.mult).then_inc(m.vchain.up(), 1)
                dve.wait_ge(m.vchain.sem, m.vchain.now())
                split_in_place(m, dve, hi, lo, m.sig("actready"), unit.turns)

            m.walk(dve, segs[2 * half], up_unit, m.vchain, 8)
            m.walk(dve, segs[2 * half + 1], lambda unit: res[half].dve_unit(dve, unit))
            res[half].dve_end(dve)

    def pool(pool):
        npool(pool)
        for seg in segs:
            m.walk(pool, seg, lambda unit: m.pool_unit(pool, unit))

    run_stage(m, dict(sp=sp, pe=pe, act=act, dve=dve, pool=pool))


def renorm_stage(m, gain):
    out = m.at(0, KD, T)
    npe, ndve, npool = norm_stage_parts(m, m.at(ACC_AT, T), gain, None, out, final=True)

    def pe(pe):
        npe(pe)

    def act(act):
        sq = m.at(4096, 2, T)
        for k in range(KD):
            act.wait_ge(m.sem("xready"), m.count("xready", k + 1))
            act.activation(m.h[:, k, :], out[:, k, :], ACT.Copy).then_inc(m.up("copied"), 1)
            if k >= 3:
                act.wait_ge(m.sem("summed"), m.count("summed", k - 2))
            act.activation(m.at(ACC_AT, T) if k == 0 else sq[:, k % 2, :],
                                               out[:, k, :], ACT.Square).then_inc(m.up("square"), 1)

    def dve(dve):
        ndve(dve)
        acc, sq = m.at(ACC_AT, T), m.at(4096, 2, T)
        for k in range(1, KD):
            dve.wait_ge(m.sem("square"), m.count("square", k + 1))
            dve.wait_ge(m.sem("summed"), m.count("summed", k - 1))
            dve.tensor_tensor(acc, acc, sq[:, k % 2, :], ALU.add).then_inc(m.up("summed"), 1)

    run_stage(m, dict(sp=lambda sp: None, pe=pe, act=act, dve=dve, pool=lambda pool: npool(pool)))


def store_stage(m, out):
    def sp(sp):
        s = m.sig("stored")
        sp.dma_start(out.rearrange("(k p) t -> p k t", p=P), m.h[:, :, :]).then_inc(s.up(16), 16)
        sp.wait_ge(s.sem, s.count(16))
    nop = lambda e: None
    run_stage(m, dict(sp=sp, pe=nop, dve=nop, pool=nop))


def softplus_abs(m, dve, x, mag):
    dve.tensor_scalar(mag, x, -1.0, None, ALU.mult).then_inc(m.vchain.up(), 1)
    dve.wait_ge(m.vchain.sem, m.vchain.now())
    dve.tensor_tensor(mag, mag, x, ALU.max).then_inc(m.up("magnitude"), 1)


def softplus_exp(m, act, mag, y, count=1):
    act.wait_ge(m.sem("magnitude"), m.count("magnitude", count))
    act.activation(y, mag, ACT.Exp, scale=-1.0).then_inc(m.up("decayed"), 1)


def softplus_sum(m, dve, x, y, z, acc, out, count=1):
    c = m.vchain
    dve.wait_ge(m.sem("decayed"), m.count("decayed", count))
    dve.tensor_scalar(z, y, 2.0, None, ALU.add).then_inc(c.up(), 1)
    dve.wait_ge(c.sem, c.now())
    dve.reciprocal(z, z).then_inc(c.up(), 1)
    dve.wait_ge(c.sem, c.now())
    dve.tensor_tensor(z, z, y, ALU.mult).then_inc(c.up(), 1)
    dve.wait_ge(c.sem, c.now())
    dve.tensor_tensor(y, z, z, ALU.mult).then_inc(c.up(), 1)
    dve.wait_ge(c.sem, c.now())
    dve.tensor_scalar(acc, y, 1.0 / 17, None, ALU.mult).then_inc(c.up(), 1)
    dve.wait_ge(c.sem, c.now())
    for k in range(7, 0, -1):
        dve.scalar_tensor_tensor(acc, acc, 1.0 / (2 * k + 1), y, ALU.add, ALU.mult).then_inc(c.up(), 1)
        dve.wait_ge(c.sem, c.now())
    dve.scalar_tensor_tensor(acc, acc, 1.0, z, ALU.add, ALU.mult).then_inc(c.up(), 1)
    dve.wait_ge(c.sem, c.now())
    dve.tensor_scalar(acc, acc, 2.0, None, ALU.mult).then_inc(c.up(), 1)
    dve.wait_ge(c.sem, c.now())
    dve.scalar_tensor_tensor(out, x, 0.0, acc, ALU.max, ALU.add).then_inc(c.up(), 1)
    dve.wait_ge(c.sem, c.now())


GATES_AT = 20480 + 4 * T


def lru_stage(m, seg_in, seg_out, v, gates_w):
    xh, xl = m.at(0, KD, T), m.at(4096, KD, T)
    xc, ga = m.at(8192, 4, T), m.at(10240, 4, T)
    ct, cv, bv = m.at(24576, 2, T), m.at(12288, 4, T), m.at(14336, 4, T)
    yh, yl = m.at(16384, KD, T), m.at(20480, KD, T)
    lru = [[m.at(25600 + (7 * p + i) * T, T) for i in range(7)] for p in range(2)]
    sp8 = m.small[:, 24:28]
    s = [m.small[:, 28 + 4 * i:32 + 4 * i] for i in range(5)]
    npe, ndve, npool = norm_stage_parts(m, m.at(ACC_AT, T), v["mix0_norm"], xh, xl)
    din = Dense(m, seg_in, lambda k: (xh[:, k, :], xl[:, k, :]), True)
    dout = Dense(m, seg_out, lambda k: (yh[:, k, :], yl[:, k, :]))
    res = Residual(m, seg_out, 0, 20, 12, True, sq_at=0)
    bank = lambda unit, t: m.psum[:, 2 * unit.slot + t, :]

    def sp(sp):
        m.walk(sp, seg_in, lambda unit: m.sp_unit(sp, unit))
        m.walk(sp, seg_out, lambda unit: m.sp_unit(sp, unit))

    def pool(pool):
        npool(pool)
        m.walk(pool, seg_in, lambda unit: m.pool_unit(pool, unit))
        m.walk(pool, seg_out, lambda unit: m.pool_unit(pool, unit))

    def units(seg):
        return [Unit(seg, u, u % 2, u // 2, 1) for u in range(seg.n)]

    def pe(pe):
        npe(pe)
        freed = m.sig("freed")

        def lru_gates(j):
            pe.wait_ge(freed.sem, freed.count(j + 1))
            if j >= 2:
                pe.wait_ge(m.sem("sigmoid"), m.count("sigmoid", 2 * (j - 1)))
            for g in range(2):
                pe.matmul(m.psum[:, 4 + 2 * (j % 2) + g, :], gates_w[:, g * 4 + j, :],
                                             xc[:, j, :], start=True, stop=True).then_inc(m.up("gates"), 1)

        for unit in units(seg_in):
            if unit.u in (4, 5):
                pe.wait_ge(m.sem("gelu"), m.count("gelu", 2 * unit.u - 6))
            elif unit.u >= 2:
                pe.wait_ge(freed.sem, freed.count(2 * unit.u - 2 if unit.u < 4 else unit.u - 1))
            din.pe_unit(pe, unit)
            if unit.u in (2, 4):
                lru_gates(unit.u - 2)
                lru_gates(unit.u - 1)
        for unit in units(seg_out):
            pe.wait_ge(freed.sem, freed.count(10 + 2 * unit.u))
            if unit.u == 0:
                pe.wait_ge(m.sem("yready"), m.count("yready", 8))
            dout.pe_unit(pe, unit)

    def act(act):
        softplus_exp(m, act, s[1], s[2])
        us = units(seg_in)

        def tap(unit):
            for t in range(2):
                j = 2 * unit.u + t
                act.wait_ge(m.sem("done"), m.count("done", j + 1))
                act.activation(xc[:, j, :], bank(unit, t), ACT.Identity,
                                                   bias=col(v["lru_conv_b"], j), scale=col(v["lru_conv_w"], 12 + j)).then_inc(m.up("tapped"), 1)

        def gelu(unit):
            for t in range(2):
                act.wait_ge(m.sem("done"), m.count("done", 2 * unit.u + t + 1))
                act.activation(ga[:, 2 * (unit.u - 2) + t, :], bank(unit, t), ACT.Gelu_apprx_tanh).then_inc(m.up("gelu"), 1)

        def gates(j):
            for g, b in enumerate(("lru_ba", "lru_bx")):
                act.wait_ge(m.sem("gates"), m.count("gates", 2 * j + g + 1))
                act.activation(lru[j % 2][g], m.psum[:, 4 + 2 * (j % 2) + g, :],
                                                    ACT.Sigmoid, bias=col(v[b], j)).then_inc(m.up("sigmoid"), 1)

        def decays(j):
            act.wait_ge(m.sem("sp8"), m.count("sp8", 1))
            act.wait_ge(m.sem("sigmoid"), m.count("sigmoid", 2 * j + 2))
            for g, f in ((2, ACT.Exp), (3, ACT.Tanh)):
                act.activation(lru[j % 2][g], lru[j % 2][0], f,
                                                   scale=col(sp8, j)).then_inc(m.up("decays"), 1)

        def root(j):
            act.wait_ge(m.sem("variance"), m.count("variance", j + 1))
            act.activation(lru[j % 2][6], lru[j % 2][4], ACT.Sqrt, scale=-1.0).then_inc(m.up("rooted"), 1)

        def copy_c(unit):
            j = unit.u - 4
            act.wait_ge(m.sem("done"), m.count("done", 2 * unit.u + 1))
            if j >= 2:
                act.wait_ge(m.sem("freed"), m.count("freed", 4 + j - 1))
            act.activation(ct[:, j % 2, :], bank(unit, 0), ACT.Copy).then_inc(m.up("copied"), 1)

        def tap_b(j):
            act.wait_ge(m.sem("freed"), m.count("freed", 4 + j + 1))
            act.activation(bv[:, j, :], cv[:, j, :], ACT.Identity,
                                                bias=col(v["sconv_b"], j), scale=col(v["sconv_w"], 8 + j)).then_inc(m.up("btapped"), 1)

        tap(us[0]), tap(us[1]), gelu(us[2])
        gates(0), gates(1), decays(0), decays(1)
        gelu(us[3]), copy_c(us[4])
        root(0), root(1), tap_b(0)
        gates(2), gates(3)
        act.wait_ge(m.sem("hidden"), m.count("hidden", 2))
        decays(2), decays(3)
        copy_c(us[5]), tap_b(1), root(2), root(3)
        copy_c(us[6]), tap_b(2), copy_c(us[7]), tap_b(3)
        for unit in units(seg_out):
            res.act_unit(act, unit)

    def dve(dve):
        c = m.vchain
        softplus_neg = v["lru_lambda"]
        dve.tensor_scalar(s[0], softplus_neg, -1.0, None, ALU.mult).then_inc(c.up(), 1)
        dve.wait_ge(c.sem, c.now())
        softplus_abs(m, dve, s[0], s[1])
        ndve(dve)
        softplus_sum(m, dve, s[0], s[2], s[3], s[4], sp8)
        dve.tensor_scalar(sp8, sp8, -8.0, None, ALU.mult).then_inc(m.up("sp8"), 1)
        us = units(seg_in)

        def begin(unit):
            dve.wait_ge(m.sem("done"), m.count("done", 2 * unit.u + 2))
            m.dve_unit(dve, unit)

        def conv_xa(unit):
            begin(unit)
            for t in range(2):
                j = 2 * unit.u + t
                out = xc[:, j, :]
                dve.wait_ge(m.sem("tapped"), m.count("tapped", j + 1))
                for k in range(1, 4):
                    ins = dve.scalar_tensor_tensor(out[:, k:T], bank(unit, t)[:, 0:T - k],
                                                   col(v["lru_conv_w"], (3 - k) * 4 + j), out[:, k:T],
                                                   ALU.mult, ALU.add)
                    if k < 3:
                        ins.then_inc(c.up(), 1)
                        dve.wait_ge(c.sem, c.now())
                    else:
                        ins.then_inc(m.up("freed"), 1)

        def variance(j):
            b = lru[j % 2]
            dve.wait_ge(m.sem("decays"), m.count("decays", 2 * j + 2))
            dve.tensor_tensor(b[4], b[2], b[2], ALU.mult).then_inc(c.up(), 1)
            dve.wait_ge(c.sem, c.now())
            dve.scalar_tensor_tensor(b[4], b[4], 1.0, b[3],
                                                           ALU.add, ALU.mult).then_inc(m.up("variance"), 1)
            dve.wait_ge(m.sem("freed"), m.count("freed", j + 1))
            dve.tensor_tensor(b[5], b[1], xc[:, j, :], ALU.mult).then_inc(c.up(), 1)
            dve.wait_ge(c.sem, c.now())

        def recur(j):
            b = lru[j % 2]
            dve.wait_ge(m.sem("rooted"), m.count("rooted", j + 1))
            dve.tensor_tensor(b[5], b[5], b[6], ALU.mult).then_inc(c.up(), 1)
            dve.wait_ge(c.sem, c.now())
            dve.tensor_tensor_scan(yl[:, j, :], b[2], b[5], 0.0, ALU.mult, ALU.add).then_inc(m.up("hidden"), 1)
            dve.wait_ge(m.sem("hidden"), m.count("hidden", j + 1))
            dve.wait_ge(m.sem("gelu"), m.count("gelu", j + 1))
            dve.tensor_tensor(yl[:, j, :], yl[:, j, :], ga[:, j, :], ALU.mult).then_inc(c.up(), 1)
            dve.wait_ge(c.sem, c.now())
            split_in_place(m, dve, yh[:, j, :], yl[:, j, :], m.sig("yready"))

        def gate_v(unit):
            begin(unit)
            j = unit.u - 4
            dve.wait_ge(m.sem("copied"), m.count("copied", j + 1))
            dve.tensor_tensor(cv[:, j, :], bank(unit, 1), ct[:, j % 2, :], ALU.mult).then_inc(m.up("freed"), 1)

        def conv_b(j):
            dve.wait_ge(m.sem("btapped"), m.count("btapped", j + 1))
            dve.wait_ge(m.sem("freed"), m.count("freed", 4 + j + 1))
            for k in (1, 2):
                dve.scalar_tensor_tensor(bv[:, j, k:T], cv[:, j, 0:T - k],
                                                     col(v["sconv_w"], (2 - k) * 4 + j), bv[:, j, k:T],
                                                     ALU.mult, ALU.add).then_inc(c.up(), 1)
                dve.wait_ge(c.sem, c.now())

        conv_xa(us[0]), conv_xa(us[1])
        begin(us[2]), variance(0), variance(1)
        begin(us[3]), gate_v(us[4])
        recur(0), recur(1), conv_b(0)
        gate_v(us[5]), variance(2), variance(3), conv_b(1)
        gate_v(us[6]), recur(2), conv_b(2)
        gate_v(us[7]), recur(3), conv_b(3)
        for unit in us[8:]:
            begin(unit)
            for t in range(2):
                j = 2 * (unit.u - 8) + t
                dve.tensor_tensor(yl[:, 4 + j, :], bank(unit, t), bv[:, j, :], ALU.mult).then_inc(m.up("freed"), 1)
                dve.wait_ge(m.sem("freed"), m.count("freed", 8 + j + 1))
                split_in_place(m, dve, yh[:, 4 + j, :], yl[:, 4 + j, :], m.sig("yready"))
        for unit in units(seg_out):
            res.dve_unit(dve, unit)
        res.dve_end(dve)

    run_stage(m, dict(sp=sp, pe=pe, act=act, dve=dve, pool=pool))


Q_AT, K_AT, V_AT, U_AT, G_AT, F_AT = 8192, 10240, 12288, 14336, 24576, 26624
Y_AT = 16384
SGU_W_AT, SGU_B_AT, SGU_N_AT = 27136, 28160, 28672
SGU_END = 29184
HEADS, HD = 8, 64
NT = T // P


def unrolled(seg):
    return [Unit(seg, u, u % 2, u // 2, 1) for u in range(seg.n)]


def pe_token_unit(m, pe, unit, halves, tiles=NT):
    pe.wait_ge(m.lo_done, unit.g + 1)
    w = unit.seg.cols
    for i in range(tiles):
        out = m.psum[:, 2 * unit.slot + i // 2, (i % 2) * w:(i % 2 + 1) * w]
        for k in range(unit.seg.k):
            wh, wl = [m.rounded(m.ring[:, part, unit.slot, k * w:(k + 1) * w]) for part in (1, 2)]
            xh, xl = [m.rounded(x[:, i * P:(i + 1) * P]) for x in halves(k)]
            pe.matmul(out, xh, wh, start=k == 0, stop=False)
            pe.matmul(out, xl, wh, start=False, stop=False)
            last = pe.matmul(out, xh, wl, start=False, stop=k == unit.seg.k - 1)
        if i % 2:
            last.then_inc(m.up("done"), 1)


def odd_in_stage(m, seg_in, seg_f, v, loads):
    xh, xl = m.at(0, KD, T), m.at(4096, KD, T)
    q, k_, vt, u_, g_ = [m.at(a, 4, T) for a in (Q_AT, K_AT, V_AT, U_AT, G_AT)]
    fs = [m.at(SGU_END + T * i, T)[0:2 * HEADS, :] for i in range(5)]
    gsq = m.at(SGU_END + 5 * T, 2, T)
    cums = m.at(F_AT, T)[0:2 * HEADS, :]
    sums, mean, root, tmp = [m.small[:, 32 * i:32 * i + 32] for i in range(2, 6)]
    half = m.small[:, 192:224]
    npe, ndve, npool = norm_stage_parts(m, m.at(ACC_AT, T), v["mix1_norm"], xh, xl)
    halves = lambda k: (xh[:, k, :], xl[:, k, :])
    din = Dense(m, seg_in, halves, True)
    dfg = Dense(m, seg_f, halves)
    bank = lambda unit, t: m.psum[:, 2 * unit.slot + t, :]
    us = unrolled(seg_in) + unrolled(seg_f)

    def sp(sp):
        for unit in us:
            m.sp_unit(sp, unit)
        for view, src in loads:
            sp.dma_start(view, src).then_inc(m.up("loaded", 16), 16)
        sp.wait_ge(m.sem("loaded"), m.count("loaded", 16 * len(loads)))

    def pe(pe):
        npe(pe)
        for n, unit in enumerate(us):
            if n in (2, 3):
                pe.wait_ge(m.sem("afreed"), m.count("afreed", 2 * n - 2))
            elif 4 <= n < 8:
                pe.wait_ge(m.sem("freed"), m.count("freed", 2 * n - 6))
            elif n >= 8:
                pe.wait_ge(m.sem("afreed"), m.count("afreed", 2 * n - 10))
            if n in (4, 5, 8, 9):
                pe_token_unit(m, pe, unit, halves)
            else:
                (dfg if n == 10 else din).pe_unit(pe, unit)

    def act(act):
        for n in (0, 1, 6, 7, 8, 9):
            for t in range(2):
                act.wait_ge(m.sem("done"), m.count("done", 2 * n + t + 1))
                b = bank(us[n], t)
                if n < 2:
                    ins = act.activation(q[:, 2 * n + t, :], b, ACT.Copy, scale=HD ** -0.5)
                elif n < 8:
                    ins = act.activation(u_[:, 2 * (n - 6) + t, :], b, ACT.Gelu_apprx_tanh)
                else:
                    c = (n - 8) * 256
                    ins = act.activation(g_[:, 2 * t:2 * t + 2, c:c + 256], b.rearrange("p (a b) -> p a b", b=256),
                                         ACT.Gelu_apprx_tanh)
                ins.then_inc(m.up("afreed"), 1)
        softplus_exp(m, act, fs[1], fs[2])

    def dve(dve):
        c = m.vchain
        ndve(dve)
        dve.memset(half, -0.5).then_inc(c.up(), 1)
        dve.wait_ge(c.sem, c.now())
        for n, unit in enumerate(us):
            dve.wait_ge(m.sem("done"), m.count("done", 2 * n + 2 if n < 10 else 21))
            m.dve_unit(dve, unit)
            for t in range(2):
                b = bank(unit, t)
                if n in (2, 3):
                    dve.tensor_copy(k_[:, 2 * (n - 2) + t, :], b).then_inc(m.up("freed"), 1)
                if n in (4, 5):
                    o = (n - 4) * 256
                    dve.tensor_copy(vt[:, 2 * t:2 * t + 2, o:o + 256],
                                                       b.rearrange("p (a b) -> p a b", b=256)).then_inc(m.up("freed"), 1)
        dve.tensor_scalar(fs[0], bank(us[10], 0)[0:2 * HEADS, :], v["fox_bf"][0:2 * HEADS, :], -1.0,
                                      ALU.add, ALU.mult).then_inc(c.up(), 1)
        dve.wait_ge(c.sem, c.now())
        softplus_abs(m, dve, fs[0], fs[1])
        dve.wait_ge(m.sem("afreed"), m.count("afreed", 12))
        for i in range(NT):
            dve.tensor_tensor(gsq[:, i % 2, :], g_[:, i, :], g_[:, i, :], ALU.mult).then_inc(c.up(), 1)
            dve.wait_ge(c.sem, c.now())
            dve.tensor_reduce(sums[:, 8 * i:8 * i + 8], gsq[:, i % 2, :].rearrange(
                "p (a b) -> p a b", b=HD), AX.X, ALU.add).then_inc(c.up(), 1)
            dve.wait_ge(c.sem, c.now())
        dve.tensor_scalar(mean, sums, 1.0 / HD, EPS, ALU.mult, ALU.add).then_inc(m.up("mean"), 1)
        softplus_sum(m, dve, fs[0], fs[2], fs[3], fs[4], fs[1])
        dve.memset(fs[4], 1.0).then_inc(c.up(), 1)
        dve.wait_ge(c.sem, c.now())
        dve.tensor_tensor_scan(cums, fs[4], fs[1], 0.0, ALU.mult, ALU.subtract).then_inc(c.up(), 1)
        dve.wait_ge(c.sem, c.now())
        dve.wait_ge(m.sem("root"), m.count("root", 2))
        dve.memset(m.small[:, 0:1], 0.0).then_inc(c.up(), 1)
        dve.wait_ge(c.sem, c.now())
        rstd_newton(m, dve, mean, root, tmp, m.sig("rstd"))
        dve.wait_ge(m.sem("rstd"), m.count("rstd", 2))
        dve.wait_ge(m.sem("loaded"), m.count("loaded", 16 * len(loads)))
        for i in range(NT):
            g3 = g_[:, i, :].rearrange("p (a b) -> p a b", b=HD)
            r3 = root[:, 8 * i:8 * i + 8].rearrange("p (a b) -> p a b", b=1).broadcast_to([P, 8, HD])
            dve.tensor_tensor(g3, g3, r3, ALU.mult).then_inc(c.up(), 1)
            dve.wait_ge(c.sem, c.now())
            dve.tensor_tensor(g_[:, i, :], g_[:, i, :], m.at(SGU_N_AT, T), ALU.mult).then_inc(c.up(), 1)
            dve.wait_ge(c.sem, c.now())
        w = m.at(SGU_W_AT, 8, P)
        lower = m.cum[:, 0:1, :].broadcast_to([P, 8, P])
        dve.tensor_tensor(w, w, lower, ALU.mult).then_inc(c.up(), 1)
        dve.wait_ge(c.sem, c.now())

    def pool(pool):
        npool(pool)
        for unit in us:
            m.pool_unit(pool, unit)
        rstd_pool(m, pool, mean, half, root, 2)

    run_stage(m, dict(sp=sp, pe=pe, act=act, dve=dve, pool=pool))


def fox_stage(m, v):
    q, k_, vt, u_, g_ = [m.at(a, 4, T) for a in (Q_AT, K_AT, V_AT, U_AT, G_AT)]
    yh, yl = m.at(Y_AT, KD, T), m.at(Y_AT + 4096, KD, T)
    cums = m.at(F_AT, T)[0:2 * HEADS, :]
    dec = m.at(0, 2, 2, T)[0:2 * HEADS]
    pr = m.at(2048, 2, T)
    pt = m.at(3072, 2, NT, P)
    negmax, total = m.small[:, 64:96], m.small[:, 96:128]
    w, bias = m.at(SGU_W_AT, 8, P), m.at(SGU_B_AT, 4, P)
    steps = [(h, b) for h in range(HEADS) for b in range(NT)]
    n = len(steps)

    def pe(pe):
        def scores(i):
            h, b = steps[i]
            o, width = HD * (h % 2), P * (b + 1)
            out = m.psum[:, i % 2, 0:width]
            if i >= 2:
                pe.wait_ge(m.sem("exped"), m.count("exped", i - 1))
            if b == 0:
                pe.wait_ge(m.sem("decrows"), m.count("decrows", 2 * h + 2))
            qs = slice(b * P, (b + 1) * P)
            pe.matmul(out, q[o:o + HD, h // 2, qs], k_[o:o + HD, h // 2, 0:width], start=True, stop=False)
            pe.matmul(out, dec[:, h % 2, 0, qs], dec[:, h % 2, 1, 0:width], start=False, stop=False)
            pe.matmul(out[:, b * P:width], m.ident[:, :], m.bar[:, 1, :], start=False, stop=True).then_inc(m.up("scored"), 1)

        def turn(i):
            h, b = steps[i]
            pe.wait_ge(m.sem("normed"), m.count("normed", i + 1))
            if i >= 2:
                pe.wait_ge(m.sem("ptcopied"), m.count("ptcopied", i - 1))
            for j in range(b + 1):
                last = pe.transpose(m.psum[:, 2 + i % 2, j * P:(j + 1) * P], pr[:, i % 2, j * P:(j + 1) * P],
                                    m.ident[:, :])
            last.then_inc(m.up("turned"), 1)

        def values(i):
            h, b = steps[i]
            pe.wait_ge(m.sem("ptcopied"), m.count("ptcopied", i + 1))
            if h % 2 == 0 and b == 0 and h >= 4:
                pe.wait_ge(m.sem("attended"), m.count("attended", h // 2 - 1))
            o = HD * (h % 2)
            for j in range(b + 1):
                last = pe.matmul(m.psum[o:o + HD, 4 + (h // 2) % 2, b * P:(b + 1) * P],
                                 vt[:, j, h * HD:(h + 1) * HD], pt[:, i % 2, j, :], start=j == 0, stop=j == b)
            last.then_inc(m.up("valued"), 1)

        def mix(j):
            if j >= 2:
                pe.wait_ge(m.sem("mixread"), m.count("mixread", j - 1))
            for h in (2 * j, 2 * j + 1):
                o = HD * (h % 2)
                for c in range(NT):
                    last = pe.matmul(m.psum[o:o + HD, 6 + j % 2, c * P:(c + 1) * P],
                                     g_[:, c, h * HD:(h + 1) * HD], w[:, h, :], start=True, stop=True)
            last.then_inc(m.up("mixed"), 1)

        for i in range(n + 2):
            if i < n:
                scores(i)
            if i % 8 == 1 and i < n:
                mix(i // 8)
            if 1 <= i <= n:
                turn(i - 1)
            if i >= 2:
                values(i - 2)

    def act(act):
        for i in range(n + 1):
            if i < n:
                h, b = steps[i]
                width = P * (b + 1)
                act.wait_ge(m.sem("maxed"), m.count("maxed", i + 1))
                if i >= 2:
                    act.wait_ge(m.sem("turned"), m.count("turned", i - 1))
                act.activation(pr[:, i % 2, 0:width], m.psum[:, i % 2, 0:width], ACT.Exp,
                                                  bias=col(negmax, i), accum_out=col(total, i)).then_inc(m.up("exped"), 1)
            if i >= 1:
                b = steps[i - 1][1]
                act.wait_ge(m.sem("turned"), m.count("turned", i))
                if i >= 3:
                    act.wait_ge(m.sem("valued"), m.count("valued", i - 2))
                act.activation(
                    pt[:, (i - 1) % 2, 0:b + 1, :], m.psum[:, 2 + (i - 1) % 2, 0:P * (b + 1)].rearrange(
                        "p (a b) -> p a b", b=P), ACT.Copy).then_inc(m.up("ptcopied"), 1)

    def dve(dve):
        c = m.vchain

        def rows(h):
            if h >= 2:
                dve.wait_ge(m.sem("scored"), m.count("scored", 4 * (h - 1)))
            sel = v["fox_select"][0:2 * HEADS, :]
            for part in range(2):
                dve.tensor_scalar(dec[:, h % 2, part, :], cums, col(sel, part),
                                                       col(sel, 2 + part * HEADS + h), ALU.mult, ALU.add).then_inc(m.up("decrows"), 1)

        def maxes(i):
            b = steps[i][1]
            dve.wait_ge(m.sem("scored"), m.count("scored", i + 1))
            dve.tensor_reduce(col(negmax, i), m.psum[:, i % 2, 0:P * (b + 1)], AX.X, ALU.max,
                                                 negate=True).then_inc(m.up("maxed"), 1)

        def norms(i):
            b = steps[i][1]
            dve.wait_ge(m.sem("exped"), m.count("exped", i + 1))
            dve.reciprocal(col(total, i), col(total, i)).then_inc(c.up(), 1)
            dve.wait_ge(c.sem, c.now())
            dve.tensor_scalar(pr[:, i % 2, 0:P * (b + 1)], pr[:, i % 2, 0:P * (b + 1)],
                                                  col(total, i), None, ALU.mult).then_inc(m.up("normed"), 1)

        def mixes(j):
            dve.wait_ge(m.sem("mixed"), m.count("mixed", j + 1))
            t = yl[:, j, :]
            dve.tensor_tensor(t.rearrange("p (a b) -> p a b", b=P),
                                                   m.psum[:, 6 + j % 2, :].rearrange("p (a b) -> p a b", b=P),
                                                   bias[:, j:j + 1, :].broadcast_to([P, NT, P]), ALU.add).then_inc(m.up("mixread"), 1)
            dve.wait_ge(m.sem("mixread"), m.count("mixread", j + 1))
            dve.tensor_tensor(t, t, u_[:, j, :], ALU.mult).then_inc(c.up(), 1)
            dve.wait_ge(c.sem, c.now())
            split_in_place(m, dve, yh[:, j, :], t, m.sig("yready"))

        def heads(j):
            dve.wait_ge(m.sem("valued"), m.count("valued", 8 * (j + 1)))
            dve.tensor_copy(yl[:, 4 + j, :], m.psum[:, 4 + j % 2, :]).then_inc(m.up("attended"), 1)
            dve.wait_ge(m.sem("attended"), m.count("attended", j + 1))
            split_in_place(m, dve, yh[:, 4 + j, :], yl[:, 4 + j, :], m.sig("yready"))

        rows(0)
        rows(1)
        for i in range(n + 3):
            if i < n:
                maxes(i)
            if i % 4 == 3 and i < n and i // 4 + 2 < HEADS:
                rows(i // 4 + 2)
            if 1 <= i <= n:
                norms(i - 1)
            if i % 8 == 4 and i < n:
                mixes(i // 8)
            if i >= 10 and (i - 10) % 8 == 0:
                heads((i - 10) // 8)

    run_stage(m, dict(sp=lambda e: None, pe=pe, act=act, dve=dve, pool=lambda e: None))


def out_stage(m, seg, y_at=None, halves=None, scale=None, sq_at=0):
    halves = halves or (lambda k: (m.at(y_at, KD, T)[:, k, :], m.at(y_at + 4096, KD, T)[:, k, :]))
    dense = Dense(m, seg, halves)
    res = Residual(m, seg, 0, 0, 0, True, sq_at=sq_at, scale=scale)
    us = unrolled(seg)

    def pe(pe):
        for unit in us:
            if unit.u >= 2:
                pe.wait_ge(m.sem("freed"), m.count("freed", 2 * (unit.u - 1)))
            dense.pe_unit(pe, unit)

    def dve(dve):
        for unit in us:
            res.dve_unit(dve, unit)
        res.dve_end(dve)

    run_stage(m, dict(sp=lambda sp: [m.sp_unit(sp, unit) for unit in us], pe=pe,
                      act=lambda act: [res.act_unit(act, unit) for unit in us], dve=dve,
                      pool=lambda pool: [m.pool_unit(pool, unit) for unit in us]))


TA = T + TC
NA = TA // P
MOD_UNITS = 24
XN_AT = 18432
O_AT = 24576
CTX = slice(T, TA)


def mod_stage(m, src, v, loads=()):
    cond = m.small[:, 224:240]
    rows = m.at(0, 6 * D)[0:2, :]
    R = 6
    ring = m.ring[:, :, :, :].rearrange("p a b f -> p (a b) f")
    loaded = [m.sig(f"mod_loaded{i}") for i in range(R)]

    def sp(sp):
        for view, src_ in loads:
            sp.dma_start(view, src_).then_inc(m.up("loaded", 16), 16)
        for u in range(MOD_UNITS):
            if u >= R:
                sp.wait_ge(m.sem("mod_done"), m.count("mod_done", u - R + 1))
            sp.dma_start(ring[:, u % R, :], src[u]).then_inc(loaded[u % R].up(16), 16)

    def pe(pe):
        pe.wait_ge(m.sem("cond"), m.count("cond", 1))
        for u in range(MOD_UNITS):
            pe.wait_ge(loaded[u % R].sem, loaded[u % R].count(16 * (u // R + 1)))
            if u >= 2:
                pe.wait_ge(m.sem("mod_rows"), m.count("mod_rows", u - 1))
            for k in range(KD):
                last = pe.matmul(m.psum[0:2, u % 2, 0:256], cond[:, 2 * k:2 * k + 2],
                                 ring[:, u % R, 256 * k:256 * (k + 1)], start=k == 0, stop=k == KD - 1)
            last.then_inc(m.up("mod_done"), 1)
        pe.wait_ge(m.sem("mod_rows"), m.count("mod_rows", MOD_UNITS))
        for c in range(6 * KD):
            last = pe.transpose(m.psum[:, 2, 2 * c:2 * c + 2], rows[:, c * P:(c + 1) * P], m.ident[0:2, 0:2])
        last.then_inc(m.up("mod_cols"), 1)

    def act(act):
        act.wait_ge(m.sem("loaded"), m.count("loaded", 16 * len(loads)))
        act.activation(cond, v["cond"], ACT.Silu).then_inc(m.up("cond"), 1)

    def dve(dve):
        for u in range(MOD_UNITS):
            dve.wait_ge(m.sem("mod_done"), m.count("mod_done", u + 1))
            dve.tensor_copy(rows[:, 256 * u:256 * (u + 1)], m.psum[0:2, u % 2, 0:256]).then_inc(m.up("mod_rows"), 1)
        dve.wait_ge(m.sem("mod_cols"), m.count("mod_cols", 1))
        b = v["b_mod"].rearrange("p (a b) -> p a b", b=1).broadcast_to([P, 48, 2])
        dve.tensor_tensor(m.mods[:, :, :], m.psum[:, 2, 0:96].rearrange(
            "p (a b) -> p a b", b=2), b, ALU.add).then_inc(m.vchain.up(), 1)
        dve.wait_ge(m.vchain.sem, m.vchain.now())

    run_stage(m, dict(sp=sp, pe=pe, act=act, dve=dve, pool=lambda e: None))


def gain_dve(m, dve, out, weight, scale):
    dve.scalar_tensor_tensor(out, scale, 1.0, weight, ALU.add, ALU.mult).then_inc(m.vchain.up(), 1)
    dve.wait_ge(m.vchain.sem, m.vchain.now())


def norm2_stage(m, v, ctx):
    xn = m.at(XN_AT, KD, TA)
    acc, accc, sq = m.at(ACC_AT, T), m.at(0, TC), m.at(TC, 2, TC)
    mean, root = m.small[:, S_MEAN:S_MEAN + 6], m.small[:, S_ROOT:S_ROOT + 6]
    tmp, half = m.small[:, S_TMP:S_TMP + 6], m.small[:, S_HALF:S_HALF + 6]
    gains = [m.small[:, 240 + 8 * i:248 + 8 * i] for i in range(2)]

    def sp(sp):
        sp.dma_start(xn[:, :, CTX], ctx.rearrange("(k p) t -> p k t", p=P)).then_inc(m.up("loaded", 16), 16)
        sp.wait_ge(m.sem("loaded"), m.count("loaded", 16))

    def pe(pe):
        pe.wait_ge(m.sem("summed"), m.count("summed", KD))
        rstd_pe_sums(m, pe, acc, 4, 7)
        for i in range(2):
            last = pe.matmul(m.psum[:, 7, 4 + i:5 + i], accc[:, i * P:(i + 1) * P], m.ones[:, 0:1],
                             start=True, stop=True)
        last.then_inc(m.up("ssq"), 1)
        pe.wait_ge(m.sem("rstd"), m.count("rstd", 1))
        rstd_pe_spread(m, pe, root, 6, lambda i: m.psum[:, 5 + i // 4, (i % 4) * P:(i % 4 + 1) * P])

    def act(act):
        act.wait_ge(m.sem("loaded"), m.count("loaded", 16))
        for k in range(KD):
            if k >= 3:
                act.wait_ge(m.sem("summed"), m.count("summed", k - 1))
            act.activation(accc if k == 0 else sq[:, k % 2, :], xn[:, k, CTX], ACT.Square).then_inc(m.up("square"), 1)

    def dve(dve):
        for i in range(2):
            gain_dve(m, dve, gains[i], v["norm_attn"], m.mods[:, KD:2 * KD, i])
        for k in range(1, KD):
            dve.wait_ge(m.sem("square"), m.count("square", k + 1))
            dve.wait_ge(m.sem("summed"), m.count("summed", k - 1))
            dve.tensor_tensor(accc, accc, sq[:, k % 2, :], ALU.add).then_inc(m.up("summed"), 1)
        dve.memset(sq[:, 0, 0:1], 0.0).then_inc(m.up("summed"), 1)
        dve.wait_ge(m.sem("ssq"), m.count("ssq", 2))
        rstd_dve_mean(m, dve, m.psum[:, 7, 0:6], mean, 1.0 / D)
        dve.wait_ge(m.sem("root"), m.count("root", 1))
        rstd_newton(m, dve, mean, root, tmp, m.sig("rstd"))
        dve.wait_ge(m.sem("spread"), m.count("spread", 1))
        for k in range(KD):
            for i, (src, cols, bank) in enumerate(((m.h[:, k, :], slice(0, T), 5), (xn[:, k, CTX], CTX, 6))):
                out = xn[:, k, cols]
                dve.scalar_tensor_tensor(out, src, col(gains[i], k), m.psum[:, bank, 0:out.shape[1]],
                                                            ALU.mult, ALU.mult).then_inc(m.vchain.up(), 1)
                dve.wait_ge(m.vchain.sem, m.vchain.now())
                dve.tensor_scalar(out, out, m.mods[:, k, i:i + 1], None, ALU.add).then_inc(m.vchain.up(), 1)
                dve.wait_ge(m.vchain.sem, m.vchain.now())

    run_stage(m, dict(sp=sp, pe=pe, act=act, dve=dve, pool=lambda pool: rstd_pool(m, pool, mean, half, root, 1)))


GH = 4
DK = 128
KT_AT, QT_AT, VT_AT, S_AT = 12288, 15360, 28672, 31744
KTOK_AT, VTOK_AT = 0, 3072
WORK_AT = 6144
BETA, GG, GC, NEG_EG, REST, TOTAL = range(6)


def split_xn(m, dve, xh, xl):
    xn = m.at(XN_AT, KD, TA)
    for k in range(KD):
        hi, lo = m.rounded(xh[:, k, :]), m.rounded(xl[:, k, :])
        dve.tensor_copy(hi, xn[:, k, :]).then_inc(m.vchain.up(), 1)
        dve.wait_ge(m.vchain.sem, m.vchain.now())
        dve.tensor_tensor(lo, xn[:, k, :], hi.bitcast(F32), ALU.subtract).then_inc(m.up("xready"), 1)


def pe_wide_unit(m, pe, unit, halves, wide, ready=False):
    pe.wait_ge(m.lo_done, unit.g + 1)
    for t in range(unit.seg.tiles):
        for cols, out in ((slice(0, T), m.psum[:, 2 * unit.slot + t, :]),
                          (CTX, m.psum[:, 4 + unit.slot, t * TC:(t + 1) * TC])):
            if cols is CTX and not wide[t]:
                continue
            for k in range(unit.seg.k):
                if ready and t == 0 and cols is not CTX:
                    pe.wait_ge(m.sem("xready"), m.count("xready", k + 1))
                o = k * unit.seg.cols + t * P
                w = [m.ring[:, part, unit.slot, o:o + P] for part in (1, 2)]
                last = m.product(pe, out, w, [x[:, cols] for x in halves(k)], k == 0, k == unit.seg.k - 1)
        last.then_inc(m.up("done"), 1)


def gdn_in_stage(m, seg, seg_bd, v, group):
    xh, xl = m.at(0, KD, TA), m.at(KD * TA, KD, TA)
    outs = [m.at(QT_AT, GH, T), m.at(KT_AT, GH, TA), m.at(VT_AT, GH, TA)]
    us = unrolled(seg) + (unrolled(seg_bd) if seg_bd else [])
    halves = lambda k: (xh[:, k, :], xl[:, k, :])
    spans = lambda part: [slice(0, T)] + ([CTX] if part else [])
    cols = lambda i: m.gcols[:, i, :]
    sp_t = [m.at(17408 + 96 * i, 96) for i in range(6)]
    ea = m.small[:, 256:272]
    bdb = m.psum[:, 7, 0:NA * 32].rearrange("p (n c) -> p n c", c=32)
    n3 = lambda x: x.rearrange("p (n c) -> p n c", c=16)
    wide_of = lambda x: x.rearrange("p (a b) -> p a b", a=1).broadcast_to([P, NA, 16])

    def banks(unit, t):
        return m.psum[:, 2 * unit.slot + t, :], m.psum[:, 4 + unit.slot, t * TC:(t + 1) * TC]

    def pe(pe):
        for unit in us[:6]:
            part = unit.u // 2
            if unit.u >= 2:
                pe.wait_ge(m.sem("freed"), m.count("freed", 2 * (unit.u - 1)))
            pe_wide_unit(m, pe, unit, halves, [part > 0] * 2, unit.u == 0)
        if seg_bd:
            unit = us[6]
            pe.wait_ge(m.lo_done, unit.g + 1)
            for i in range(NA):
                for k in range(KD):
                    wh, wl = [m.rounded(m.ring[:, part, unit.slot, k * 32:(k + 1) * 32]) for part in (1, 2)]
                    a, b = [m.rounded(x[:, k, i * P:(i + 1) * P]) for x in (xh, xl)]
                    pe.matmul(bdb[:, i, :], a, wh, start=k == 0, stop=False)
                    pe.matmul(bdb[:, i, :], b, wh, start=False, stop=False)
                    last = pe.matmul(bdb[:, i, :], a, wl, start=False, stop=k == KD - 1)
            last.then_inc(m.up("done"), 1)
            pe.wait_ge(m.sem("decays"), m.count("decays", 1))
            g = n3(cols(GG))
            for d in range(2):
                pe.matmul(m.psum[:, 6, 48 * d:48 * d + 48], m.cum[:, d, :], g[:, :, 8 * d:8 * d + 8],
                          start=True, stop=True)
            pe.matmul(m.psum[:, 6, 96:192], m.ones[:, 0:1].broadcast_to([P, P]), cols(GG),
                                         start=True, stop=True).then_inc(m.up("gsums"), 1)

    def act(act):
        n = 0
        if seg_bd:
            act.activation(ea, v["gdn_a_log"], ACT.Exp).then_inc(m.up("expa"), 1)
        for unit in us[:6]:
            part = unit.u // 2
            for t in range(2):
                h = 2 * (unit.u % 2) + t
                w = part * 8 + GH * group + h
                act.wait_ge(m.sem("done"), m.count("done", 2 * unit.u + (2 if part else t + 1)))
                for i, span in enumerate(spans(part)):
                    act.activation(outs[part][:, h, span], banks(unit, t)[i], ACT.Copy,
                                                       scale=col(v["conv_qkv"], 2 * 24 + w)).then_inc(m.up("tapped"), 1)
            for t in range(2):
                h = 2 * (unit.u % 2) + t
                act.wait_ge(m.sem("freed"), m.count("freed", 2 * unit.u + t + 1))
                o = outs[part][:, h, :]
                act.activation(o, o, ACT.Silu).then_inc(m.up("silu"), 1)
        if seg_bd:
            act.wait_ge(m.sem("done"), m.count("done", 13))
            softplus_exp(m, act, sp_t[1], sp_t[2])
            act.activation(n3(cols(BETA)), bdb[:, :, 0:16], ACT.Sigmoid).then_inc(m.up("beta"), 1)
            act.wait_ge(m.sem("gsums"), m.count("gsums", 1))
            act.wait_ge(m.sem("restsum"), m.count("restsum", 1))
            act.activation(cols(NEG_EG), cols(GC), ACT.Exp).then_inc(m.up("edec"), 1)
            act.activation(cols(REST), cols(REST), ACT.Exp).then_inc(m.up("edec"), 1)
            act.activation(cols(TOTAL), m.psum[:, 6, 96:192], ACT.Exp).then_inc(m.up("edec"), 1)

    def dve(dve):
        c = m.vchain
        split_xn(m, dve, xh, xl)
        taps = 0
        for unit in us[:6]:
            part = unit.u // 2
            dve.wait_ge(m.sem("done"), m.count("done", 2 * unit.u + 2))
            m.dve_unit(dve, unit)
            taps += 2 * len(spans(part))
            dve.wait_ge(m.sem("tapped"), m.count("tapped", taps))
            for t in range(2):
                h = 2 * (unit.u % 2) + t
                w = part * 8 + GH * group + h
                for i in (0, 1, 3, 4):
                    s = i - 2
                    for j, span in enumerate(spans(part)):
                        n = span.stop - span.start
                        a, b = max(0, -s), n - max(0, s)
                        o = outs[part][:, h, span.start + a:span.start + b]
                        ins = dve.scalar_tensor_tensor(o, banks(unit, t)[j][:, a + s:b + s],
                                                       col(v["conv_qkv"], i * 24 + w), o, ALU.mult, ALU.add)
                        if i == 4 and j == len(spans(part)) - 1:
                            ins.then_inc(m.up("freed"), 1)
                        else:
                            ins.then_inc(c.up(), 1)
                    if i < 4:
                        dve.wait_ge(c.sem, c.now())
        if seg_bd:
            unit = us[6]
            dve.wait_ge(m.sem("done"), m.count("done", 13))
            m.dve_unit(dve, unit)
            dve.wait_ge(m.sem("expa"), m.count("expa", 1))
            x3 = n3(sp_t[0])
            dve.tensor_tensor(x3, bdb[:, :, 16:32], wide_of(v["gdn_dt_bias"]), ALU.add).then_inc(c.up(), 1)
            dve.wait_ge(c.sem, c.now())
            softplus_abs(m, dve, sp_t[0], sp_t[1])
            softplus_sum(m, dve, sp_t[0], sp_t[2], sp_t[3], sp_t[4], sp_t[5])
            dve.scalar_tensor_tensor(n3(cols(GG)), n3(sp_t[5]), -1.0, wide_of(ea),
                                                         ALU.mult, ALU.mult).then_inc(m.up("decays"), 1)
            dve.wait_ge(m.sem("gsums"), m.count("gsums", 1))
            g4 = cols(GC).rearrange("p (n d h) -> p n d h", d=2, h=8)
            for d in range(2):
                dve.tensor_copy(g4[:, :, d, :], m.psum[:, 6, 48 * d:48 * d + 48].rearrange(
                    "p (n h) -> p n h", h=8)).then_inc(c.up(), 1)
                dve.wait_ge(c.sem, c.now())
            dve.scalar_tensor_tensor(cols(REST), cols(GC), -1.0, m.psum[:, 6, 96:192],
                                                          ALU.mult, ALU.add).then_inc(m.up("restsum"), 1)
            dve.wait_ge(m.sem("edec"), m.count("edec", 3))
            dve.tensor_scalar(cols(NEG_EG), cols(NEG_EG), -1.0, None, ALU.mult).then_inc(c.up(), 1)
            dve.wait_ge(c.sem, c.now())

    run_stage(m, dict(sp=lambda sp: [m.sp_unit(sp, unit) for unit in us], pe=pe, act=act, dve=dve,
                      pool=lambda pool: [m.pool_unit(pool, unit) for unit in us]))


def gdn_token_stage(m):
    kt, qt, vt = m.at(KT_AT, GH, TA), m.at(QT_AT, GH, T), m.at(VT_AT, GH, TA)
    ktok, vtok = m.at(KTOK_AT, NA, GH, P), m.at(VTOK_AT, NA, GH, P)
    qtok, sq = m.at(WORK_AT, NT, GH, P), m.at(WORK_AT + NT * GH * P, 2, GH, P)
    N = NA + NT
    ss, root, tmp = [m.small[:, 40 * i + 24:40 * i + 64] for i in range(3)]
    jobs = [(kt, ktok, i) for i in range(NA)] + [(qt, qtok, i) for i in range(NT)] + [(vt, vtok, i) for i in range(NA)]

    def pe(pe):
        for n, (src, _, i) in enumerate(jobs):
            if n >= 4:
                pe.wait_ge(m.sem("tokcopied"), m.count("tokcopied", n - 3))
            for h in range(GH):
                last = pe.transpose(m.psum[:, n % 4, h * P:(h + 1) * P], src[:, h, i * P:(i + 1) * P], m.ident[:, :])
            last.then_inc(m.up("turned"), 1)
        for n in range(N):
            if n >= 4:
                pe.wait_ge(m.sem("backcopied"), m.count("backcopied", n - 3))
            pe.wait_ge(m.sem("toknormed"), m.count("toknormed", n + 1))
            src = jobs[n][1][:, jobs[n][2]]
            for h in range(GH):
                last = pe.transpose(m.psum[:, 4 + n % 4, h * P:(h + 1) * P], src[:, h, :], m.ident[:, :])
            last.then_inc(m.up("back"), 1)

    def act(act):
        for n, (_, dst, i) in enumerate(jobs):
            act.wait_ge(m.sem("turned"), m.count("turned", n + 1))
            act.activation(dst[:, i].rearrange("p a b -> p (a b)"), m.psum[:, n % 4, :], ACT.Copy).then_inc(m.up("tokcopied"), 1)
        act.wait_ge(m.sem("sums"), m.count("sums", 1))
        act.activation(root, ss, ACT.Sqrt).then_inc(m.up("roots"), 1)
        for n in range(N):
            act.wait_ge(m.sem("back"), m.count("back", n + 1))
            dst, i = jobs[n][0], jobs[n][2]
            act.activation(dst[:, :, i * P:(i + 1) * P], m.psum[:, 4 + n % 4, :].rearrange(
                "p (a b) -> p a b", b=P), ACT.Copy).then_inc(m.up("backcopied"), 1)

    def pool(pool):
        for n in range(N):
            pool.wait_ge(m.sem("tokcopied"), m.count("tokcopied", n + 1))
            if n >= 2:
                pool.wait_ge(m.sem("reduced"), m.count("reduced", n - 1))
            src = jobs[n][1][:, jobs[n][2]]
            pool.tensor_tensor(sq[:, n % 2], src, src, ALU.mult).then_inc(m.up("squared"), 1)

    def dve(dve):
        c = m.vchain
        for n in range(N):
            dve.wait_ge(m.sem("squared"), m.count("squared", n + 1))
            dve.tensor_reduce(ss[:, GH * n:GH * n + GH], sq[:, n % 2], AX.X, ALU.add).then_inc(m.up("reduced"), 1)
        dve.wait_ge(m.sem("reduced"), m.count("reduced", N))
        dve.tensor_scalar(ss, ss, EPS, None, ALU.add).then_inc(m.up("sums"), 1)
        dve.wait_ge(m.sem("roots"), m.count("roots", 1))
        dve.reciprocal(root, root).then_inc(c.up(), 1)
        dve.wait_ge(c.sem, c.now())
        rstd_newton(m, dve, ss, root, tmp, m.sig("rstd"))
        dve.wait_ge(m.sem("rstd"), m.count("rstd", 1))
        dve.tensor_scalar(root[:, GH * NA:GH * N], root[:, GH * NA:GH * N], DK ** -0.5, None, ALU.mult).then_inc(c.up(), 1)
        dve.wait_ge(c.sem, c.now())
        for n in range(N):
            x = jobs[n][1][:, jobs[n][2]]
            r = root[:, GH * n:GH * n + GH].rearrange("p (a b) -> p a b", b=1).broadcast_to([P, GH, P])
            dve.tensor_tensor(x, x, r, ALU.mult).then_inc(m.up("toknormed"), 1)

    run_stage(m, dict(sp=lambda e: None, pe=pe, act=act, dve=dve, pool=pool))


def gdn_scan_stage(m, group):
    kt, qt, o = m.at(KT_AT, GH, TA), m.at(QT_AT, GH, T), m.at(O_AT, 8, T)
    ktok, vtok = m.at(KTOK_AT, NA, GH, P), m.at(VTOK_AT, NA, GH, P)
    places = [WORK_AT + 512 * i for i in range(12)] + [VT_AT + 512 * i for i in range(6)] + [17408, 17920]
    B = [{name: m.at(places[10 * d + i], GH, P) for i, name in enumerate(
        ("E", "A", "Z", "X", "Y", "QK", "QE", "R", "VN", "KD"))} for d in range(2)]
    S = [m.at(S_AT + 512 * d, GH, P) for d in range(2)]
    tiles = [[4, 5, 0, 1, 2, 3], [5, 4, 3, 2, 1, 0]]
    LEVELS = 7
    bank = lambda d, i: m.psum[:, 4 * d + i, :].rearrange("p (h c) -> p h c", c=P)
    sig = lambda name, d: m.sig(f"{name}{d}")
    wide = lambda x: x.rearrange("p (a b) -> p a b", a=1).broadcast_to([P, GH, P])
    nt = lambda n: slice(n * P, (n + 1) * P)

    def gcol(which, n, d, h):
        c = n * 16 + d * 8 + GH * group + h
        return m.gcols[:, which, c:c + 1]

    def gcols(which, n, d):
        c = n * 16 + d * 8 + GH * group
        return m.gcols[:, which, c:c + GH].rearrange("p (a b) -> p a b", b=1).broadcast_to([P, GH, P])

    def pe(pe):
        def each(d, i, f, name):
            for h in range(GH):
                last = f(bank(d, i)[:, h, :], h)
            last.then_inc(sig(name, d).up(), 1)

        for t in range(NA):
            for d in range(2):
                n, b = tiles[d][t], B[d]
                if t:
                    pe.wait_ge(sig("vnew", d).sem, sig("vnew", d).count(t))
                each(d, 0, lambda out, h: pe.matmul(out, gcol(GG, n, d, h).broadcast_to([P, P]), m.cum[:, d, :],
                                                    start=True, stop=True), "rsum")
                if t > 2:
                    pe.wait_ge(sig("oadd", d).sem, sig("oadd", d).count(t - 2))
                each(d, 1, lambda out, h: pe.matmul(out, kt[:, h, nt(n)], kt[:, h, nt(n)], start=True, stop=True),
                     "gram")
                if t >= 2:
                    each(d, 2, lambda out, h: pe.matmul(out, kt[:, h, nt(n)], qt[:, h, nt(n)],
                                                        start=True, stop=True), "qgram")
            for s in range(LEVELS):
                for d in range(2):
                    b = B[d]
                    if s:
                        pe.wait_ge(sig("xcopy", d).sem, sig("xcopy", d).count(6 * t + s))
                        if s == 1 and t >= 2:
                            pe.wait_ge(sig("qexp", d).sem, sig("qexp", d).count(t - 1))
                        each(d, 0, lambda out, h: pe.matmul(out, b["A"][:, h, :], b["X"][:, h, :],
                                                            start=True, stop=True), "ymul")
                for d in range(2):
                    b = B[d]
                    if s:
                        pe.wait_ge(sig("ymask", d).sem, sig("ymask", d).count(6 * t + s))
                        each(d, 1, lambda out, h: pe.matmul(out, b["Y"][:, h, :], b["Z"][:, h, :],
                                                            start=True, stop=True), "zmul")
                if s < LEVELS - 1:
                    for d in range(2):
                        pe.wait_ge(sig("znew", d).sem, sig("znew", d).count(LEVELS * t + s + 1))
                        if t and s == 0 and t < NA:
                            pe.wait_ge(sig("snew", d).sem, sig("snew", d).count(t))
                        each(d, 3, lambda out, h: pe.transpose(out, B[d]["Z"][:, h, :], m.ident[:, :]), "turn")
            for d in range(2):
                n = tiles[d][t]
                if t:
                    if t >= 2:
                        pe.wait_ge(sig("qk", d).sem, sig("qk", d).count(t - 1))
                    each(d, 2, lambda out, h: pe.matmul(out, kt[:, h, nt(n)], S[d][:, h, :], start=True, stop=True),
                         "ks")
            for d in range(2):
                pe.wait_ge(sig("znew", d).sem, sig("znew", d).count(LEVELS * (t + 1)))
                pe.wait_ge(sig("resid", d).sem, sig("resid", d).count(t + 1))
                each(d, 0, lambda out, h: pe.matmul(out, B[d]["Z"][:, h, :], B[d]["R"][:, h, :],
                                                    start=True, stop=True), "tmul")
            for d in range(2):
                b = B[d]
                pe.wait_ge(sig("vnew", d).sem, sig("vnew", d).count(t + 1))
                if t < NA - 1:
                    pe.wait_ge(sig("kdec", d).sem, sig("kdec", d).count(t + 1))
                    each(d, 3, lambda out, h: pe.matmul(out, b["KD"][:, h, :], b["VN"][:, h, :],
                                                        start=True, stop=True), "smul")
                if t >= 2:
                    pe.wait_ge(sig("qe", d).sem, sig("qe", d).count(t - 1))

                    def output(out, h):
                        pe.matmul(out, S[d][:, h, :], b["QE"][:, h, :], start=True, stop=False)
                        return pe.matmul(out, b["VN"][:, h, :], b["QK"][:, h, :], start=False, stop=True)
                    each(d, 1, output, "omul")

    def act(act):
        for t in range(NA):
            for d in range(2):
                b = B[d]
                act.wait_ge(sig("esum", d).sem, sig("esum", d).count(t + 1))
                act.activation(b["E"], b["E"], ACT.Exp).then_inc(sig("eexp", d).up(), 1)
                if t >= 2:
                    if t >= 3:
                        act.wait_ge(sig("omul", d).sem, sig("omul", d).count(t - 2))
                    act.activation(b["QE"], bank(d, 0), ACT.Exp).then_inc(sig("qexp", d).up(), 1)
            for s in range(LEVELS - 1):
                for d in range(2):
                    act.wait_ge(sig("turn", d).sem, sig("turn", d).count(6 * t + s + 1))
                    act.activation(B[d]["X"], bank(d, 3), ACT.Copy).then_inc(sig("xcopy", d).up(), 1)

    def pool(pool):
        for t in range(NA):
            for d in range(2):
                n, b = tiles[d][t], B[d]
                if t < NA - 1:
                    if t:
                        pool.wait_ge(sig("smul", d).sem, sig("smul", d).count(t))
                    pool.tensor_tensor(b["KD"], ktok[:, n], gcols(REST, n, d), ALU.mult).then_inc(sig("kdec", d).up(), 1)
                if t >= 2:
                    pool.wait_ge(sig("qexp", d).sem, sig("qexp", d).count(t - 1))
                    pool.tensor_tensor(b["QE"], b["QE"], qt[:, :, nt(n)], ALU.mult).then_inc(sig("qe", d).up(), 1)

    def dve(dve):
        c = m.vchain
        for t in range(NA):
            for d in range(2):
                n, b = tiles[d][t], B[d]
                dve.wait_ge(sig("rsum", d).sem, sig("rsum", d).count(t + 1))
                for h in range(GH):
                    ins = dve.scalar_tensor_tensor(b["E"][:, h, :], bank(d, 0)[:, h, :], gcol(GC, n, d, h),
                                                   m.bar[:, d, :], ALU.subtract, ALU.add)
                ins.then_inc(sig("esum", d).up(), 1)
            for d in range(2):
                n, b = tiles[d][t], B[d]
                dve.wait_ge(sig("eexp", d).sem, sig("eexp", d).count(t + 1))
                dve.wait_ge(sig("gram", d).sem, sig("gram", d).count(t + 1))
                for h in range(GH):
                    ins = dve.scalar_tensor_tensor(b["A"][:, h, :], bank(d, 1)[:, h, :], gcol(BETA, n, d, h),
                                                   b["E"][:, h, :], ALU.mult, ALU.mult)
                ins.then_inc(c.up(), 1)
                dve.wait_ge(c.sem, c.now())
                dve.tensor_tensor(b["Z"], b["A"], wide(m.lev[:, 1 - d, 0, :]), ALU.mult).then_inc(c.up(), 1)
                dve.wait_ge(c.sem, c.now())
                dve.tensor_tensor(b["Z"], wide(m.ident[:, :]), b["Z"], ALU.subtract).then_inc(sig("znew", d).up(), 1)
            for d in range(2):
                b = B[d]
                if t >= 2:
                    dve.wait_ge(sig("qgram", d).sem, sig("qgram", d).count(t - 1))
                    dve.tensor_tensor(b["QK"], b["E"], bank(d, 2), ALU.mult).then_inc(sig("qk", d).up(), 1)
            for s in range(1, LEVELS):
                for d in range(2):
                    dve.wait_ge(sig("ymul", d).sem, sig("ymul", d).count(6 * t + s))
                    dve.tensor_tensor(B[d]["Y"], bank(d, 0), wide(m.lev[:, d, s, :]), ALU.mult).then_inc(sig("ymask", d).up(), 1)
                for d in range(2):
                    dve.wait_ge(sig("zmul", d).sem, sig("zmul", d).count(6 * t + s))
                    dve.tensor_tensor(B[d]["Z"], B[d]["Z"], bank(d, 1), ALU.subtract).then_inc(sig("znew", d).up(), 1)
            for d in range(2):
                n, b = tiles[d][t], B[d]
                if t:
                    dve.wait_ge(sig("ks", d).sem, sig("ks", d).count(t))
                    for h in range(GH):
                        ins = dve.scalar_tensor_tensor(b["R"][:, h, :], bank(d, 2)[:, h, :], gcol(NEG_EG, n, d, h),
                                                       vtok[:, n, h, :], ALU.mult, ALU.add)
                else:
                    ins = dve.tensor_copy(b["R"], vtok[:, n])
                ins.then_inc(sig("resid", d).up(), 1)
            for d in range(2):
                n, b = tiles[d][t], B[d]
                dve.wait_ge(sig("tmul", d).sem, sig("tmul", d).count(t + 1))
                dve.tensor_tensor(b["VN"], bank(d, 0), gcols(BETA, n, d), ALU.mult).then_inc(sig("vnew", d).up(), 1)
            for d in range(2):
                n, b = tiles[d][t], B[d]
                if t >= 2:
                    dve.wait_ge(sig("omul", d).sem, sig("omul", d).count(t - 1))
                    out = o[:, GH * group:GH * (group + 1), nt(n)]
                    if (n < 2) == (d == 0):
                        ins = dve.tensor_copy(out, bank(d, 1))
                    else:
                        ins = dve.tensor_tensor(out, out, bank(d, 1), ALU.add)
                    ins.then_inc(sig("oadd", d).up(), 1)
                if t < NA - 1:
                    dve.wait_ge(sig("smul", d).sem, sig("smul", d).count(t + 1))
                    for h in range(GH):
                        if t:
                            ins = dve.scalar_tensor_tensor(S[d][:, h, :], S[d][:, h, :], gcol(TOTAL, n, d, h),
                                                           bank(d, 3)[:, h, :], ALU.mult, ALU.add)
                        else:
                            ins = dve.tensor_copy(S[d][:, h, :], bank(d, 3)[:, h, :])
                    ins.then_inc(sig("snew", d).up(), 1)

    run_stage(m, dict(sp=lambda e: None, pe=pe, act=act, dve=dve, pool=pool))


QK_N, ROPE = 128, 64
K_ALL, V_ALL, CQ_AT, CKV_AT, QR_AT, QN_AT = 0, 6144, 12288, 15360, 18432, 20480
KR_AT, COS_AT, SIN_AT, ROT_AT, SEL_AT, PAIR_AT, KROW_AT, QROW_AT = \
    28672, 29440, 29952, 30464, 30592, 30720, 31744, 31232
KRS_AT, PR_AT, PT_AT = 12288, 15360, 16896


def mla_in_stage(m, seg, v, loads):
    xh, xl = m.at(0, KD, TA), m.at(KD * TA, KD, TA)
    cqh, cql = m.at(CQ_AT, 3, T), m.at(CQ_AT + 3 * T, 3, T)
    ckh, ckl = m.at(CKV_AT, 2, TA), m.at(CKV_AT + 2 * TA, 2, TA)
    kr, krsq = m.at(KR_AT, TA), m.at(KROW_AT, TA)
    accs = [m.at(XN_AT, T), m.at(XN_AT + T, TA)]
    sq = m.at(XN_AT + T + TA, 2, TA)
    rot = m.at(XN_AT + T + 3 * TA, T)
    outs = [cql[:, 0, :], cql[:, 1, :], cql[:, 2, :], ckl[:, 0, :], ckl[:, 1, :], kr]
    wide = [False] * 3 + [True] * 3
    mean, root, tmp, half = [m.small[:, 24 + 10 * i:34 + 10 * i] for i in range(4)]
    us = unrolled(seg)

    def sp(sp):
        for view, src in loads:
            sp.dma_start(view, src).then_inc(m.up("loaded", 16), 16)
        for unit in us:
            m.sp_unit(sp, unit)
        sp.wait_ge(m.sem("loaded"), m.count("loaded", 16 * len(loads)))

    def pe(pe):
        for unit in us:
            if unit.u == 2:
                pe.wait_ge(m.sem("freed"), m.count("freed", 2))
            pe_wide_unit(m, pe, unit, lambda k: (xh[:, k, :], xl[:, k, :]), wide[2 * unit.u:2 * unit.u + 2],
                         unit.u == 0)
        pe.wait_ge(m.sem("summed"), m.count("summed", 3))
        for i in range(4):
            pe.matmul(m.psum[:, 7, i:i + 1], accs[0][:, i * P:(i + 1) * P], m.ones[:, 0:1], start=True, stop=True)
        for i in range(NA):
            last = pe.matmul(m.psum[:, 7, 4 + i:5 + i], accs[1][:, i * P:(i + 1) * P], m.ones[:, 0:1],
                             start=True, stop=True)
        last.then_inc(m.up("ssq"), 1)
        pe.wait_ge(m.sem("loaded"), m.count("loaded", 16 * len(loads)))
        pe.wait_ge(m.sem("krgain"), m.count("krgain", 1))
        pe.matmul(m.psum[:, 0, :], m.at(ROT_AT, P), kr[:, 0:T], start=True, stop=True).then_inc(m.up("rotated"), 1)
        pe.wait_ge(m.sem("rstd"), m.count("rstd", 1))
        rstd_pe_spread(m, pe, root, 4, lambda i: m.psum[:, 6, i * P:(i + 1) * P])
        rstd_pe_spread(m, pe, root[:, 4:10], 6, lambda i: m.psum[:, 4 + i // 4, (i % 4) * P:(i % 4 + 1) * P])

    def act(act):
        for t in range(6):
            act.wait_ge(m.sem("freed"), m.count("freed", t + 1))
            n = TA if wide[t] else T
            dst = {0: accs[0], 3: accs[1], 5: krsq}.get(t, sq[:, t % 2, 0:n])
            act.activation(dst, outs[t], ACT.Square).then_inc(m.up("square"), 1)

    def dve(dve):
        c = m.vchain
        dve.memset(half, -0.5).then_inc(c.up(), 1)
        dve.wait_ge(c.sem, c.now())
        split_xn(m, dve, xh, xl)
        for unit in us:
            dve.wait_ge(m.sem("done"), m.count("done", 2 * unit.u + 2))
            m.dve_unit(dve, unit)
            for t in range(2):
                n = 2 * unit.u + t
                ins = dve.tensor_copy(outs[n][:, 0:T], m.psum[:, 2 * unit.slot + t, :])
                if wide[n]:
                    ins.then_inc(c.up(), 1)
                    ins = dve.tensor_copy(outs[n][:, CTX], m.psum[:, 4 + unit.slot, t * TC:(t + 1) * TC])
                ins.then_inc(m.up("freed"), 1)
            for t in range(2):
                n = 2 * unit.u + t
                if n in (1, 2, 4):
                    dve.wait_ge(m.sem("square"), m.count("square", n + 1))
                    if n == 2:
                        dve.wait_ge(m.sem("summed"), m.count("summed", 1))
                    a = accs[n // 3]
                    dve.tensor_tensor(a, a, sq[:, n % 2, 0:TA if wide[n] else T], ALU.add).then_inc(m.up("summed"), 1)
        dve.wait_ge(m.sem("square"), m.count("square", 6))
        dve.tensor_scalar(kr, kr, v["k_norm_rope"], None, ALU.mult).then_inc(m.up("krgain"), 1)
        dve.wait_ge(m.sem("ssq"), m.count("ssq", 1))
        dve.tensor_scalar(mean[:, 0:4], m.psum[:, 7, 0:4], 1.0 / 384, EPS, ALU.mult, ALU.add).then_inc(c.up(), 1)
        dve.wait_ge(c.sem, c.now())
        dve.tensor_scalar(mean[:, 4:10], m.psum[:, 7, 4:10], 1.0 / 256, EPS, ALU.mult, ALU.add).then_inc(m.up("mean"), 1)
        dve.wait_ge(m.sem("rotated"), m.count("rotated", 1))
        dve.wait_ge(m.sem("loaded"), m.count("loaded", 16 * len(loads)))
        dve.tensor_tensor(rot, m.at(SIN_AT, T), m.psum[:, 0, :], ALU.mult).then_inc(c.up(), 1)
        dve.wait_ge(c.sem, c.now())
        dve.tensor_tensor(kr[:, 0:T], kr[:, 0:T], m.at(COS_AT, T), ALU.mult).then_inc(c.up(), 1)
        dve.wait_ge(c.sem, c.now())
        dve.tensor_tensor(kr[:, 0:T], kr[:, 0:T], rot, ALU.add).then_inc(c.up(), 1)
        dve.wait_ge(c.sem, c.now())
        dve.wait_ge(m.sem("root"), m.count("root", 1))
        rstd_newton(m, dve, mean, root, tmp, m.sig("rstd"))
        dve.wait_ge(m.sem("spread"), m.count("spread", 2))
        for k in range(3):
            dve.scalar_tensor_tensor(cql[:, k, :], cql[:, k, :], col(v["q_a_norm"], k),
                                                 m.psum[:, 6, :], ALU.mult, ALU.mult).then_inc(c.up(), 1)
            dve.wait_ge(c.sem, c.now())
            split_in_place(m, dve, cqh[:, k, :], cql[:, k, :], m.sig("lready"))
        for k in range(2):
            for cols, bank in ((slice(0, T), 4), (CTX, 5)):
                o = ckl[:, k, cols]
                dve.scalar_tensor_tensor(o, o, col(v["kv_a_norm"], k), m.psum[:, bank, 0:o.shape[1]],
                                                     ALU.mult, ALU.mult).then_inc(c.up(), 1)
                dve.wait_ge(c.sem, c.now())
            split_in_place(m, dve, ckh[:, k, :], ckl[:, k, :], m.sig("lready"))

    def pool(pool):
        for unit in us:
            m.pool_unit(pool, unit)
        rstd_pool(m, pool, mean, half, root, 1)

    run_stage(m, dict(sp=sp, pe=pe, act=act, dve=dve, pool=pool))


def mla_heads_stage(m, segs, v):
    qn, qr = m.at(QN_AT, 8, T), m.at(QR_AT, 4, T)
    ka, va = m.at(K_ALL, 8, TA), m.at(V_ALL, NA, 8 * P)
    cqh, cql = m.at(CQ_AT, 3, T), m.at(CQ_AT + 3 * T, 3, T)
    ckh, ckl = m.at(CKV_AT, 2, TA), m.at(CKV_AT + 2 * TA, 2, TA)
    sq, rot = m.at(V_ALL, 2, TA), m.at(V_ALL + 2 * TA, T)
    krsq, krow, qrow = m.at(KROW_AT, TA), m.at(KROW_AT, TA)[0:8, :], m.at(QROW_AT, T)[0:8, :]
    sel = m.at(SEL_AT, 13, 8)
    us = [u for s in segs for u in unrolled(s)]
    bank = lambda unit, t: m.psum[:, 2 * unit.slot + t, :]

    def kind(n):
        return "q" if n < 4 else "r" if n < 6 else "k" if n < 10 else "v"

    def pe(pe):
        def sums(i):
            pe.wait_ge(m.sem("square"), m.count("square", i + 1))
            if i < 12:
                last = pe.matmul(m.psum[0:8, 7, :], sel[:, i, :], sq[:, i % 2, 0:T], start=i == 0, stop=i == 11)
                last.then_inc(m.up("qsum" if i == 11 else "sqread"), 1)
            else:
                if i == 12:
                    pe.wait_ge(m.sem("qrow"), m.count("qrow", 1))
                    pe.wait_ge(m.sem("qturned"), m.count("qturned", 4))
                    pe.matmul(m.psum[0:8, 6, :], sel[:, 12, :], krsq[:, 0:T], start=True, stop=False)
                    pe.matmul(m.psum[0:8, 7, 0:TC], sel[:, 12, :], krsq[:, CTX], start=True, stop=False)
                pe.matmul(m.psum[0:8, 6, :], sel[:, i - 12, :], sq[:, i % 2, 0:T], start=False, stop=i == 19)
                last = pe.matmul(m.psum[0:8, 7, 0:TC], sel[:, i - 12, :], sq[:, i % 2, CTX], start=False, stop=i == 19)
                last.then_inc(m.up("sqread"), 1)

        def turn(j):
            pe.wait_ge(m.sem("freed"), m.count("freed", 9 + j))
            if j:
                pe.wait_ge(m.sem("qturned"), m.count("qturned", j))
            pe.matmul(m.psum[:, 6, :], m.at(ROT_AT, P), qr[:, j, :], start=True, stop=True).then_inc(m.up("rotated"), 1)

        qhalves = lambda k: (cqh[:, k, :], cql[:, k, :])
        khalves = lambda k: (ckh[:, k, :], ckl[:, k, :])
        for n, unit in enumerate(us):
            if n >= 2:
                pe.wait_ge(m.sem("freed"), m.count("freed", 2 * (n - 1)))
            if kind(n) in "qr":
                pe_wide_unit(m, pe, unit, qhalves, [False] * 2)
            elif kind(n) == "k":
                pe_wide_unit(m, pe, unit, khalves, [True] * 2)
            else:
                pe.wait_ge(m.lo_done, unit.g + 1)
                for i in range(NA):
                    out = m.psum[:, 2 * unit.slot + i // 2 if i < 4 else 4 + unit.slot, (i % 2) * 256:(i % 2 + 1) * 256]
                    for k in range(2):
                        wh, wl = [m.rounded(m.ring[:, part, unit.slot, k * 256:(k + 1) * 256]) for part in (1, 2)]
                        a, b = [m.rounded(x[:, i * P:(i + 1) * P]) for x in khalves(k)]
                        pe.matmul(out, a, wh, start=k == 0, stop=False)
                        pe.matmul(out, b, wh, start=False, stop=False)
                        last = pe.matmul(out, a, wl, start=False, stop=k == 1)
                    if i in (3, 5):
                        last.then_inc(m.up("done"), 1)
            if 1 <= n <= 10:
                for t in range(2):
                    i = 2 * (n - 1) + t
                    sums(i)
                    if 8 <= i < 12:
                        turn(i - 8)

    def act(act):
        for n, unit in enumerate(us[:10]):
            for t in range(2):
                i = 2 * n + t
                act.wait_ge(m.sem("done"), m.count("done", 2 * n + (2 if kind(n) == "k" else t + 1)))
                if i >= 2:
                    if i - 1 >= 12:
                        act.wait_ge(m.sem("qsum"), m.count("qsum", 1))
                    act.wait_ge(m.sem("sqread"), m.count("sqread", i - 1 if i <= 12 else i - 2))
                if kind(n) != "k":
                    act.activation(sq[:, i % 2, 0:T], bank(unit, t), ACT.Square).then_inc(m.up("square"), 1)
                else:
                    act.activation(sq[:, i % 2, 0:T], bank(unit, t), ACT.Square).then_inc(m.achain.up(), 1)
                    act.activation(sq[:, i % 2, CTX], m.psum[:, 4 + unit.slot, t * TC:(t + 1) * TC],
                                                       ACT.Square).then_inc(m.up("square"), 1)
        act.wait_ge(m.sem("sqread"), m.count("sqread", 19))
        act.activation(krow[:, 0:T], m.psum[0:8, 6, :], ACT.Copy).then_inc(m.achain.up(), 1)
        act.activation(krow[:, CTX], m.psum[0:8, 7, 0:TC], ACT.Copy).then_inc(m.achain.up(), 1)

    def dve(dve):
        c = m.vchain
        for n, unit in enumerate(us):
            dve.wait_ge(m.sem("done"), m.count("done", 2 * n + 2))
            m.dve_unit(dve, unit)
            k_ = kind(n)
            if k_ == "v":
                if n == 10:
                    dve.wait_ge(m.sem("sqread"), m.count("sqread", 19))
                o = (n - 10) * 256
                for t in range(2):
                    dve.tensor_copy(
                        va[:, 2 * t:2 * t + 2, o:o + 256], bank(unit, t).rearrange("p (a b) -> p a b", b=256)).then_inc(m.up("freed"), 1)
                    if t == 0:
                        dve.tensor_copy(va[:, 4:6, o:o + 256], m.psum[:, 4 + unit.slot, :].rearrange(
                            "p (a b) -> p a b", b=256)).then_inc(c.up(), 1)
                continue
            dve.wait_ge(m.sem("square"), m.count("square", 2 * n + 2))
            for t in range(2):
                i = 2 * n + t
                if k_ == "k":
                    dve.tensor_scalar(ka[:, i - 12, CTX], m.psum[:, 4 + unit.slot, t * TC:(t + 1) * TC],
                                             v["k_norm_nope"], None, ALU.mult).then_inc(c.up(), 1)
                    dve.tensor_scalar(ka[:, i - 12, 0:T], bank(unit, t), v["k_norm_nope"], None,
                                                         ALU.mult).then_inc(m.up("freed"), 1)
                elif k_ == "q":
                    dve.tensor_scalar(qn[:, i, :], bank(unit, t), v["q_norm_nope"], None, ALU.mult).then_inc(m.up("freed"), 1)
                else:
                    dve.tensor_scalar(qr[:, i - 8, :], bank(unit, t), v["q_norm_rope"], None,
                                                         ALU.mult).then_inc(m.up("freed"), 1)
            if k_ == "r":
                dve.wait_ge(m.sem("freed"), m.count("freed", 2 * n + 2))
            if n in (5, 6):
                for j in (2 * (n - 5), 2 * (n - 5) + 1):
                    dve.wait_ge(m.sem("rotated"), m.count("rotated", j + 1))
                    dve.tensor_tensor(rot, m.at(SIN_AT, T), m.psum[:, 6, :], ALU.mult).then_inc(c.up(), 1)
                    dve.wait_ge(c.sem, c.now())
                    dve.tensor_tensor(qr[:, j, :], qr[:, j, :], m.at(COS_AT, T), ALU.mult).then_inc(c.up(), 1)
                    dve.wait_ge(c.sem, c.now())
                    dve.tensor_tensor(qr[:, j, :], qr[:, j, :], rot, ALU.add).then_inc(m.up("qturned"), 1)
                    dve.wait_ge(m.sem("qturned"), m.count("qturned", j + 1))
            if n == 6:
                dve.wait_ge(m.sem("qsum"), m.count("qsum", 1))
                dve.tensor_copy(qrow, m.psum[0:8, 7, :]).then_inc(m.up("qrow"), 1)

    run_stage(m, dict(sp=lambda sp: [m.sp_unit(sp, unit) for unit in us], pe=pe, act=act, dve=dve,
                      pool=lambda pool: [m.pool_unit(pool, unit) for unit in us]))


def head_roots(m, pe=None, act=None, dve=None, rows=None, tiles=0, scale=1.0, back=0, out=None, n=1):
    w = 8 * tiles
    mean, root, tmp = [m.small[:, 24 + 80 * i:24 + 80 * i + w] for i in range(3)]
    if pe is not None:
        for i in range(tiles):
            src = rows(i)
            last = pe.transpose(m.psum[:, 0, 8 * i:8 * i + 8], src, m.ident[0:8, 0:8])
        last.then_inc(m.up("rcols"), 1)
        pe.wait_ge(m.sem("rstd"), m.count("rstd", 1))
        for i in range(back):
            o = 8 * (tiles - back + i)
            last = pe.transpose(m.psum[0:8, 1 + i // 4, (i % 4) * P:(i % 4 + 1) * P], root[:, o:o + 8], m.ident[:, :])
        last.then_inc(m.up("rback"), 1)
    if act is not None:
        act.wait_ge(m.sem("mean"), m.count("mean", 1))
        act.activation(root, mean, ACT.Sqrt).then_inc(m.up("root"), 1)
        act.wait_ge(m.sem("rback"), m.count("rback", 1))
        for cols, bank in ((slice(0, T), 1), (CTX, 2))[:1 if back == 4 else 2]:
            act.activation(out[:, cols], m.psum[0:8, bank, 0:cols.stop - cols.start], ACT.Copy).then_inc(m.up("rrows"), 1)
    if dve is not None:
        dve.wait_ge(m.sem("rcols"), m.count("rcols", 1))
        dve.tensor_scalar(mean, m.psum[:, 0, 0:w], scale, EPS, ALU.mult, ALU.add).then_inc(m.up("mean"), 1)
        dve.wait_ge(m.sem("root"), m.count("root", 1))
        dve.reciprocal(root, root).then_inc(m.vchain.up(), 1)
        dve.wait_ge(m.vchain.sem, m.vchain.now())
        rstd_newton(m, dve, mean, root, tmp, m.sig("rstd"))
    return root


def mla_norm_stage(m):
    ka, krs, kr = m.at(K_ALL, 8, TA), m.at(KRS_AT, 4, TA), m.at(KR_AT, TA)
    krow, qrow = m.at(KROW_AT, TA)[0:8, :], m.at(QROW_AT, T)[0:8, :]
    pair = m.at(PAIR_AT, 4, P)[0:8]
    rows = lambda i: qrow[:, i * P:(i + 1) * P] if i < NT else krow[:, (i - NT) * P:(i - NT + 1) * P]
    args = dict(rows=rows, tiles=NT + NA, scale=1.0 / (QK_N + ROPE), back=NA, out=krow)
    root = m.small[:, 24 + 80:24 + 160]

    def pe(pe):
        head_roots(m, pe=pe, **args)
        pe.wait_ge(m.sem("rrows"), m.count("rrows", 2))
        for i in range(12):
            w = m.ident[0:8, i:i + 1].broadcast_to([8, P]) if i < 8 else pair[:, i - 8, :]
            if i >= 2:
                pe.wait_ge(m.sem("scaled"), m.count("scaled", i - 1))
            b = 4 + 2 * (i % 2)
            pe.matmul(m.psum[:, b, :], w, krow[:, 0:T], start=True, stop=True)
            pe.matmul(m.psum[:, b + 1, 0:TC], w, krow[:, CTX], start=True, stop=True).then_inc(m.up("spread"), 1)

    def dve(dve):
        head_roots(m, dve=dve, **args)
        dve.wait_ge(m.sem("rstd"), m.count("rstd", 1))
        dve.tensor_scalar(root[:, 0:32], root[:, 0:32], float(QK_N + ROPE) ** -0.5, None, ALU.mult).then_inc(m.vchain.up(), 1)
        dve.wait_ge(m.vchain.sem, m.vchain.now())
        flat = m.psum[:, :, :].rearrange("p a b -> p (a b)")
        for i in range(12):
            dve.wait_ge(m.sem("spread"), m.count("spread", i + 1))
            o = (4 + 2 * (i % 2)) * 512
            src, dst = (ka[:, i, :], ka[:, i, :]) if i < 8 else (kr, krs[:, i - 8, :])
            dve.tensor_tensor(dst, src, flat[:, o:o + TA], ALU.mult).then_inc(m.up("scaled"), 1)

    run_stage(m, dict(sp=lambda e: None, pe=pe, act=lambda act: head_roots(m, act=act, **args), dve=dve,
                      pool=lambda e: None))


def mla_attend_stage(m):
    qn, qr = m.at(QN_AT, 8, T), m.at(QR_AT, 4, T)
    ka, va, krs = m.at(K_ALL, 8, TA), m.at(V_ALL, NA, 8 * P), m.at(KRS_AT, 4, TA)
    pr, pt = m.at(PR_AT, 2, TA), m.at(PT_AT, 2, NA, P)
    root = m.small[:, 24 + 80:24 + 160]
    negmax, total = m.small[:, 184:216], m.small[:, 216:248]
    flat = m.psum[:, :, :].rearrange("p a b -> p (a b)")
    steps = [(h, b) for h in range(8) for b in range(NT)]
    n = len(steps)
    scale = lambda i: col(root, 8 * steps[i][1] + steps[i][0])

    def pe(pe):
        def scores(i):
            h, b = steps[i]
            o, qs = ROPE * (h % 2), slice(b * P, (b + 1) * P)
            if i >= 2:
                pe.wait_ge(m.sem("exped"), m.count("exped", i - 1))
            for cols, bank in ((slice(0, T), 2 * (i % 2)), (CTX, 2 * (i % 2) + 1)):
                out = m.psum[:, bank, 0:cols.stop - cols.start]
                pe.matmul(out, qn[:, h, qs], ka[:, h, cols], start=True, stop=False)
                last = pe.matmul(out, qr[o:o + ROPE, h // 2, qs], krs[o:o + ROPE, h // 2, cols], start=False, stop=True)
            last.then_inc(m.up("scored"), 1)

        def turn(i):
            pe.wait_ge(m.sem("normed"), m.count("normed", i + 1))
            if i:
                pe.wait_ge(m.sem("ptcopied"), m.count("ptcopied", i))
            for j in range(NA):
                last = pe.transpose(flat[:, 2048 + j * P:2048 + (j + 1) * P], pr[:, i % 2, j * P:(j + 1) * P],
                                    m.ident[:, :])
            last.then_inc(m.up("turned"), 1)

        def values(i):
            h, b = steps[i]
            pe.wait_ge(m.sem("ptcopied"), m.count("ptcopied", i + 1))
            if b == 0 and h >= 2:
                pe.wait_ge(m.sem("attended"), m.count("attended", h - 1))
            for j in range(NA):
                last = pe.matmul(m.psum[:, 6 + h % 2, b * P:(b + 1) * P], va[:, j, h * P:(h + 1) * P],
                                 pt[:, i % 2, j, :], start=j == 0, stop=j == NA - 1)
            last.then_inc(m.up("valued"), 1)

        for i in range(n + 2):
            if i < n:
                scores(i)
            if 1 <= i <= n:
                turn(i - 1)
            if i >= 2:
                values(i - 2)

    def act(act):
        for i in range(n + 1):
            if i < n:
                act.wait_ge(m.sem("biased"), m.count("biased", i + 1))
                if i >= 2:
                    act.wait_ge(m.sem("turned"), m.count("turned", i - 1))
                act.activation(pr[:, i % 2, :], flat[:, 1024 * (i % 2):1024 * (i % 2) + TA], ACT.Exp,
                                                  bias=col(negmax, i), scale=scale(i), accum_out=col(total, i)).then_inc(m.up("exped"), 1)
            if i >= 1:
                act.wait_ge(m.sem("turned"), m.count("turned", i))
                if i >= 3:
                    act.wait_ge(m.sem("valued"), m.count("valued", i - 2))
                act.activation(pt[:, (i - 1) % 2].rearrange("p a b -> p (a b)"),
                                                     flat[:, 2048:2048 + TA], ACT.Copy).then_inc(m.up("ptcopied"), 1)

    def dve(dve):
        c = m.vchain
        for i in range(n + 3):
            if i < n:
                dve.wait_ge(m.sem("scored"), m.count("scored", i + 1))
                dve.tensor_reduce(col(negmax, i), flat[:, 1024 * (i % 2):1024 * (i % 2) + TA], AX.X,
                                              ALU.max, negate=True).then_inc(c.up(), 1)
                dve.wait_ge(c.sem, c.now())
                dve.tensor_tensor(col(negmax, i), col(negmax, i), scale(i), ALU.mult).then_inc(m.up("biased"), 1)
            if 1 <= i <= n:
                dve.wait_ge(m.sem("exped"), m.count("exped", i))
                dve.reciprocal(col(total, i - 1), col(total, i - 1)).then_inc(c.up(), 1)
                dve.wait_ge(c.sem, c.now())
                dve.tensor_scalar(pr[:, (i - 1) % 2, :], pr[:, (i - 1) % 2, :], col(total, i - 1),
                                                      None, ALU.mult).then_inc(m.up("normed"), 1)
            if i >= 6 and (i - 6) % 4 == 0:
                h = (i - 6) // 4
                dve.wait_ge(m.sem("valued"), m.count("valued", 4 * (h + 1)))
                dve.tensor_copy(qn[:, h, :], m.psum[:, 6 + h % 2, :]).then_inc(m.up("attended"), 1)

    run_stage(m, dict(sp=lambda e: None, pe=pe, act=act, dve=dve, pool=lambda e: None))


OGH_AT, OGL_AT, OMH_AT, OML_AT, GATE_AT = 8192, 12288, 16384, 20480, 24576


def branch_stage(m, v):
    o, og = m.at(O_AT, 8, T), m.at(OGL_AT, 8, T)
    sq, row = m.at(0, 2, T), m.at(2048, T)[0:8, :]
    omh, oml = m.at(OMH_AT, 8, T), m.at(OML_AT, 8, T)
    sel = m.at(SEL_AT, 13, 8)
    rows = lambda i: row[:, i * P:(i + 1) * P]
    args = dict(rows=rows, tiles=NT, scale=1.0 / DK, back=NT, out=row)

    def pe(pe):
        for h in range(8):
            pe.wait_ge(m.sem("square"), m.count("square", h + 1))
            pe.matmul(m.psum[0:8, 7, :], sel[:, h, :], sq[:, h % 2, :], start=h == 0, stop=h == 7).then_inc(m.up("sqread"), 1)
        pe.wait_ge(m.sem("rowed"), m.count("rowed", 1))
        head_roots(m, pe=pe, **args)
        pe.wait_ge(m.sem("rrows"), m.count("rrows", 1))
        for h in range(8):
            if h >= 2:
                pe.wait_ge(m.sem("scaled"), m.count("scaled", h - 1))
            pe.matmul(m.psum[:, 3 + h % 2, :], m.ident[0:8, h:h + 1].broadcast_to([8, P]), row,
                                          start=True, stop=True).then_inc(m.up("spread"), 1)

    def act(act):
        for h in range(8):
            if h >= 2:
                act.wait_ge(m.sem("sqread"), m.count("sqread", h - 1))
            act.activation(sq[:, h % 2, :], o[:, h, :], ACT.Square).then_inc(m.up("square"), 1)
        act.wait_ge(m.sem("sqread"), m.count("sqread", 8))
        act.activation(row, m.psum[0:8, 7, :], ACT.Copy).then_inc(m.up("rowed"), 1)
        head_roots(m, act=act, **args)

    def dve(dve):
        for h in range(8):
            dve.tensor_copy(m.rounded(omh[:, h, :]), oml[:, h, :]).then_inc(m.up("omhi"), 1)
        head_roots(m, dve=dve, **args)
        for h in range(8):
            dve.wait_ge(m.sem("spread"), m.count("spread", h + 1))
            dve.scalar_tensor_tensor(og[:, h, :], o[:, h, :], v["out_norm"], m.psum[:, 3 + h % 2, :],
                                                         ALU.mult, ALU.mult).then_inc(m.up("scaled"), 1)

    def pool(pool):
        for h in range(8):
            pool.wait_ge(m.sem("omhi"), m.count("omhi", h + 1))
            pool.tensor_tensor(m.rounded(oml[:, h, :]), oml[:, h, :],
                                                 m.rounded(omh[:, h, :]).bitcast(F32), ALU.subtract).then_inc(m.up("omlo"), 1)

    run_stage(m, dict(sp=lambda e: None, pe=pe, act=act, dve=dve, pool=pool))


def merge_stage(m, segs, v):
    sz, sg, sb, so = segs
    xh, xl = m.at(0, KD, T), m.at(4096, KD, T)
    ogh, ogl, omh, oml = [m.at(a, 8, T) for a in (OGH_AT, OGL_AT, OMH_AT, OML_AT)]
    zt = m.at(GATE_AT + 8 * T, 2, T)
    gate = lambda i: m.at(GATE_AT + i * T, T) if isinstance(i, int) else pick(m.at(GATE_AT, 14, T), i)
    gain = m.small[:, 240:248]
    npe, ndve, npool = norm_stage_parts(m, m.at(ACC_AT, T), gain, xh, xl, shift=m.mods[:, 0:KD, 0])
    bank = lambda unit, t: m.psum[:, 2 * unit.slot + t, :]
    res = Residual(m, so, 0, 40, 24, True, sq_at=8192, scale=m.mods[:, 2 * KD:3 * KD, 0])
    x = lambda k: (xh[:, k, :], xl[:, k, :])
    dz, dg, do = [Dense(m, s, x, s is sz) for s in (sz, sg, so)]

    def sp(sp):
        for s in segs:
            m.walk(sp, s, lambda unit: m.sp_unit(sp, unit))

    def pool(pool):
        npool(pool)
        for s in segs:
            m.walk(pool, s, lambda unit: m.pool_unit(pool, unit))

    def pe(pe):
        npe(pe)
        freed, gated = m.sig("freed"), m.sig("gated")
        for unit in unrolled(sz):
            if unit.u >= 2:
                pe.wait_ge(freed.sem, freed.count(2 * (unit.u - 1)))
            dz.pe_unit(pe, unit)

        def g_unit(unit):
            if isinstance(unit.u, int) and unit.u < 2:
                pe.wait_ge(freed.sem, freed.count(4 + 2 * (unit.u + 1)))
            else:
                pe.wait_ge(gated.sem, gated.count(2 * (unit.u - 1)))
            dg.pe_unit(pe, unit)

        def b_unit(unit):
            pe.wait_ge(m.lo_done, unit.g + 1)
            if isinstance(unit.u, int) and unit.u < 2:
                pe.wait_ge(gated.sem, gated.count(14 + 2 * unit.u))
            else:
                pe.wait_ge(freed.sem, freed.count(8 + 2 * (unit.u - 1)))
            if isinstance(unit.u, int) and unit.u == 0:
                pe.wait_ge(m.sem("ogready"), m.count("ogready", 8))
            for t, (hi, lo) in enumerate(((ogh, ogl), (omh, oml))):
                for k in range(KD):
                    o = k * sb.cols + t * P
                    w = [m.ring[:, part, unit.slot, o:o + P] for part in (1, 2)]
                    last = m.product(pe, bank(unit, t), w, (hi[:, k, :], lo[:, k, :]), k == 0, k == KD - 1)
                last.then_inc(m.up("done", unit.turns), 1)

        m.walk(pe, sg, g_unit)
        m.walk(pe, sb, b_unit)
        for unit in unrolled(so):
            pe.wait_ge(freed.sem, freed.count(22 + 2 * unit.u))
            if unit.u == 0:
                pe.wait_ge(m.sem("yready"), m.count("yready", 8))
            do.pe_unit(pe, unit)

    def act(act):
        for unit in unrolled(sz):
            for t in range(2):
                h = 2 * unit.u + t
                act.wait_ge(m.sem("done"), m.count("done", h + 1))
                if h >= 2:
                    act.wait_ge(m.sem("ogready"), m.count("ogready", h - 1))
                act.activation(zt[:, t, :], bank(unit, t), ACT.Silu).then_inc(m.up("silu"), 1)
        act.wait_ge(m.sem("ogready"), m.count("ogready", 8))

        def g_unit(unit):
            for t in range(2):
                act.wait_ge(m.sem("done"), m.count("done", 8 + 2 * unit.u + (t + 1)))
                act.activation(gate(unit.u * 2 + t), bank(unit, t), ACT.Sigmoid).then_inc(m.up("gated", unit.turns), 1)

        m.walk(act, sg, g_unit)
        for unit in unrolled(so):
            res.act_unit(act, unit)

    def dve(dve):
        c = m.vchain
        dve.scalar_tensor_tensor(gain, m.mods[:, KD:2 * KD, 0], 1.0, v["norm_attn"], ALU.add, ALU.mult).then_inc(c.up(), 1)
        dve.wait_ge(c.sem, c.now())
        ndve(dve)
        for unit in unrolled(sz):
            dve.wait_ge(m.sem("done"), m.count("done", 2 * unit.u + 2))
            m.dve_unit(dve, unit)
            for t in range(2):
                h = 2 * unit.u + t
                dve.wait_ge(m.sem("silu"), m.count("silu", h + 1))
                dve.tensor_tensor(ogl[:, h, :], ogl[:, h, :], zt[:, t, :], ALU.mult).then_inc(m.up("freed"), 1)
                dve.wait_ge(m.sem("freed"), m.count("freed", h + 1))
                split_in_place(m, dve, ogh[:, h, :], ogl[:, h, :], m.sig("ogready"))

        def g_unit(unit):
            dve.wait_ge(m.sem("done"), m.count("done", 8 + 2 * unit.u + 2))
            m.dve_unit(dve, unit)

        def b_unit(unit):
            dve.wait_ge(m.sem("done"), m.count("done", 24 + 2 * unit.u + 2))
            m.dve_unit(dve, unit)
            for t in range(2):
                g = gate(unit.u * 2 + t)
                dve.tensor_tensor(g, g, bank(unit, t), ALU.mult).then_inc(m.up("freed", unit.turns), 1)
            dve.wait_ge(m.sem("freed"), m.count("freed", 8 + 2 * unit.u + 2))
            hi, lo = pick(xh, unit.u), pick(xl, unit.u)
            dve.tensor_tensor(lo, gate(unit.u * 2), gate(unit.u * 2 + 1), ALU.add).then_inc(c.up(), 1)
            dve.wait_ge(c.sem, c.now())
            split_in_place(m, dve, hi, lo, m.sig("yready"), unit.turns)

        m.walk(dve, sg, g_unit)
        dve.wait_ge(m.sem("gated"), m.count("gated", 16))
        m.walk(dve, sb, b_unit, c, 4)
        for unit in unrolled(so):
            res.dve_unit(dve, unit)
        res.dve_end(dve)

    run_stage(m, dict(sp=sp, pe=pe, act=act, dve=dve, pool=pool))


def mlp_stage(m, segs, v):
    NU = 8
    KT_ = 2 * NU
    xh, xl = m.at(0, KD, T), m.at(4096, KD, T)
    ah, al = m.at(8192, KT_, T), m.at(8192 + KT_ * T, KT_, T)
    gain = m.small[:, 240:248]
    npe, ndve, npool = norm_stage_parts(m, m.at(ACC_AT, T), gain, xh, xl, shift=m.mods[:, 3 * KD:4 * KD, 0])
    per_half = 2 * NU + KD
    up = [Dense(m, segs[2 * i], lambda k: (xh[:, k, :], xl[:, k, :]), i == 0)
          for i in range(2)]
    down = [Dense(m, segs[2 * i + 1], lambda k: (ah[:, k, :], al[:, k, :])) for i in range(2)]
    res = [Residual(m, segs[2 * i + 1], 0, i * per_half + 2 * NU, 0, False, scale=m.mods[:, 5 * KD:6 * KD, 0])
           for i in range(2)]
    bank = lambda unit, t: m.psum[:, 2 * unit.slot + t, :]

    def sp(sp):
        for s in segs:
            m.walk(sp, s, lambda unit: m.sp_unit(sp, unit))

    def pool(pool):
        npool(pool)
        for s in segs:
            m.walk(pool, s, lambda unit: m.pool_unit(pool, unit))

    def pe(pe):
        npe(pe)
        freed = m.sig("freed")
        for half in range(2):
            f0 = half * per_half

            def up_unit(unit):
                if not isinstance(unit.u, int) or unit.u >= 2:
                    pe.wait_ge(freed.sem, freed.count(f0 + (unit.u - 1) * 2))
                elif half:
                    pe.wait_ge(freed.sem, freed.count(f0 - 1 + unit.u))
                up[half].pe_unit(pe, unit)

            def down_unit(unit):
                if not isinstance(unit.u, int) or unit.u >= 2:
                    pe.wait_ge(freed.sem, freed.count(f0 + 2 * NU + unit.u - 1))
                else:
                    pe.wait_ge(freed.sem, freed.count(f0 + 2 * NU - 2 + 2 * unit.u))
                if isinstance(unit.u, int) and unit.u == 0:
                    pe.wait_ge(m.sem("actready"), m.count("actready", (half + 1) * KT_))
                down[half].pe_unit(pe, unit)

            m.walk(pe, segs[2 * half], up_unit)
            m.walk(pe, segs[2 * half + 1], down_unit)

    def act(act):
        for half in range(2):
            f0 = half * per_half

            def up_unit(unit):
                for t in range(2):
                    act.wait_ge(m.sem("done"), m.count("done", f0 + 2 * unit.u + (t + 1)))
                    act.activation(pick(al, unit.u * 2 + t), bank(unit, t), ACT.Relu).then_inc(m.up("relu", unit.turns), 1)

            m.walk(act, segs[2 * half], up_unit)

    def dve(dve):
        c = m.vchain
        dve.scalar_tensor_tensor(gain, m.mods[:, 4 * KD:5 * KD, 0], 1.0, v["norm_mlp"], ALU.add, ALU.mult).then_inc(c.up(), 1)
        dve.wait_ge(c.sem, c.now())
        ndve(dve)
        for half in range(2):
            f0 = half * per_half

            def up_unit(unit):
                dve.wait_ge(m.sem("done"), m.count("done", f0 + 2 * unit.u + 2))
                m.dve_unit(dve, unit)
                for t in range(2):
                    hi, lo = pick(ah, unit.u * 2 + t), pick(al, unit.u * 2 + t)
                    dve.wait_ge(m.sem("relu"), m.count("relu", half * KT_ + 2 * unit.u + (t + 1)))
                    dve.scalar_tensor_tensor(lo, bank(unit, t), 0.0, lo, ALU.max, ALU.mult).then_inc(m.up("freed", unit.turns), 1)
                    dve.wait_ge(m.sem("freed"), m.count("freed", f0 + 2 * unit.u + (t + 1)))
                    split_in_place(m, dve, hi, lo, m.sig("actready"), unit.turns)

            m.walk(dve, segs[2 * half], up_unit, c, 4)
            m.walk(dve, segs[2 * half + 1], lambda unit: res[half].dve_unit(dve, unit))

    run_stage(m, dict(sp=sp, pe=pe, act=act, dve=dve, pool=pool))


def program(nc, d, vcols, nvec):
    ctx = ExitStack()
    with ctx:
        m = Machine(nc, ctx)
        vectors = ctx.enter_context(nc.sbuf_tensor("vectors", [P, nvec], F32))
        v = {n: vectors[:, o:o + c] for n, (o, c) in vcols.items()}
        S = {"lru_in": Segment(d["w_lru_in"], 10, 8, 2), "lru_out": Segment(d["w_lru_out"], 4, 8, 2)}
        for l in range(2):
            for half in range(2):
                S[f"up{l}{half}"] = Segment(d[f"w_up{l}{half}"], FF_HALF, 8, 2)
                S[f"down{l}{half}"] = Segment(d[f"w_down{l}{half}"], 8, FF_HALF, 1)
        ffn = lambda l: [S[f"{n}{l}{h}"] for h in range(2) for n in ("up", "down")]
        S["odd_in"], S["odd_f"] = Segment(d["w_odd_in"], 10, 8, 2), Segment(d["w_odd_f"], 1, 8, 1)
        S["odd_out"] = Segment(d["w_odd_out"], 4, 8, 2)
        order = [S["lru_in"], S["lru_out"]] + ffn(0) + [S["odd_in"], S["odd_f"], S["odd_out"]] + ffn(1)
        for g in range(2):
            S[f"gdn{g}"] = Segment(d[f"w_gdn{g}"], 6, 8, 2)
        S["bd"] = Segment(d["w_bd"], 1, 8, 1, cols=32)
        S["lat"] = Segment(d["w_lat"], 3, 8, 2)
        S["uqn"], S["uqr"] = Segment(d["w_uqn"], 4, 3, 2), Segment(d["w_uqr"], 2, 3, 2)
        S["ukn"], S["uv"] = Segment(d["w_ukn"], 4, 2, 2), Segment(d["w_uv"], 4, 2, 2)
        S["z"], S["gates"] = Segment(d["w_z"], 4, 8, 2), Segment(d["w_gates"], 8, 8, 2)
        S["branch"], S["out"] = Segment(d["w_branch"], 8, 8, 2), Segment(d["w_out"], 4, 8, 2)
        for half in range(2):
            S[f"mup{half}"] = Segment(d[f"w_mup{half}"], 8, 8, 2)
            S[f"mdown{half}"] = Segment(d[f"w_mdown{half}"], 8, 16, 1)
        two = [S[n] for n in ("gdn0", "bd", "gdn1", "lat", "uqn", "uqr", "ukn", "uv", "z", "gates", "branch",
                              "out", "mup0", "mdown0", "mup1", "mdown1")]
        order += two
        m.plan(order)
        gates_w = m.at(GATES_AT, 8, P)
        consts = [(m.ident[:, :], d["ident"]), (m.cum[:, :, :].rearrange("p a b -> p (a b)"), d["cum"]),
                  (m.bar[:, :, :].rearrange("p a b -> p (a b)"), d["bar"]),
                  (m.lev[:, :, :, :].rearrange("p a b c -> p (a b c)").bitcast(mybir.dt.uint16), d["lev"]),
                  (m.ones[:, :], d["ones"]), (vectors[:, :], d["vec"]),
                  (gates_w[:, :, :].rearrange("p a b -> p (a b)"), d["lru_gates"])]
        mod_stage(m, d["w_mod"], v, consts + [(m.h[:, :, :], d["xT"].rearrange("(k p) t -> p k t", p=P))])
        begin_stage(m)
        lru_stage(m, S["lru_in"], S["lru_out"], v, gates_w)
        ffn_stage(m, ffn(0), v["ffn_norm0"], v["ffn_taps0"])
        odd_in_stage(m, S["odd_in"], S["odd_f"], v,
                     [(m.at(SGU_W_AT, 1024), d["sgu_w"]), (m.at(SGU_B_AT, 512), d["sgu_b"]),
                      (m.at(SGU_N_AT, 512), d["sgu_n"])])
        fox_stage(m, v)
        out_stage(m, S["odd_out"], Y_AT)
        ffn_stage(m, ffn(1), v["ffn_norm1"], v["ffn_taps1"])
        renorm_stage(m, v["final_norm"])
        second(m, S, v, d)
        store_stage(m, d["out"])


def second(m, S, v, d):
    norm2_stage(m, v, d["ctxT"])
    for g in range(2):
        gdn_in_stage(m, S[f"gdn{g}"], S["bd"] if g == 0 else None, v, g)
        gdn_token_stage(m)
        gdn_scan_stage(m, g)
    mla_in_stage(m, S["lat"], v, [(m.at(COS_AT, 1792), d["rope"])])
    mla_heads_stage(m, [S["uqn"], S["uqr"], S["ukn"], S["uv"]], v)
    mla_norm_stage(m)
    mla_attend_stage(m)
    branch_stage(m, v)
    merge_stage(m, [S[n] for n in ("z", "gates", "branch", "out")], v)
    mlp_stage(m, [S[n] for n in ("mup0", "mdown0", "mup1", "mdown1")], v)


def columns(a):
    a = np.asarray(a)
    a = a.reshape(-1, a.shape[-1])
    return a.reshape(a.shape[0] * (a.shape[1] // P), P).T


def units_of(w, tile_order, k_tiles, tiles):
    w = np.asarray(w).reshape(k_tiles, P, -1, P)[:, :, tile_order]
    w = w.reshape(k_tiles, P, len(tile_order) // tiles, tiles, P)
    return np.ascontiguousarray(w.transpose(2, 1, 0, 3, 4)).reshape(len(tile_order) // tiles, P, -1)


def lay_out(a):
    f = {}
    vec = {}
    f["xT"] = np.ascontiguousarray(a["x"][0].T)
    xa, ga, c, b, vb = [list(range(4 * i, 4 * i + 4)) for i in range(5)]
    order = xa + ga + [t for pair in zip(c, vb) for t in pair] + b
    f["w_lru_in"] = units_of(a["mix0_w_in"][0], order, 8, 2)
    f["w_lru_out"] = units_of(a["mix0_w_out"][0], list(range(8)), 8, 2)
    bd = np.zeros((P, 8, P), a["lru_wa"].dtype)
    for g, w in enumerate(("lru_wa", "lru_wx")):
        for head in range(8):
            o = 64 * (head % 2)
            bd[o:o + 64, g * 4 + head // 2, o:o + 64] = a[w][0, head]
    f["lru_gates"] = bd.reshape(P, -1)
    for n in ("mix0_norm", "lru_conv_w", "lru_conv_b", "lru_ba", "lru_bx", "lru_lambda", "sconv_w", "sconv_b",
              "mix1_norm"):
        vec[n] = columns(a[n])
    nf = 2 * FF_HALF
    for l in range(2):
        order = [t for j in range(nf) for t in (j, nf + j)]
        up = units_of(a["ffn_up"][l], order, 8, 2)
        down = a["ffn_down"][l]
        for half in range(2):
            f[f"w_up{l}{half}"] = up[half * FF_HALF:(half + 1) * FF_HALF]
            f[f"w_down{l}{half}"] = units_of(down[half * FF_HALF * P:(half + 1) * FF_HALF * P], list(range(8)),
                                             FF_HALF, 1)
        taps = np.concatenate([a["ffn_conv_w"][l], a["ffn_conv_b"][l][None]]).reshape(4, 2 * nf, P)[:, order]
        vec[f"ffn_taps{l}"] = taps.transpose(2, 1, 0).reshape(P, -1)
        vec[f"ffn_norm{l}"] = columns(a["ffn_norm"][l])
    vec["final_norm"] = columns(a["final_norm"])
    w = a["mix1_w_in"][0]
    f["w_odd_in"] = units_of(w[:, :20 * P], [8, 9, 10, 11, 12, 13, 14, 15, 16, 17, 18, 19, 0, 1, 2, 3, 4, 5, 6, 7], 8, 2)
    gates = np.zeros((D, P), w.dtype)
    gates[:, 0:8] = gates[:, 8:16] = w[:, 20 * P:]
    f["w_odd_f"] = units_of(gates, [0], 8, 1)
    f["w_odd_out"] = units_of(a["mix1_w_out"][0], list(range(8)), 8, 2)
    bf = np.zeros((P, 1), w.dtype)
    bf[0:8, 0] = bf[8:16, 0] = a["fox_bf"][0]
    vec["fox_bf"] = bf
    sel = np.zeros((P, 18), np.float32)
    sel[0:8, 0] = 1
    sel[8:16, 1] = -1
    for h in range(8):
        sel[8 + h, 2 + h] = 1
        sel[h, 10 + h] = 1
    vec["fox_select"] = sel
    f["sgu_w"] = np.ascontiguousarray(a["sgu_w"][0].transpose(2, 0, 1)).reshape(P, -1)
    f["sgu_b"] = np.repeat(a["sgu_b"][0].reshape(4, 2, 1, P), 64, axis=2).reshape(4, P, P).transpose(1, 0, 2).reshape(P, -1)
    f["sgu_n"] = np.repeat(a["sgu_norm"][0][None], P, axis=0)
    f["ctxT"] = np.ascontiguousarray(a["ctx_2"][0].T)
    vec["cond"] = np.stack([a["c_2"][0].reshape(8, P), a["c_ctx_2"].reshape(8, P)], 2).transpose(1, 0, 2).reshape(P, 16)
    f["w_mod"] = units_of(a["w_mod_2"][0], list(range(48)), 8, 2)
    vec["b_mod"] = columns(a["b_mod_2"])
    vec["norm_attn"], vec["norm_mlp"] = columns(a["norm_attn_2"]), columns(a["norm_mlp_2"])
    vec["conv_qkv"] = columns(a["conv_qkv_2"])
    vec["gdn_a_log"] = np.repeat(a["gdn_a_log_2"].reshape(1, 16), P, axis=0)
    vec["gdn_dt_bias"] = np.repeat(a["gdn_dt_bias_2"].reshape(1, 16), P, axis=0)
    w = a["w_in_2"][0]
    qkv, rest = w[:, :3072], w[:, 3072:]
    for g in range(2):
        f[f"w_gdn{g}"] = units_of(qkv, [8 * part + 4 * g + h for part in range(3) for h in range(4)], 8, 2)
    bd = rest[:, 1024:1056]
    lat = np.concatenate([rest[:, 1056:1696], rest[:, 1696:1760], rest[:, 1696:1760]], 1)
    f["w_lat"] = units_of(lat, list(range(6)), 8, 2)
    uq = a["w_uq_2"][0].reshape(384, 8, 192)
    f["w_uqn"] = units_of(uq[:, :, :128].reshape(384, 1024), list(range(8)), 3, 2)
    f["w_uqr"] = units_of(uq[:, :, 128:].reshape(384, 512), list(range(4)), 3, 2)
    ukv = a["w_ukv_2"][0].reshape(256, 8, 256)
    f["w_ukn"] = units_of(ukv[:, :, :128].reshape(256, 1024), list(range(8)), 2, 2)
    f["w_uv"] = units_of(ukv[:, :, 128:].reshape(256, 1024), list(range(8)), 2, 2)
    vec["q_a_norm"], vec["kv_a_norm"] = columns(a["mla_q_a_norm_2"]), columns(a["mla_kv_a_norm_2"])
    vec["out_norm"] = columns(a["gdn_out_norm_2"])
    for n in ("q_norm", "k_norm"):
        w2 = a[n + "_2"][0]
        vec[n + "_nope"] = w2[:128, None]
        vec[n + "_rope"] = np.concatenate([w2[128:], w2[128:]])[:, None]
    f["w_z"] = units_of(rest[:, 0:1024], list(range(8)), 8, 2)
    pairs = [t for i in range(8) for t in (i, 8 + i)]
    f["w_gates"] = units_of(rest[:, 1760:], pairs, 8, 2)
    f["w_branch"] = units_of(np.concatenate([a["w_branch_gdn_2"][0], a["w_branch_mla_2"][0]], 1), pairs, 8, 2)
    f["w_out"] = units_of(a["w_out_2"][0], list(range(8)), 8, 2)
    up, down = units_of(a["w_mlp_in_2"][0], list(range(32)), 8, 2), a["w_mlp_out_2"][0]
    for half in range(2):
        f[f"w_mup{half}"] = up[8 * half:8 * half + 8]
        f[f"w_mdown{half}"] = units_of(down[2048 * half:2048 * (half + 1)], list(range(8)), 16, 1)
    f["w_bd"] = np.ascontiguousarray(bd.reshape(8, P, 32).transpose(1, 0, 2)).reshape(1, P, 256)
    return f, vec


def shape_constants():
    i, j = np.arange(P)[:, None], np.arange(P)[None, :]
    f = {"ident": np.eye(P, dtype=np.float32)}
    f["cum"] = np.stack([i <= j, i >= j], 1).astype(np.float32).reshape(P, -1)
    f["bar"] = np.where(np.stack([i <= j, i >= j], 1), 0, -1e30).astype(np.float32).reshape(P, -1)
    lev = []
    for s in (1, 2, 4, 8, 16, 32, 64):
        lev.append((i // (2 * s) == j // (2 * s)) & (i // s > j // s))
    lev = np.stack(lev, 1)
    pos = np.arange(T)
    inv = 10000.0 ** (-np.arange(16, dtype=np.float32) / np.float32(16))
    ang = np.concatenate([(pos // 64)[None] * inv[:, None]] * 2 + [(pos % 64)[None] * inv[:, None]] * 2)
    ang = np.concatenate([ang, ang]).astype(np.float32)
    rot = np.zeros((P, P), np.float32)
    for b in range(0, P, 32):
        for r in range(16):
            rot[b + 16 + r, b + r] = -1
            rot[b + r, b + 16 + r] = 1
    sel = np.zeros((P, 16, 8), np.float32)
    for h in range(8):
        sel[:, h, h] = 1
        sel[64 * (h % 2):64 * (h % 2) + 64, 8 + h // 2, h] = 1
    sel[0:64, 12, :] = 1
    pair = np.zeros((P, 4, P), np.float32)
    for h in range(8):
        pair[h, h // 2, 64 * (h % 2):64 * (h % 2) + 64] = 1
    f["rope"] = np.concatenate([np.cos(ang), np.sin(ang), rot, sel.reshape(P, -1), pair.reshape(P, -1)], 1).astype(np.float32)
    f["lev"] = (np.stack([lev, np.transpose(lev, (2, 1, 0))], 1) * 0x3F80).astype(np.uint16).reshape(P, -1)
    return f


def kernel(**inputs):
    import concourse.bacc as bacc
    from concourse.bass_utils import run_bass_kernel_spmd

    f, vec = lay_out({name: np.asarray(value) for name, value in inputs.items()})
    f.update(shape_constants())
    f["ones"] = np.ones((P, 1), np.float32)
    vcols, n = {}, 0
    for name, value in vec.items():
        vcols[name] = (n, value.shape[1])
        n += value.shape[1]
    f["vec"] = np.concatenate(list(vec.values()), axis=1)
    nc = bacc.Bacc("TRN2", target_bir_lowering=False, num_devices=1)
    arrays, d = {}, {}
    for name, value in f.items():
        arrays["in_" + name] = value = np.ascontiguousarray(value)
        d[name] = nc.dram_tensor("in_" + name, value.shape, mybir.dt.from_np(value.dtype), kind="ExternalInput").ap()
    d["out"] = nc.dram_tensor("out", (D, T), F32, kind="ExternalOutput").ap()
    program(nc, d, vcols, n)
    result = run_bass_kernel_spmd(nc, [arrays], core_ids=[0])
    return np.ascontiguousarray(result.results[0]["out"].T)[None]
```

```python
from contextlib import ExitStack

import numpy as np

import concourse.bass as bass
from concourse import mybir

F32, F32R, BF16, U32 = mybir.dt.float32, mybir.dt.float32r, mybir.dt.bfloat16, mybir.dt.uint32
ACT = mybir.ActivationFunctionType
ALU = mybir.AluOpType
AX = mybir.AxisListType

P = 128
T = 512
TC = 256
D = 1024
KD = D // P
EPS = 1e-6
FF_HALF = 11
SLOT = 2048
ARENA = 31744
SPLIT = 24576
TAIL = 1536


class Signal:

    def __init__(self, nc, ctx, name):
        self.sem = ctx.enter_context(nc.semaphore(name))
        self.base = 0
        self.total = 0

    def up(self, amount=1):
        self.total += amount
        return self.sem

    def count(self, n):
        return n + self.base


class Chain:

    def __init__(self, nc, ctx, name):
        self.sem = ctx.enter_context(nc.semaphore(name))
        self.n, self.loop, self.j = 0, None, 0

    def enter(self, i, per_turn):
        self.loop, self.j = (i, per_turn), 0

    def leave(self, turns):
        assert self.j == self.loop[1], (self.j, self.loop[1])
        self.n += turns * self.loop[1]
        self.loop, self.j = None, 0

    def up(self):
        if self.loop:
            self.j += 1
        else:
            self.n += 1
        return self.sem

    def now(self):
        return self.n if not self.loop else self.loop[0] * self.loop[1] + (self.n + self.j)


class Segment:

    def __init__(self, src, n, k, tiles, cols=None):
        self.src, self.n, self.k, self.tiles = src, n, k, tiles
        self.cols = cols or tiles * P
        self.size = k * self.cols
        self.g0 = None


class Unit:
    def __init__(self, seg, u, parity, i, turns):
        self.seg, self.u, self.turns = seg, u, turns
        self.slot = (seg.g0 + parity) % 2
        self.use = (seg.g0 + parity) // 2 + i
        self.g = u + seg.g0
        self.parity, self.turn = parity, i


class Machine:

    def __init__(self, nc, ctx):
        self.nc, self.ctx = nc, ctx
        self.signals = {}
        sb = lambda name, shape, dt=F32: ctx.enter_context(nc.sbuf_tensor(name, shape, dt))
        self.h = sb("h", [P, KD, T])
        self.rounded_names = {}
        for name, shape, split in (("ring", [P, 3, 2, SLOT], 6 * SLOT), ("arena", [P, ARENA], SPLIT)):
            with nc.sbuf_tensor(name, shape, F32) as plain:
                pass
            rounded = sb(name + "_rounded", [P, split], F32R)
            self.rounded_names[name] = rounded
            if name == "ring":
                self.ring = plain
            else:
                sb("arena_rest", [P, ARENA - SPLIT])
                self.arena = plain
        self.tail = sb("tail", [P, TAIL])
        self.ident = sb("ident", [P, P])
        self.ones = sb("ones", [P, 1])
        self.cum = sb("cum", [P, 2, P])
        self.bar = sb("bar", [P, 2, P])
        self.lev = sb("lev", [P, 2, 7, P], BF16)
        self.small = sb("small", [P, 288])
        self.gcols = sb("gcols", [P, 6, 96])
        self.mods = sb("mods", [P, 48, 2])
        self.psum = ctx.enter_context(nc.psum_tensor("psum", [P, 8, 512], F32))
        self.raw_full = [ctx.enter_context(nc.semaphore(f"raw_full{s}")) for s in range(2)]
        self.hi_done = ctx.enter_context(nc.semaphore("hi_done"))
        self.lo_done = ctx.enter_context(nc.semaphore("lo_done"))
        self.vchain = Chain(nc, ctx, "vector_order")
        self.achain = Chain(nc, ctx, "scalar_order")
        self.gchain = Chain(nc, ctx, "gpsimd_order")
        self.segments, self.units = [], []

    def sig(self, name):
        if name not in self.signals:
            self.signals[name] = Signal(self.nc, self.ctx, name)
        return self.signals[name]

    def sem(self, name):
        return self.sig(name).sem

    def count(self, name, n):
        return self.sig(name).count(n)

    def up(self, name, amount=1):
        return self.sig(name).up(amount)

    def end_stage(self):
        for s in self.signals.values():
            s.base += s.total
            s.total = 0

    def at(self, offset, *shape):
        n = int(np.prod(shape))
        v = self.arena[:, offset:offset + n] if offset < ARENA else self.tail[:, offset - ARENA:offset - ARENA + n]
        if len(shape) == 2:
            v = v.rearrange("p (a b) -> p a b", b=shape[1])
        if len(shape) == 3:
            v = v.rearrange("p (a b c) -> p a b c", b=shape[1], c=shape[2])
        return v

    def rounded(self, view):
        rounded = self.rounded_names[view.tensor.name]
        ap = [[rounded.shape[1], P]] + [list(x) for x in view.ap][1:]
        return bass.AP(tensor=rounded, offset=view.offset, ap=ap)

    def plan(self, segments):
        for seg in segments:
            seg.g0 = len(self.units)
            self.units += [(seg, u) for u in range(seg.n)]
        self.segments = segments

    def walk(self, eng, seg, body, chain=None, per_turn=0, head=2):
        pairs = max(0, (seg.n - 2 - head) // 2)
        if pairs < 2:
            pairs = 0
        for u in range(head if pairs else 0):
            body(Unit(seg, u, u % 2, u // 2, 1))
        if pairs:
            with eng.Fori(0, pairs) as i:
                if chain:
                    chain.enter(i, per_turn)
                for p in range(2):
                    body(Unit(seg, i * 2 + (head + p), p, i + head // 2, pairs))
                if chain:
                    chain.leave(pairs)
        for u in range(head + 2 * pairs if pairs else 0, seg.n):
            body(Unit(seg, u, u % 2, u // 2, 1))

    def ahead(self, unit):
        if not isinstance(unit.u, int):
            return unit.seg, unit.u + 2
        g = unit.g + 2
        return self.units[g] if g < len(self.units) else None

    def load(self, sp, seg, u, slot):
        src = seg.src[u] if isinstance(u, int) else \
            seg.src[bass.ds(u, 1), :, :].rearrange("a p f -> (a p) f")
        sp.dma_start(self.ring[:, 0, slot, 0:seg.size], src).then_inc(self.raw_full[slot], 16)

    def sp_unit(self, sp, unit):
        nxt = self.ahead(unit)
        if nxt:
            sp.wait_ge(self.lo_done, unit.g + 1)
            self.load(sp, nxt[0], nxt[1], unit.slot)

    def split_hi(self, dve, seg, slot, use):
        dve.wait_ge(self.raw_full[slot], (use + 1) * 16)
        dve.tensor_copy(self.rounded(self.ring[:, 1, slot, 0:seg.size]),
                        self.ring[:, 0, slot, 0:seg.size]).then_inc(self.hi_done, 1)

    def split_lo(self, pool, seg, slot, g):
        pool.wait_ge(self.hi_done, g + 1)
        pool.tensor_tensor(self.rounded(self.ring[:, 2, slot, 0:seg.size]), self.ring[:, 0, slot, 0:seg.size],
                           self.rounded(self.ring[:, 1, slot, 0:seg.size]).bitcast(F32),
                           ALU.subtract).then_inc(self.lo_done, 1)

    def dve_unit(self, dve, unit):
        nxt = self.ahead(unit)
        if nxt:
            self.split_hi(dve, nxt[0], unit.slot, unit.use + 1)

    def pool_unit(self, pool, unit):
        nxt = self.ahead(unit)
        if nxt:
            self.split_lo(pool, nxt[0], unit.slot, unit.g + 2)

    def product(self, pe, out, weights, moving, start, stop):
        (wh, wl), (xh, xl) = weights, moving
        r = self.rounded
        pe.matmul(out, r(wh), r(xh), start=start, stop=False)
        pe.matmul(out, r(wh), r(xl), start=False, stop=False)
        return pe.matmul(out, r(wl), r(xh), start=False, stop=stop)


class Dense:

    def __init__(self, m, seg, halves, ready=False, last=(None, 0)):
        self.m, self.seg, self.halves, self.ready = m, seg, halves, ready
        self.last_name, self.last_count = last

    def weights(self, unit, k, t):
        o = k * self.seg.cols + t * P
        return [self.m.ring[:, part, unit.slot, o:o + P] for part in (1, 2)]

    def pe_unit(self, pe, unit):
        m, seg = self.m, self.seg
        pe.wait_ge(m.lo_done, unit.g + 1)
        first = isinstance(unit.u, int) and unit.u == 0
        order = [(t, k) for t in range(seg.tiles) for k in range(seg.k)]
        if first and self.ready:
            order.sort(key=lambda tk: tk[1])
        for t, k in order:
            if first and self.ready and t == 0:
                pe.wait_ge(m.sem("xready"), m.count("xready", k + 1))
            if first and self.last_name and t == 0 and k == seg.k - 1:
                pe.wait_ge(m.sem(self.last_name), m.count(self.last_name, self.last_count))
            last = m.product(pe, m.psum[:, 2 * unit.slot + t, :], self.weights(unit, k, t),
                             self.halves(k), k == 0, k == seg.k - 1)
            if k == seg.k - 1:
                last.then_inc(m.up("done", unit.turns), 1)


def split_in_place(m, dve, hi, lo, ready, times=1):
    dve.tensor_copy(m.rounded(hi), lo).then_inc(m.vchain.up(), 1)
    dve.wait_ge(m.vchain.sem, m.vchain.now())
    dve.tensor_tensor(m.rounded(lo), lo, m.rounded(hi).bitcast(F32), ALU.subtract).then_inc(ready.up(times), 1)


def rstd_pe_sums(m, pe, acc, cols, bank, sig="ssq"):
    for i in range(cols):
        last = pe.matmul(m.psum[:, bank, i:i + 1], acc[:, i * P:(i + 1) * P], m.ones[:, 0:1],
                         start=True, stop=True)
    last.then_inc(m.up(sig), 1)


def rstd_dve_mean(m, dve, psum, mean, scale, eps=EPS):
    dve.tensor_scalar(mean, psum, scale, eps, ALU.mult, ALU.add).then_inc(m.up("mean"), 1)


def rstd_pool(m, pool, mean, half, out, count):
    pool.wait_ge(m.sem("mean"), m.count("mean", count))
    pool.tensor_tensor(out, mean, half, ALU.pow).then_inc(m.up("root"), 1)


def rstd_newton(m, dve, mean, root, tmp, sig):
    c = m.vchain
    dve.tensor_tensor(tmp, root, root, ALU.mult).then_inc(c.up(), 1)
    dve.wait_ge(c.sem, c.now())
    dve.tensor_tensor(tmp, tmp, mean, ALU.mult).then_inc(c.up(), 1)
    dve.wait_ge(c.sem, c.now())
    dve.tensor_scalar(tmp, tmp, -0.5, 1.5, ALU.mult, ALU.add).then_inc(c.up(), 1)
    dve.wait_ge(c.sem, c.now())
    dve.tensor_tensor(root, root, tmp, ALU.mult).then_inc(sig.up(), 1)


def rstd_pe_spread(m, pe, root, cols, out):
    for i in range(cols):
        last = pe.matmul(out(i), root[:, i:i + 1].broadcast_to([P, P]), m.ident[:, :],
                         start=True, stop=True)
    last.then_inc(m.up("spread"), 1)


S_MEAN, S_ROOT, S_TMP, S_HALF = 0, 6, 12, 18


def norm_stage_parts(m, acc, gain, xh, xl, final=False, shift=None):
    mean, root = m.small[:, S_MEAN:S_MEAN + 4], m.small[:, S_ROOT:S_ROOT + 4]
    tmp, half = m.small[:, S_TMP:S_TMP + 4], m.small[:, S_HALF:S_HALF + 4]

    def pe_part(pe):
        rstd_pe_sums(m, pe, acc, 4, 7)
        pe.wait_ge(m.sem("rstd"), m.count("rstd", 1))
        rstd_pe_spread(m, pe, root, 4, lambda i: m.psum[:, 6, i * P:(i + 1) * P])

    def dve_part(dve):
        dve.wait_ge(m.sem("ssq"), m.count("ssq", 1))
        rstd_dve_mean(m, dve, m.psum[:, 7, 0:4], mean, 1.0 / D)
        dve.wait_ge(m.sem("root"), m.count("root", 1))
        rstd_newton(m, dve, mean, root, tmp, m.sig("rstd"))
        dve.wait_ge(m.sem("spread"), m.count("spread", 1))
        if final:
            for k in range(KD):
                normed(dve, k, "xready")
            return
        for k in range(KD + 1):
            if k < KD:
                normed(dve, k, "xnormed")
            if k:
                hi, lo = m.rounded(xh[:, k - 1, :]).bitcast(F32), xl[:, k - 1, :]
                dve.wait_ge(m.sem("xnormed"), m.count("xnormed", k))
                dve.wait_ge(m.sem("xhigh"), m.count("xhigh", k))
                if shift is None:
                    dve.tensor_tensor(m.rounded(lo), lo, hi, ALU.subtract).then_inc(m.up("xready"), 1)
                else:
                    dve.scalar_tensor_tensor(m.rounded(lo), lo, shift[:, k - 1:k], hi, ALU.add,
                                             ALU.subtract).then_inc(m.up("xready"), 1)

    def normed(dve, k, signal):
        dve.scalar_tensor_tensor(xl[:, k, :], m.h[:, k, :], gain[:, k:k + 1], m.psum[:, 6, :],
                                 ALU.mult, ALU.mult).then_inc(m.up(signal), 1)

    def act_part(act):
        for k in range(KD):
            act.wait_ge(m.sem("xnormed"), m.count("xnormed", k + 1))
            act.activation(m.rounded(xh[:, k, :]), xl[:, k, :], ACT.Identity,
                           bias=0.0 if shift is None else shift[:, k:k + 1]).then_inc(m.up("xhigh"), 1)

    def pool_part(pool):
        rstd_pool(m, pool, mean, half, root, 1)

    return pe_part, act_part, dve_part, pool_part


ACC_AT = ARENA + TAIL - T


def pick(view, i):
    if isinstance(i, int):
        return view[:, i, :]
    return view[:, bass.ds(i, 1), :].rearrange("p a b -> p (a b)")


def col(view, i):
    return view[:, i:i + 1] if isinstance(i, int) else view[:, bass.ds(i, 1)]


class Residual:

    def __init__(self, m, seg, tile0, done0, freed0, squares, sq_at=None, scale=None, final_sum=False):
        self.m, self.seg, self.done0, self.freed0 = m, seg, done0, freed0
        self.squares, self.scale = squares, scale
        self.acc = m.at(ACC_AT, T)
        self.sq = m.at(sq_at, 2, T) if squares else None

    def tile(self, unit, t):
        return unit.u * self.seg.tiles + t

    def dve_unit(self, dve, unit):
        m, tiles = self.m, self.seg.tiles
        dve.wait_ge(m.sem("done"), m.count("done", self.done0 + (unit.u + 1) * tiles))
        m.dve_unit(dve, unit)
        for t in range(tiles):
            tile = self.tile(unit, t)
            h = pick(m.h, tile)
            bank = m.psum[:, 2 * unit.slot + t, :]
            if self.scale is None:
                ins = dve.tensor_tensor(h, bank, h, ALU.add)
            else:
                ins = dve.scalar_tensor_tensor(h, bank, col(self.scale, tile), h, ALU.mult, ALU.add)
            ins.then_inc(m.up("freed", unit.turns), 1)
            if self.squares and not (isinstance(tile, int) and tile < 2):
                self.add_square(dve, tile - 1, unit, t)

    def slot_of(self, tile, unit, t):
        if isinstance(tile, int):
            return tile % 2
        return (unit.seg.tiles * ((unit.slot - unit.seg.g0) % 2) + t) % 2

    def add_square(self, dve, tile, unit, t):
        m = self.m
        dve.wait_ge(m.sem("square"), m.count("square", tile + 1))
        dve.wait_ge(m.sem("summed"), m.count("summed", tile - 1))
        slot = tile % 2 if isinstance(tile, int) else 1 - self.slot_of(tile + 1, unit, t)
        ins = dve.tensor_tensor(self.acc, self.acc, self.sq[:, slot, :], ALU.add)
        ins.then_inc(m.up("summed", unit.turns), 1)

    def dve_end(self, dve):
        if self.squares:
            self.add_square(dve, KD - 1, Unit(self.seg, self.seg.n - 1, 0, 0, 1), 0)

    def act_unit(self, act, unit):
        if not self.squares:
            return
        m = self.m
        for t in range(self.seg.tiles):
            tile = self.tile(unit, t)
            act.wait_ge(m.sem("freed"), m.count("freed", self.freed0 + tile + 1))
            if not (isinstance(tile, int) and tile < 3):
                act.wait_ge(m.sem("summed"), m.count("summed", tile - 2))
            out = self.acc if isinstance(tile, int) and tile == 0 else \
                self.sq[:, self.slot_of(tile, unit, t), :]
            act.activation(out, pick(m.h, tile), ACT.Square).then_inc(m.up("square", unit.turns), 1)


def run_stage(m, parts):
    with m.nc.Block() as block:
        @block.sync
        def _(sp):
            parts["sp"](sp)

        @block.tensor
        def _(pe):
            parts["pe"](pe)

        @block.scalar
        def _(act):
            if "act" in parts:
                parts["act"](act)

        @block.vector
        def _(dve):
            parts["dve"](dve)

        @block.gpsimd
        def _(pool):
            parts["pool"](pool)
    m.end_stage()


def begin_stage(m, loads):
    def sp(sp):
        for slot in range(2):
            m.load(sp, *m.units[slot], slot)
        for view, src in loads:
            sp.dma_start(view, src).then_inc(m.up("loaded", 16), 16)

    def dve(dve):
        dve.memset(m.small[:, S_HALF:S_HALF + 6], -0.5).then_inc(m.vchain.up(), 1)
        dve.wait_ge(m.vchain.sem, m.vchain.now())
        for slot in range(2):
            m.split_hi(dve, m.units[slot][0], slot, 0)
        dve.wait_ge(m.sem("loaded"), m.count("loaded", 16 * len(loads)))
        acc, sq = m.at(ACC_AT, T), m.at(0, T)
        dve.tensor_tensor(acc, m.h[:, 0, :], m.h[:, 0, :], ALU.mult).then_inc(m.vchain.up(), 1)
        dve.wait_ge(m.vchain.sem, m.vchain.now())
        for k in range(1, KD):
            dve.tensor_tensor(sq, m.h[:, k, :], m.h[:, k, :], ALU.mult).then_inc(m.vchain.up(), 1)
            dve.wait_ge(m.vchain.sem, m.vchain.now())
            dve.tensor_tensor(acc, acc, sq, ALU.add).then_inc(m.vchain.up(), 1)
            dve.wait_ge(m.vchain.sem, m.vchain.now())

    def pool(pool):
        for slot in range(2):
            m.split_lo(pool, m.units[slot][0], slot, slot)

    run_stage(m, dict(sp=sp, pe=lambda e: None, dve=dve, pool=pool))


COND_AT, MOD_W_AT, MOD_TMP_AT = 22528, 24576, 30720


class Modulation:

    def __init__(self, m, src, cond_src, layer):
        self.m, self.src, self.cond_src, self.layer = m, src, cond_src, layer
        self.cond = m.at(COND_AT, 2, D)
        self.sums = m.mods[:, :, :].rearrange("p a b -> p (a b)")

    def place(self, unit, half, up):
        if not up:
            return 44 + 2 * self.layer + unit.u, self.m.at(MOD_W_AT + D * (4 + unit.u), D), \
                f"mod_extra_loaded{unit.u}", "mod_extra_used"
        return unit.u + (2 * self.layer + half) * FF_HALF, self.m.at(MOD_W_AT + D * (2 * half + unit.parity), D), \
            f"mod_loaded{half}{unit.parity}", f"mod_used{half}"

    def sp_begin(self, sp):
        sp.dma_start(self.cond[:, :, :].rearrange("p a b -> p (a b)"), self.cond_src).then_inc(
            self.m.up("cond_loaded", 16), 16)

    def act_begin(self, act):
        m = self.m
        act.wait_ge(m.sem("cond_loaded"), m.count("cond_loaded", 16))
        act.activation(self.cond, self.cond, ACT.Silu).then_inc(m.up("cond"), 1)

    def sp_unit(self, sp, unit, half, up):
        m = self.m
        tile, buffer, loaded, used = self.place(unit, half, up)
        if up and not (isinstance(unit.u, int) and unit.u < 2):
            sp.wait_ge(m.sem(used), m.count(used, unit.u - 1))
        src = self.src[tile] if isinstance(tile, int) else self.src[bass.ds(tile, 1), :, :].rearrange("a p f -> (a p) f")
        sp.dma_start(buffer, src).then_inc(m.up(loaded, 16 * unit.turns), 16)

    def dve_unit(self, dve, unit, half, up):
        m = self.m
        tile, buffer, loaded, used = self.place(unit, half, up)
        if up and half == 0 and isinstance(unit.u, int) and unit.u == 0:
            dve.wait_ge(m.sem("cond"), m.count("cond", 1))
        dve.wait_ge(m.sem(loaded), m.count(loaded, (unit.turn + 1) * 16 if up else 16))
        tmp = m.at(MOD_TMP_AT, D)
        dve.scalar_tensor_tensor(tmp, buffer, 1.0, self.cond[:, 0, :], ALU.mult, ALU.mult,
                                 accum_out=col(self.sums, tile * 2)).then_inc(m.vchain.up(), 1)
        dve.wait_ge(m.vchain.sem, m.vchain.now())
        dve.scalar_tensor_tensor(tmp, buffer, 1.0, self.cond[:, 1, :], ALU.mult, ALU.mult,
                                 accum_out=col(self.sums, tile * 2 + 1)).then_inc(m.up(used, unit.turns), 1)
        dve.wait_ge(m.sem(used), m.count(used, unit.u + 1))


def ffn_stage(m, segs, gain, taps, mod):
    xh, xl = m.at(0, KD, T), m.at(4096, KD, T)
    ah, al = m.at(8192, FF_HALF, T), m.at(8192 + FF_HALF * T, FF_HALF, T)
    tmp = m.at(8192 + 2 * FF_HALF * T, 2, 2, T)
    sq_at = 8192 + 2 * FF_HALF * T + 4 * T
    npe, nact, ndve, npool = norm_stage_parts(m, m.at(ACC_AT, T), gain, xh, xl)
    up = [Dense(m, s, lambda k: (xh[:, k, :], xl[:, k, :]), i == 0)
          for i, s in ((0, segs[0]), (2, segs[2]))]
    down = [Dense(m, segs[2 * i + 1], lambda k: (ah[:, k, :], al[:, k, :]), last=("actready", (i + 1) * FF_HALF))
            for i in range(2)]
    U, Dn = FF_HALF, KD
    per_half = 2 * U + Dn
    res = [Residual(m, segs[2 * i + 1], 0, i * per_half + 2 * U, i * per_half + 2 * U, i == 1, sq_at)
           for i in range(2)]

    def sp(sp):
        mod.sp_begin(sp)
        for half in range(2):

            def up_unit(unit):
                m.sp_unit(sp, unit)
                mod.sp_unit(sp, unit, half, True)

            def down_unit(unit):
                m.sp_unit(sp, unit)
                if half == 0 and isinstance(unit.u, int) and unit.u < 2:
                    mod.sp_unit(sp, unit, half, False)

            m.walk(sp, segs[2 * half], up_unit)
            m.walk(sp, segs[2 * half + 1], down_unit)

    def pe(pe):
        npe(pe)
        for half in range(2):
            f0 = half * per_half

            def up_unit(unit):
                if not isinstance(unit.u, int) or unit.u >= 2:
                    pe.wait_ge(m.sem("freed"), m.count("freed", f0 + (unit.u - 1) * 2))
                elif half:
                    pe.wait_ge(m.sem("freed"), m.count("freed", f0 - 1 + unit.u))
                up[half].pe_unit(pe, unit)

            def down_unit(unit):
                if not isinstance(unit.u, int) or unit.u >= 2:
                    pe.wait_ge(m.sem("freed"), m.count("freed", f0 + 2 * U + unit.u - 1))
                else:
                    pe.wait_ge(m.sem("freed"), m.count("freed", f0 + 2 * U - 2 + 2 * unit.u))
                if isinstance(unit.u, int) and unit.u == 0:
                    pe.wait_ge(m.sem("actready"), m.count("actready", (half + 1) * U - 1))
                down[half].pe_unit(pe, unit)

            m.walk(pe, segs[2 * half], up_unit)
            m.walk(pe, segs[2 * half + 1], down_unit)

    def act(act):
        nact(act)
        mod.act_begin(act)
        for half in range(2):
            f0 = half * per_half

            def up_unit(unit):
                for t in range(2):
                    c = (unit.u * 2 + (half * 2 * U + t)) * 4
                    act.wait_ge(m.sem("done"), m.count("done", f0 + unit.u * 2 + (t + 1)))
                    if t == 0 and not (isinstance(unit.u, int) and half * U + unit.u < 2):
                        act.wait_ge(m.sem("actready"), m.count("actready", half * U + unit.u - 1))
                    act.activation(
                        tmp[:, unit.slot, t, :], m.psum[:, 2 * unit.slot + t, :], ACT.Identity,
                        bias=col(taps, c + 3), scale=col(taps, c + 2)).then_inc(m.up("tapped", unit.turns), 1)
                act.wait_ge(m.sem("freed"), m.count("freed", f0 + unit.u * 2 + 1))
                gate = tmp[:, unit.slot, 0, :]
                act.activation(gate, gate, ACT.Silu).then_inc(m.up("silu", unit.turns), 1)

            m.walk(act, segs[2 * half], up_unit)
            m.walk(act, segs[2 * half + 1], lambda unit: res[half].act_unit(act, unit))

    def dve(dve):
        ndve(dve)
        for half in range(2):
            f0 = half * per_half

            def up_unit(unit):
                dve.wait_ge(m.sem("done"), m.count("done", f0 + unit.u * 2 + 2))
                m.dve_unit(dve, unit)
                for t in range(2):
                    c = (unit.u * 2 + (half * 2 * U + t)) * 4
                    out, bank = tmp[:, unit.slot, t, :], m.psum[:, 2 * unit.slot + t, :]
                    dve.wait_ge(m.sem("tapped"), m.count("tapped", (half * U + unit.u) * 2 + (t + 1)))
                    dve.scalar_tensor_tensor(
                        out[:, 1:T], bank[:, 0:T - 1], col(taps, c + 1), out[:, 1:T], ALU.mult, ALU.add).then_inc(m.vchain.up(), 1)
                    dve.wait_ge(m.vchain.sem, m.vchain.now())
                    dve.scalar_tensor_tensor(
                        out[:, 2:T], bank[:, 0:T - 2], col(taps, c), out[:, 2:T], ALU.mult, ALU.add).then_inc(m.up("freed", unit.turns), 1)
                dve.wait_ge(m.sem("silu"), m.count("silu", half * U + unit.u + 1))
                dve.wait_ge(m.sem("freed"), m.count("freed", f0 + unit.u * 2 + 2))
                hi, lo = pick(ah, unit.u), pick(al, unit.u)
                dve.tensor_tensor(lo, tmp[:, unit.slot, 0, :], tmp[:, unit.slot, 1, :],
                                                     ALU.mult).then_inc(m.vchain.up(), 1)
                dve.wait_ge(m.vchain.sem, m.vchain.now())
                split_in_place(m, dve, hi, lo, m.sig("actready"), unit.turns)
                mod.dve_unit(dve, unit, half, True)

            def down_unit(unit):
                res[half].dve_unit(dve, unit)
                if half == 0 and isinstance(unit.u, int) and unit.u < 2:
                    mod.dve_unit(dve, unit, half, False)

            m.walk(dve, segs[2 * half], up_unit, m.vchain, 10)
            m.walk(dve, segs[2 * half + 1], down_unit)
            res[half].dve_end(dve)

    def pool(pool):
        npool(pool)
        for seg in segs:
            m.walk(pool, seg, lambda unit: m.pool_unit(pool, unit))

    run_stage(m, dict(sp=sp, pe=pe, act=act, dve=dve, pool=pool))


def renorm_stage(m, gain, mod_bias):
    out = m.at(0, KD, T)
    npe, nact, ndve, npool = norm_stage_parts(m, m.at(ACC_AT, T), gain, None, out, final=True)

    def pe(pe):
        npe(pe)

    def act(act):
        sq = m.at(4096, 2, T)
        for k in range(KD):
            act.wait_ge(m.sem("xready"), m.count("xready", k + 1))
            act.activation(m.h[:, k, :], out[:, k, :], ACT.Copy).then_inc(m.up("copied"), 1)
            if k >= 3:
                act.wait_ge(m.sem("summed"), m.count("summed", k - 2))
            act.activation(m.at(ACC_AT, T) if k == 0 else sq[:, k % 2, :],
                                               out[:, k, :], ACT.Square).then_inc(m.up("square"), 1)

    def dve(dve):
        b = mod_bias.rearrange("p (a b) -> p a b", b=1).broadcast_to([P, 48, 2])
        dve.tensor_tensor(m.mods[:, :, :], m.mods[:, :, :], b, ALU.add).then_inc(m.vchain.up(), 1)
        dve.wait_ge(m.vchain.sem, m.vchain.now())
        ndve(dve)
        acc, sq = m.at(ACC_AT, T), m.at(4096, 2, T)
        for k in range(1, KD):
            dve.wait_ge(m.sem("square"), m.count("square", k + 1))
            dve.wait_ge(m.sem("summed"), m.count("summed", k - 1))
            dve.tensor_tensor(acc, acc, sq[:, k % 2, :], ALU.add).then_inc(m.up("summed"), 1)

    run_stage(m, dict(sp=lambda sp: None, pe=pe, act=act, dve=dve, pool=lambda pool: npool(pool)))


def store_stage(m, out):
    def sp(sp):
        s = m.sig("stored")
        sp.dma_start(out.rearrange("(k p) t -> p k t", p=P), m.h[:, :, :]).then_inc(s.up(16), 16)
        sp.wait_ge(s.sem, s.count(16))
    nop = lambda e: None
    run_stage(m, dict(sp=sp, pe=nop, dve=nop, pool=nop))


def softplus_abs(m, dve, x, mag):
    dve.tensor_scalar(mag, x, -1.0, None, ALU.mult).then_inc(m.vchain.up(), 1)
    dve.wait_ge(m.vchain.sem, m.vchain.now())
    dve.tensor_tensor(mag, mag, x, ALU.max).then_inc(m.up("magnitude"), 1)


def softplus_exp(m, act, mag, y, count=1):
    act.wait_ge(m.sem("magnitude"), m.count("magnitude", count))
    act.activation(y, mag, ACT.Exp, scale=-1.0).then_inc(m.up("decayed"), 1)


def softplus_sum(m, dve, x, y, z, acc, out, count=1):
    c = m.vchain
    dve.wait_ge(m.sem("decayed"), m.count("decayed", count))
    dve.tensor_scalar(z, y, 2.0, None, ALU.add).then_inc(c.up(), 1)
    dve.wait_ge(c.sem, c.now())
    dve.reciprocal(z, z).then_inc(c.up(), 1)
    dve.wait_ge(c.sem, c.now())
    dve.tensor_tensor(z, z, y, ALU.mult).then_inc(c.up(), 1)
    dve.wait_ge(c.sem, c.now())
    dve.tensor_tensor(y, z, z, ALU.mult).then_inc(c.up(), 1)
    dve.wait_ge(c.sem, c.now())
    dve.tensor_scalar(acc, y, 1.0 / 17, None, ALU.mult).then_inc(c.up(), 1)
    dve.wait_ge(c.sem, c.now())
    for k in range(7, 0, -1):
        dve.scalar_tensor_tensor(acc, acc, 1.0 / (2 * k + 1), y, ALU.add, ALU.mult).then_inc(c.up(), 1)
        dve.wait_ge(c.sem, c.now())
    dve.scalar_tensor_tensor(acc, acc, 1.0, z, ALU.add, ALU.mult).then_inc(c.up(), 1)
    dve.wait_ge(c.sem, c.now())
    dve.tensor_scalar(acc, acc, 2.0, None, ALU.mult).then_inc(c.up(), 1)
    dve.wait_ge(c.sem, c.now())
    dve.scalar_tensor_tensor(out, x, 0.0, acc, ALU.max, ALU.add).then_inc(c.up(), 1)
    dve.wait_ge(c.sem, c.now())


GATES_AT = 20480 + 4 * T


def lru_stage(m, seg_in, seg_out, v, gates_w):
    xh, xl = m.at(0, KD, T), m.at(4096, KD, T)
    xc, ga = m.at(8192, 4, T), m.at(10240, 4, T)
    ct, cv, bv = m.at(24576, 2, T), m.at(12288, 4, T), m.at(14336, 4, T)
    yh, yl = m.at(16384, KD, T), m.at(20480, KD, T)
    lru = [[m.at(25600 + (7 * p + i) * T, T) for i in range(7)] for p in range(2)]
    sp8 = m.small[:, 24:28]
    s = [m.small[:, 28 + 4 * i:32 + 4 * i] for i in range(5)]
    npe, nact, ndve, npool = norm_stage_parts(m, m.at(ACC_AT, T), v["mix0_norm"], xh, xl)
    din = Dense(m, seg_in, lambda k: (xh[:, k, :], xl[:, k, :]), True)
    dout = Dense(m, seg_out, lambda k: (yh[:, k, :], yl[:, k, :]), last=("yready", 8))
    res = Residual(m, seg_out, 0, 20, 12, True, sq_at=0)
    bank = lambda unit, t: m.psum[:, 2 * unit.slot + t, :]

    def sp(sp):
        m.walk(sp, seg_in, lambda unit: m.sp_unit(sp, unit))
        m.walk(sp, seg_out, lambda unit: m.sp_unit(sp, unit))

    def pool(pool):
        npool(pool)
        m.walk(pool, seg_in, lambda unit: m.pool_unit(pool, unit))
        m.walk(pool, seg_out, lambda unit: m.pool_unit(pool, unit))

    def units(seg):
        return [Unit(seg, u, u % 2, u // 2, 1) for u in range(seg.n)]

    def pe(pe):
        npe(pe)
        freed = m.sig("freed")

        def lru_gates(j):
            pe.wait_ge(freed.sem, freed.count(j + 1))
            if j >= 2:
                pe.wait_ge(m.sem("sigmoid"), m.count("sigmoid", 2 * (j - 1)))
            for g in range(2):
                pe.matmul(m.psum[:, 4 + 2 * (j % 2) + g, :], gates_w[:, g * 4 + j, :],
                                             xc[:, j, :], start=True, stop=True).then_inc(m.up("gates"), 1)

        for unit in units(seg_in):
            if unit.u in (4, 5):
                pe.wait_ge(m.sem("gelu"), m.count("gelu", 2 * unit.u - 6))
            elif unit.u >= 2:
                pe.wait_ge(freed.sem, freed.count(2 * unit.u - 2 if unit.u < 4 else unit.u - 1))
            din.pe_unit(pe, unit)
            if unit.u in (2, 4):
                lru_gates(unit.u - 2)
                lru_gates(unit.u - 1)
        for unit in units(seg_out):
            pe.wait_ge(freed.sem, freed.count(10 + 2 * unit.u))
            if unit.u == 0:
                pe.wait_ge(m.sem("yready"), m.count("yready", 7))
            dout.pe_unit(pe, unit)

    def act(act):
        softplus_exp(m, act, s[1], s[2])
        nact(act)
        us = units(seg_in)

        def tap(unit):
            for t in range(2):
                j = 2 * unit.u + t
                act.wait_ge(m.sem("done"), m.count("done", j + 1))
                act.activation(xc[:, j, :], bank(unit, t), ACT.Identity,
                                                   bias=col(v["lru_conv_b"], j), scale=col(v["lru_conv_w"], 12 + j)).then_inc(m.up("tapped"), 1)

        def gelu(unit):
            for t in range(2):
                act.wait_ge(m.sem("done"), m.count("done", 2 * unit.u + t + 1))
                act.activation(ga[:, 2 * (unit.u - 2) + t, :], bank(unit, t), ACT.Gelu_apprx_tanh).then_inc(m.up("gelu"), 1)

        def gates(j):
            for g, b in enumerate(("lru_ba", "lru_bx")):
                act.wait_ge(m.sem("gates"), m.count("gates", 2 * j + g + 1))
                act.activation(lru[j % 2][g], m.psum[:, 4 + 2 * (j % 2) + g, :],
                                                    ACT.Sigmoid, bias=col(v[b], j)).then_inc(m.up("sigmoid"), 1)

        def decays(j):
            act.wait_ge(m.sem("sp8"), m.count("sp8", 1))
            act.wait_ge(m.sem("sigmoid"), m.count("sigmoid", 2 * j + 2))
            for g, f in ((2, ACT.Exp), (3, ACT.Tanh)):
                act.activation(lru[j % 2][g], lru[j % 2][0], f,
                                                   scale=col(sp8, j)).then_inc(m.up("decays"), 1)

        def root(j):
            act.wait_ge(m.sem("variance"), m.count("variance", j + 1))
            act.activation(lru[j % 2][6], lru[j % 2][4], ACT.Sqrt, scale=-1.0).then_inc(m.up("rooted"), 1)

        def copy_c(unit):
            j = unit.u - 4
            act.wait_ge(m.sem("done"), m.count("done", 2 * unit.u + 1))
            if j >= 2:
                act.wait_ge(m.sem("freed"), m.count("freed", 4 + j - 1))
            act.activation(ct[:, j % 2, :], bank(unit, 0), ACT.Copy).then_inc(m.up("copied"), 1)

        def tap_b(j):
            act.wait_ge(m.sem("freed"), m.count("freed", 4 + j + 1))
            act.activation(bv[:, j, :], cv[:, j, :], ACT.Identity,
                                                bias=col(v["sconv_b"], j), scale=col(v["sconv_w"], 8 + j)).then_inc(m.up("btapped"), 1)

        tap(us[0]), tap(us[1]), gelu(us[2])
        gates(0), gates(1), decays(0), decays(1)
        gelu(us[3]), copy_c(us[4])
        root(0), root(1), tap_b(0)
        gates(2), gates(3)
        act.wait_ge(m.sem("hidden"), m.count("hidden", 2))
        decays(2), decays(3)
        copy_c(us[5]), tap_b(1), root(2), root(3)
        copy_c(us[6]), tap_b(2), copy_c(us[7]), tap_b(3)
        for unit in units(seg_out):
            res.act_unit(act, unit)

    def dve(dve):
        c = m.vchain
        softplus_neg = v["lru_lambda"]
        dve.tensor_scalar(s[0], softplus_neg, -1.0, None, ALU.mult).then_inc(c.up(), 1)
        dve.wait_ge(c.sem, c.now())
        softplus_abs(m, dve, s[0], s[1])
        ndve(dve)
        softplus_sum(m, dve, s[0], s[2], s[3], s[4], sp8)
        dve.tensor_scalar(sp8, sp8, -8.0, None, ALU.mult).then_inc(m.up("sp8"), 1)
        us = units(seg_in)

        def begin(unit):
            dve.wait_ge(m.sem("done"), m.count("done", 2 * unit.u + 2))
            m.dve_unit(dve, unit)

        def conv_xa(unit):
            begin(unit)
            for t in range(2):
                j = 2 * unit.u + t
                out = xc[:, j, :]
                dve.wait_ge(m.sem("tapped"), m.count("tapped", j + 1))
                for k in range(1, 4):
                    ins = dve.scalar_tensor_tensor(out[:, k:T], bank(unit, t)[:, 0:T - k],
                                                   col(v["lru_conv_w"], (3 - k) * 4 + j), out[:, k:T],
                                                   ALU.mult, ALU.add)
                    if k < 3:
                        ins.then_inc(c.up(), 1)
                        dve.wait_ge(c.sem, c.now())
                    else:
                        ins.then_inc(m.up("freed"), 1)

        def variance(j):
            b = lru[j % 2]
            dve.wait_ge(m.sem("decays"), m.count("decays", 2 * j + 2))
            dve.tensor_tensor(b[4], b[2], b[2], ALU.mult).then_inc(c.up(), 1)
            dve.wait_ge(c.sem, c.now())
            dve.scalar_tensor_tensor(b[4], b[4], 1.0, b[3],
                                                           ALU.add, ALU.mult).then_inc(m.up("variance"), 1)
            dve.wait_ge(m.sem("freed"), m.count("freed", j + 1))
            dve.tensor_tensor(b[5], b[1], xc[:, j, :], ALU.mult).then_inc(c.up(), 1)
            dve.wait_ge(c.sem, c.now())

        def recur(j):
            b = lru[j % 2]
            dve.wait_ge(m.sem("rooted"), m.count("rooted", j + 1))
            dve.tensor_tensor(b[5], b[5], b[6], ALU.mult).then_inc(c.up(), 1)
            dve.wait_ge(c.sem, c.now())
            dve.tensor_tensor_scan(yl[:, j, :], b[2], b[5], 0.0, ALU.mult, ALU.add).then_inc(m.up("hidden"), 1)
            dve.wait_ge(m.sem("hidden"), m.count("hidden", j + 1))
            dve.wait_ge(m.sem("gelu"), m.count("gelu", j + 1))
            dve.tensor_tensor(yl[:, j, :], yl[:, j, :], ga[:, j, :], ALU.mult).then_inc(c.up(), 1)
            dve.wait_ge(c.sem, c.now())
            split_in_place(m, dve, yh[:, j, :], yl[:, j, :], m.sig("yready"))

        def gate_v(unit):
            begin(unit)
            j = unit.u - 4
            dve.wait_ge(m.sem("copied"), m.count("copied", j + 1))
            dve.tensor_tensor(cv[:, j, :], bank(unit, 1), ct[:, j % 2, :], ALU.mult).then_inc(m.up("freed"), 1)

        def conv_b(j):
            dve.wait_ge(m.sem("btapped"), m.count("btapped", j + 1))
            dve.wait_ge(m.sem("freed"), m.count("freed", 4 + j + 1))
            for k in (1, 2):
                dve.scalar_tensor_tensor(bv[:, j, k:T], cv[:, j, 0:T - k],
                                                     col(v["sconv_w"], (2 - k) * 4 + j), bv[:, j, k:T],
                                                     ALU.mult, ALU.add).then_inc(c.up(), 1)
                dve.wait_ge(c.sem, c.now())

        conv_xa(us[0]), conv_xa(us[1])
        begin(us[2]), variance(0), variance(1)
        begin(us[3]), gate_v(us[4])
        recur(0), recur(1), conv_b(0)
        gate_v(us[5]), variance(2), variance(3), conv_b(1)
        gate_v(us[6]), recur(2), conv_b(2)
        gate_v(us[7]), recur(3), conv_b(3)
        for unit in us[8:]:
            begin(unit)
            for t in range(2):
                j = 2 * (unit.u - 8) + t
                dve.tensor_tensor(yl[:, 4 + j, :], bank(unit, t), bv[:, j, :], ALU.mult).then_inc(m.up("freed"), 1)
                dve.wait_ge(m.sem("freed"), m.count("freed", 8 + j + 1))
                split_in_place(m, dve, yh[:, 4 + j, :], yl[:, 4 + j, :], m.sig("yready"))
        for unit in units(seg_out):
            res.dve_unit(dve, unit)
        res.dve_end(dve)

    run_stage(m, dict(sp=sp, pe=pe, act=act, dve=dve, pool=pool))


Q_AT, K_AT, V_AT, U_AT, G_AT, F_AT = 8192, 10240, 12288, 14336, 24576, 26624
Y_AT = 16384
SGU_W_AT, SGU_B_AT, SGU_N_AT = 27136, 28160, 28672
SGU_END = 29184
HEADS, HD = 8, 64
NT = T // P


def unrolled(seg):
    return [Unit(seg, u, u % 2, u // 2, 1) for u in range(seg.n)]


def pe_token_unit(m, pe, unit, halves, tiles=NT):
    pe.wait_ge(m.lo_done, unit.g + 1)
    w = unit.seg.cols
    for i in range(tiles):
        out = m.psum[:, 2 * unit.slot + i // 2, (i % 2) * w:(i % 2 + 1) * w]
        for k in range(unit.seg.k):
            wh, wl = [m.rounded(m.ring[:, part, unit.slot, k * w:(k + 1) * w]) for part in (1, 2)]
            xh, xl = [m.rounded(x[:, i * P:(i + 1) * P]) for x in halves(k)]
            pe.matmul(out, xh, wh, start=k == 0, stop=False)
            pe.matmul(out, xl, wh, start=False, stop=False)
            last = pe.matmul(out, xh, wl, start=False, stop=k == unit.seg.k - 1)
        if i % 2:
            last.then_inc(m.up("done"), 1)


def odd_in_stage(m, seg_in, seg_f, v, loads):
    xh, xl = m.at(0, KD, T), m.at(4096, KD, T)
    q, k_, vt, u_, g_ = [m.at(a, 4, T) for a in (Q_AT, K_AT, V_AT, U_AT, G_AT)]
    fs = [m.at(SGU_END + T * i, T) for i in range(5)]
    gsq = m.at(SGU_END + 5 * T, 2, T)
    cums = m.at(F_AT, T)
    sums, mean, root, tmp = [m.small[:, 32 * i:32 * i + 32] for i in range(2, 6)]
    half = m.small[:, 192:224]
    npe, nact, ndve, npool = norm_stage_parts(m, m.at(ACC_AT, T), v["mix1_norm"], xh, xl)
    halves = lambda k: (xh[:, k, :], xl[:, k, :])
    din = Dense(m, seg_in, halves, True)
    dfg = Dense(m, seg_f, halves)
    bank = lambda unit, t: m.psum[:, 2 * unit.slot + t, :]
    us = unrolled(seg_in) + unrolled(seg_f)

    def sp(sp):
        for unit in us:
            m.sp_unit(sp, unit)
        for view, src in loads:
            sp.dma_start(view, src).then_inc(m.up("loaded", 16), 16)
        sp.wait_ge(m.sem("loaded"), m.count("loaded", 16 * len(loads)))

    def pe(pe):
        npe(pe)
        for n, unit in enumerate(us):
            if n in (2, 3):
                pe.wait_ge(m.sem("afreed"), m.count("afreed", 2 * n - 2))
            elif 4 <= n < 8:
                pe.wait_ge(m.sem("freed"), m.count("freed", 2 * n - 6))
            elif n >= 8:
                pe.wait_ge(m.sem("afreed"), m.count("afreed", 2 * n - 10))
            if n in (4, 5, 8, 9):
                pe_token_unit(m, pe, unit, halves)
            else:
                (dfg if n == 10 else din).pe_unit(pe, unit)

    def act(act):
        nact(act)
        for n in (0, 1, 6, 7, 8, 9):
            for t in range(2):
                act.wait_ge(m.sem("done"), m.count("done", 2 * n + t + 1))
                b = bank(us[n], t)
                if n < 2:
                    ins = act.activation(q[:, 2 * n + t, :], b, ACT.Copy, scale=HD ** -0.5)
                elif n < 8:
                    ins = act.activation(u_[:, 2 * (n - 6) + t, :], b, ACT.Gelu_apprx_tanh)
                else:
                    c = (n - 8) * 256
                    ins = act.activation(g_[:, 2 * t:2 * t + 2, c:c + 256], b.rearrange("p (a b) -> p a b", b=256),
                                         ACT.Gelu_apprx_tanh)
                ins.then_inc(m.up("afreed"), 1)
        softplus_exp(m, act, fs[1], fs[2])

    def dve(dve):
        c = m.vchain
        ndve(dve)
        dve.memset(half, -0.5).then_inc(c.up(), 1)
        dve.wait_ge(c.sem, c.now())
        for n, unit in enumerate(us):
            dve.wait_ge(m.sem("done"), m.count("done", 2 * n + 2 if n < 10 else 21))
            m.dve_unit(dve, unit)
            for t in range(2):
                b = bank(unit, t)
                if n in (2, 3):
                    dve.tensor_copy(k_[:, 2 * (n - 2) + t, :], b).then_inc(m.up("freed"), 1)
                if n in (4, 5):
                    o = (n - 4) * 256
                    dve.tensor_copy(vt[:, 2 * t:2 * t + 2, o:o + 256],
                                                       b.rearrange("p (a b) -> p a b", b=256)).then_inc(m.up("freed"), 1)
        dve.tensor_scalar(fs[0], bank(us[10], 0), v["fox_bf"], -1.0,
                                      ALU.add, ALU.mult).then_inc(c.up(), 1)
        dve.wait_ge(c.sem, c.now())
        softplus_abs(m, dve, fs[0], fs[1])
        dve.wait_ge(m.sem("afreed"), m.count("afreed", 12))
        for i in range(NT):
            dve.tensor_tensor(gsq[:, i % 2, :], g_[:, i, :], g_[:, i, :], ALU.mult).then_inc(c.up(), 1)
            dve.wait_ge(c.sem, c.now())
            dve.tensor_reduce(sums[:, 8 * i:8 * i + 8], gsq[:, i % 2, :].rearrange(
                "p (a b) -> p a b", b=HD), AX.X, ALU.add).then_inc(c.up(), 1)
            dve.wait_ge(c.sem, c.now())
        dve.tensor_scalar(mean, sums, 1.0 / HD, EPS, ALU.mult, ALU.add).then_inc(m.up("mean"), 1)
        softplus_sum(m, dve, fs[0], fs[2], fs[3], fs[4], fs[1])
        dve.memset(fs[4], 1.0).then_inc(c.up(), 1)
        dve.wait_ge(c.sem, c.now())
        dve.tensor_tensor_scan(cums, fs[4], fs[1], 0.0, ALU.mult, ALU.subtract).then_inc(c.up(), 1)
        dve.wait_ge(c.sem, c.now())
        dve.wait_ge(m.sem("root"), m.count("root", 2))
        dve.memset(m.small[:, 0:1], 0.0).then_inc(c.up(), 1)
        dve.wait_ge(c.sem, c.now())
        rstd_newton(m, dve, mean, root, tmp, m.sig("rstd"))
        dve.wait_ge(m.sem("rstd"), m.count("rstd", 2))
        dve.wait_ge(m.sem("loaded"), m.count("loaded", 16 * len(loads)))
        for i in range(NT):
            g3 = g_[:, i, :].rearrange("p (a b) -> p a b", b=HD)
            r3 = root[:, 8 * i:8 * i + 8].rearrange("p (a b) -> p a b", b=1).broadcast_to([P, 8, HD])
            dve.tensor_tensor(g3, g3, r3, ALU.mult).then_inc(c.up(), 1)
            dve.wait_ge(c.sem, c.now())
            dve.tensor_tensor(g_[:, i, :], g_[:, i, :], m.at(SGU_N_AT, T), ALU.mult).then_inc(c.up(), 1)
            dve.wait_ge(c.sem, c.now())
        w = m.at(SGU_W_AT, 8, P)
        lower = m.cum[:, 0:1, :].broadcast_to([P, 8, P])
        dve.tensor_tensor(w, w, lower, ALU.mult).then_inc(c.up(), 1)
        dve.wait_ge(c.sem, c.now())

    def pool(pool):
        npool(pool)
        for unit in us:
            m.pool_unit(pool, unit)
        rstd_pool(m, pool, mean, half, root, 2)

    run_stage(m, dict(sp=sp, pe=pe, act=act, dve=dve, pool=pool))


def fox_stage(m, v):
    q, k_, vt, u_, g_ = [m.at(a, 4, T) for a in (Q_AT, K_AT, V_AT, U_AT, G_AT)]
    yh, yl = m.at(Y_AT, KD, T), m.at(Y_AT + 4096, KD, T)
    cums = m.at(F_AT, T)
    dec = m.at(0, 2, 2, T)
    pr = m.at(2048, 3, T)
    pt = m.at(3584, 2, NT, P)
    negmax, total = m.small[:, 64:96], m.small[:, 96:128]
    w, bias = m.at(SGU_W_AT, 8, P), m.at(SGU_B_AT, 4, P)
    steps = [(h, b) for h in range(HEADS) for b in range(NT)]
    n = len(steps)

    def pe(pe):
        def scores(i):
            h, b = steps[i]
            width = P * (b + 1)
            out = m.psum[:, i % 2, 0:width]
            if i >= 2:
                pe.wait_ge(m.sem("exped"), m.count("exped", i - 1))
            if b == 0:
                pe.wait_ge(m.sem("decrows"), m.count("decrows", 2 * h + 2))
                pe.wait_ge(m.sem("headrows"), m.count("headrows", 2 * h + 2))
            qs = slice(b * P, (b + 1) * P)
            pe.matmul(out, dec[:, h % 2, 0, qs], dec[:, h % 2, 1, 0:width], start=True, stop=False)
            pe.matmul(out[:, b * P:width], m.ident[:, :], m.bar[:, 1, :], start=False, stop=True).then_inc(m.up("scored"), 1)

        def turn(i):
            h, b = steps[i]
            pe.wait_ge(m.sem("normed"), m.count("normed", i + 1))
            if i >= 2:
                pe.wait_ge(m.sem("ptcopied"), m.count("ptcopied", i - 1))
            for j in range(b + 1):
                last = pe.transpose(m.psum[:, 2 + i % 2, j * P:(j + 1) * P], pr[:, i % 3, j * P:(j + 1) * P],
                                    m.ident[:, :])
            last.then_inc(m.up("turned"), 1)

        def values(i):
            h, b = steps[i]
            pe.wait_ge(m.sem("ptcopied"), m.count("ptcopied", i + 1))
            if h % 2 == 0 and b == 0 and h >= 4:
                pe.wait_ge(m.sem("attended"), m.count("attended", h // 2 - 1))
            o = HD * (h % 2)
            for j in range(b + 1):
                last = pe.matmul(m.psum[o:o + HD, 4 + (h // 2) % 2, b * P:(b + 1) * P],
                                 vt[:, j, h * HD:(h + 1) * HD], pt[:, i % 2, j, :], start=j == 0, stop=j == b)
            last.then_inc(m.up("valued"), 1)

        def mix(j):
            if j >= 2:
                pe.wait_ge(m.sem("mixread"), m.count("mixread", j - 1))
            for h in (2 * j, 2 * j + 1):
                o = HD * (h % 2)
                for c in range(NT):
                    last = pe.matmul(m.psum[o:o + HD, 6 + j % 2, c * P:(c + 1) * P],
                                     g_[:, c, h * HD:(h + 1) * HD], w[:, h, :], start=True, stop=True)
            last.then_inc(m.up("mixed"), 1)

        for i in range(n + 3):
            if i < n:
                scores(i)
            if i % 8 == 1 and i < n:
                mix(i // 8)
            if 2 <= i <= n + 1:
                turn(i - 2)
            if i >= 3:
                values(i - 3)

    def act(act):
        for i in range(n + 2):
            if i < n:
                h, b = steps[i]
                width = P * (b + 1)
                act.wait_ge(m.sem("maxed"), m.count("maxed", i + 1))
                if i >= 3:
                    act.wait_ge(m.sem("turned"), m.count("turned", i - 2))
                act.activation(pr[:, i % 3, 0:width], m.psum[:, i % 2, 0:width], ACT.Exp,
                                                  bias=col(negmax, i), accum_out=col(total, i)).then_inc(m.up("exped"), 1)
            if i >= 2:
                b = steps[i - 2][1]
                act.wait_ge(m.sem("turned"), m.count("turned", i - 1))
                if i >= 4:
                    act.wait_ge(m.sem("valued"), m.count("valued", i - 3))
                act.activation(
                    pt[:, i % 2, 0:b + 1, :], m.psum[:, 2 + i % 2, 0:P * (b + 1)].rearrange(
                        "p (a b) -> p a b", b=P), ACT.Copy).then_inc(m.up("ptcopied"), 1)

    def dve(dve):
        c = m.vchain

        def rows(h):
            if h >= 2:
                dve.wait_ge(m.sem("scored"), m.count("scored", 4 * (h - 1)))
            rs = slice(HD - HD * (h % 2), 2 * HD - HD * (h % 2))
            sel = v["fox_select"][rs, :]
            for part in range(2):
                dve.tensor_scalar(dec[rs, h % 2, part, :], cums[rs, :], col(sel, part),
                                                       col(sel, 2 + part * HEADS + h), ALU.mult, ALU.add).then_inc(m.up("decrows"), 1)

        def maxes(i):
            b = steps[i][1]
            dve.wait_ge(m.sem("scored"), m.count("scored", i + 1))
            dve.tensor_reduce(col(negmax, i), m.psum[:, i % 2, 0:P * (b + 1)], AX.X, ALU.max,
                                                 negate=True).then_inc(m.up("maxed"), 1)

        def norms(i):
            b = steps[i][1]
            dve.wait_ge(m.sem("exped"), m.count("exped", i + 1))
            dve.reciprocal(col(total, i), col(total, i)).then_inc(c.up(), 1)
            dve.wait_ge(c.sem, c.now())
            dve.tensor_scalar(pr[:, i % 3, 0:P * (b + 1)], pr[:, i % 3, 0:P * (b + 1)],
                                                  col(total, i), None, ALU.mult).then_inc(m.up("normed"), 1)

        def mixes(j):
            dve.wait_ge(m.sem("mixed"), m.count("mixed", j + 1))
            t = yl[:, j, :]
            dve.tensor_tensor(t.rearrange("p (a b) -> p a b", b=P),
                                                   m.psum[:, 6 + j % 2, :].rearrange("p (a b) -> p a b", b=P),
                                                   bias[:, j:j + 1, :].broadcast_to([P, NT, P]), ALU.add).then_inc(m.up("mixread"), 1)
            dve.wait_ge(m.sem("mixread"), m.count("mixread", j + 1))
            dve.tensor_tensor(t, t, u_[:, j, :], ALU.mult).then_inc(c.up(), 1)
            dve.wait_ge(c.sem, c.now())
            split_in_place(m, dve, yh[:, j, :], t, m.sig("yready"))

        def heads(j):
            dve.wait_ge(m.sem("valued"), m.count("valued", 8 * (j + 1)))
            dve.tensor_copy(yl[:, 4 + j, :], m.psum[:, 4 + j % 2, :]).then_inc(m.up("attended"), 1)
            dve.wait_ge(m.sem("attended"), m.count("attended", j + 1))
            split_in_place(m, dve, yh[:, 4 + j, :], yl[:, 4 + j, :], m.sig("yready"))

        rows(0)
        rows(1)
        for i in range(n + 4):
            if i < n:
                maxes(i)
            if i % 4 == 3 and i < n and i // 4 + 2 < HEADS:
                rows(i // 4 + 2)
            if 1 <= i <= n:
                norms(i - 1)
            if i % 8 == 4 and i < n:
                mixes(i // 8)
            if i >= 11 and (i - 11) % 8 == 0:
                heads((i - 11) // 8)

    def pool(pool):
        for h in range(HEADS):
            if h >= 2:
                pool.wait_ge(m.sem("scored"), m.count("scored", 4 * (h - 1)))
            rs = slice(HD * (h % 2), HD * (h % 2) + HD)
            for part, x in enumerate((q, k_)):
                pool.tensor_copy(dec[rs, h % 2, part, :], x[rs, h // 2, :]).then_inc(m.up("headrows"), 1)

    run_stage(m, dict(sp=lambda e: None, pe=pe, act=act, dve=dve, pool=pool))


def out_stage(m, seg, y_at=None, halves=None, scale=None, sq_at=0):
    halves = halves or (lambda k: (m.at(y_at, KD, T)[:, k, :], m.at(y_at + 4096, KD, T)[:, k, :]))
    dense = Dense(m, seg, halves)
    res = Residual(m, seg, 0, 0, 0, True, sq_at=sq_at, scale=scale)
    us = unrolled(seg)

    def pe(pe):
        for unit in us:
            if unit.u >= 2:
                pe.wait_ge(m.sem("freed"), m.count("freed", 2 * (unit.u - 1)))
            dense.pe_unit(pe, unit)

    def dve(dve):
        for unit in us:
            res.dve_unit(dve, unit)
        res.dve_end(dve)

    run_stage(m, dict(sp=lambda sp: [m.sp_unit(sp, unit) for unit in us], pe=pe,
                      act=lambda act: [res.act_unit(act, unit) for unit in us], dve=dve,
                      pool=lambda pool: [m.pool_unit(pool, unit) for unit in us]))


TA = T + TC
NA = TA // P
XN_AT = 18432
O_AT = 24576
CTX = slice(T, TA)


def gain_dve(m, dve, out, weight, scale):
    dve.scalar_tensor_tensor(out, scale, 1.0, weight, ALU.add, ALU.mult).then_inc(m.vchain.up(), 1)
    dve.wait_ge(m.vchain.sem, m.vchain.now())


def norm2_stage(m, v, ctx):
    xn = m.at(XN_AT, KD, TA)
    acc, accc, sq = m.at(ACC_AT, T), m.at(0, TC), m.at(TC, 2, TC)
    mean, root = m.small[:, S_MEAN:S_MEAN + 6], m.small[:, S_ROOT:S_ROOT + 6]
    tmp, half = m.small[:, S_TMP:S_TMP + 6], m.small[:, S_HALF:S_HALF + 6]
    gains = [m.small[:, 240 + 8 * i:248 + 8 * i] for i in range(2)]

    def sp(sp):
        sp.dma_start(xn[:, :, CTX], ctx.rearrange("(k p) t -> p k t", p=P)).then_inc(m.up("loaded", 16), 16)
        sp.wait_ge(m.sem("loaded"), m.count("loaded", 16))

    def pe(pe):
        pe.wait_ge(m.sem("summed"), m.count("summed", KD))
        rstd_pe_sums(m, pe, acc, 4, 7)
        for i in range(2):
            last = pe.matmul(m.psum[:, 7, 4 + i:5 + i], accc[:, i * P:(i + 1) * P], m.ones[:, 0:1],
                             start=True, stop=True)
        last.then_inc(m.up("ssq"), 1)
        pe.wait_ge(m.sem("rstd"), m.count("rstd", 1))
        rstd_pe_spread(m, pe, root, 6, lambda i: m.psum[:, 5 + i // 4, (i % 4) * P:(i % 4 + 1) * P])

    def act(act):
        act.wait_ge(m.sem("loaded"), m.count("loaded", 16))
        for k in range(KD):
            if k >= 3:
                act.wait_ge(m.sem("summed"), m.count("summed", k - 1))
            act.activation(accc if k == 0 else sq[:, k % 2, :], xn[:, k, CTX], ACT.Square).then_inc(m.up("square"), 1)
        for k in range(KD):
            for i, cols in enumerate((slice(0, T), CTX)):
                act.wait_ge(m.sem("xnormed"), m.count("xnormed", 2 * k + i + 1))
                act.activation(xn[:, k, cols], xn[:, k, cols], ACT.Identity, bias=m.mods[:, k, i:i + 1]).then_inc(
                    m.up("xshifted"), 1)

    def dve(dve):
        for i in range(2):
            gain_dve(m, dve, gains[i], v["norm_attn"], m.mods[:, KD:2 * KD, i])
        for k in range(1, KD):
            dve.wait_ge(m.sem("square"), m.count("square", k + 1))
            dve.wait_ge(m.sem("summed"), m.count("summed", k - 1))
            dve.tensor_tensor(accc, accc, sq[:, k % 2, :], ALU.add).then_inc(m.up("summed"), 1)
        dve.memset(sq[:, 0, 0:1], 0.0).then_inc(m.up("summed"), 1)
        dve.wait_ge(m.sem("ssq"), m.count("ssq", 2))
        rstd_dve_mean(m, dve, m.psum[:, 7, 0:6], mean, 1.0 / D)
        dve.wait_ge(m.sem("root"), m.count("root", 1))
        rstd_newton(m, dve, mean, root, tmp, m.sig("rstd"))
        dve.wait_ge(m.sem("spread"), m.count("spread", 1))
        for k in range(KD):
            for i, (src, cols, bank) in enumerate(((m.h[:, k, :], slice(0, T), 5), (xn[:, k, CTX], CTX, 6))):
                out = xn[:, k, cols]
                dve.scalar_tensor_tensor(out, src, col(gains[i], k), m.psum[:, bank, 0:out.shape[1]],
                                         ALU.mult, ALU.mult).then_inc(m.up("xnormed"), 1)

    run_stage(m, dict(sp=sp, pe=pe, act=act, dve=dve, pool=lambda pool: rstd_pool(m, pool, mean, half, root, 1)))


GH = 4
DK = 128
KT_AT, QT_AT, VT_AT, S_AT = 12288, 15360, 28672, 31744
KTOK_AT, VTOK_AT = 0, 3072
WORK_AT = 6144
BETA, GG, GC, NEG_EG, REST, TOTAL = range(6)


def round_xn(m, act, xh):
    xn = m.at(XN_AT, KD, TA)
    for k in range(KD):
        act.activation(m.rounded(xh[:, k, :]), xn[:, k, :], ACT.Copy).then_inc(m.up("xhigh"), 1)


def split_xn(m, dve, xh, xl):
    xn = m.at(XN_AT, KD, TA)
    for k in range(KD):
        hi, lo = m.rounded(xh[:, k, :]), m.rounded(xl[:, k, :])
        dve.wait_ge(m.sem("xhigh"), m.count("xhigh", k + 1))
        dve.tensor_tensor(lo, xn[:, k, :], hi.bitcast(F32), ALU.subtract).then_inc(m.up("xready"), 1)


def pe_wide_unit(m, pe, unit, halves, wide, ready=False):
    pe.wait_ge(m.lo_done, unit.g + 1)
    if ready:
        for k in range(unit.seg.k):
            pe.wait_ge(m.sem("xready"), m.count("xready", k + 1))
            for t in range(unit.seg.tiles):
                o = k * unit.seg.cols + t * P
                w = [m.ring[:, part, unit.slot, o:o + P] for part in (1, 2)]
                last = m.product(pe, m.psum[:, 2 * unit.slot + t, :], w, [x[:, 0:T] for x in halves(k)],
                                 k == 0, k == unit.seg.k - 1)
                if k == unit.seg.k - 1:
                    last.then_inc(m.up("done"), 1)
        return
    for t in range(unit.seg.tiles):
        for cols, out in ((slice(0, T), m.psum[:, 2 * unit.slot + t, :]),
                          (CTX, m.psum[:, 4 + unit.slot, t * TC:(t + 1) * TC])):
            if cols is CTX and not wide[t]:
                continue
            for k in range(unit.seg.k):
                o = k * unit.seg.cols + t * P
                w = [m.ring[:, part, unit.slot, o:o + P] for part in (1, 2)]
                last = m.product(pe, out, w, [x[:, cols] for x in halves(k)], k == 0, k == unit.seg.k - 1)
        last.then_inc(m.up("done"), 1)


def gdn_in_stage(m, seg, seg_bd, v, group):
    xh, xl = m.at(0, KD, TA), m.at(KD * TA, KD, TA)
    outs = [m.at(QT_AT, GH, T), m.at(KT_AT, GH, TA), m.at(VT_AT, GH, TA)]
    us = unrolled(seg) + (unrolled(seg_bd) if seg_bd else [])
    halves = lambda k: (xh[:, k, :], xl[:, k, :])
    spans = lambda part: [slice(0, T)] + ([CTX] if part else [])
    cols = lambda i: m.gcols[:, i, :]
    sp_t = [m.at(17408 + 96 * i, 96) for i in range(6)]
    ea = m.small[:, 256:272]
    bdb = m.psum[:, 7, 0:NA * 32].rearrange("p (n c) -> p n c", c=32)
    bdt = m.at(S_AT, TA)[0:32, :]
    n3 = lambda x: x.rearrange("p (n c) -> p n c", c=16)
    wide_of = lambda x: x.rearrange("p (a b) -> p a b", a=1).broadcast_to([P, NA, 16])

    def banks(unit, t):
        return m.psum[:, 2 * unit.slot + t, :], m.psum[:, 4 + unit.slot, t * TC:(t + 1) * TC]

    def pe(pe):
        for unit in us[:6]:
            part = unit.u // 2
            if unit.u >= 2:
                pe.wait_ge(m.sem("freed"), m.count("freed", 2 * (unit.u - 1)))
            pe_wide_unit(m, pe, unit, halves, [part > 0] * 2, unit.u == 0)
        if seg_bd:
            unit = us[6]
            pe.wait_ge(m.lo_done, unit.g + 1)
            for x, out in ((slice(0, T), m.psum[0:32, 6, :]), (CTX, m.psum[0:32, 7, TC:2 * TC])):
                for k in range(KD):
                    w = [m.ring[:, part, unit.slot, k * 32:(k + 1) * 32] for part in (1, 2)]
                    last = m.product(pe, out, w, (xh[:, k, x], xl[:, k, x]), k == 0, k == KD - 1)
            last.then_inc(m.up("bdrows"), 1)
            pe.wait_ge(m.sem("bdcopied"), m.count("bdcopied", 2))
            for i in range(NA):
                last = pe.transpose(bdb[:, i, :], bdt[:, i * P:(i + 1) * P], m.ident[0:32, 0:32])
            last.then_inc(m.up("done"), 1)
            pe.wait_ge(m.sem("decays"), m.count("decays", 1))
            g = n3(cols(GG))
            for d in range(2):
                pe.matmul(m.psum[:, 6, 48 * d:48 * d + 48], m.cum[:, d, :], g[:, :, 8 * d:8 * d + 8],
                          start=True, stop=True)
            pe.matmul(m.psum[:, 6, 96:192], m.ones[:, 0:1].broadcast_to([P, P]), cols(GG),
                                         start=True, stop=True).then_inc(m.up("gsums"), 1)

    def act(act):
        n = 0
        round_xn(m, act, xh)
        if seg_bd:
            act.activation(ea, v["gdn_a_log"], ACT.Exp).then_inc(m.up("expa"), 1)
        for unit in us[:6]:
            part = unit.u // 2
            for t in range(2):
                h = 2 * (unit.u % 2) + t
                w = part * 8 + GH * group + h
                act.wait_ge(m.sem("done"), m.count("done", 2 * unit.u + (2 if part else t + 1)))
                for i, span in enumerate(spans(part)):
                    act.activation(outs[part][:, h, span], banks(unit, t)[i], ACT.Copy,
                                                       scale=col(v["conv_qkv"], 2 * 24 + w)).then_inc(m.up("tapped"), 1)
            for t in range(2):
                h = 2 * (unit.u % 2) + t
                act.wait_ge(m.sem("freed"), m.count("freed", 2 * unit.u + t + 1))
                o = outs[part][:, h, :]
                act.activation(o, o, ACT.Silu).then_inc(m.up("silu"), 1)
        if seg_bd:
            act.wait_ge(m.sem("bdrows"), m.count("bdrows", 1))
            act.activation(bdt[:, 0:T], m.psum[0:32, 6, :], ACT.Copy).then_inc(m.up("bdcopied"), 1)
            act.activation(bdt[:, CTX], m.psum[0:32, 7, TC:2 * TC], ACT.Copy).then_inc(m.up("bdcopied"), 1)
            act.wait_ge(m.sem("done"), m.count("done", 13))
            softplus_exp(m, act, sp_t[1], sp_t[2])
            act.activation(n3(cols(BETA)), bdb[:, :, 0:16], ACT.Sigmoid).then_inc(m.up("beta"), 1)
            act.wait_ge(m.sem("gsums"), m.count("gsums", 1))
            act.wait_ge(m.sem("restsum"), m.count("restsum", 1))
            act.activation(cols(NEG_EG), cols(GC), ACT.Exp).then_inc(m.up("edec"), 1)
            act.activation(cols(REST), cols(REST), ACT.Exp).then_inc(m.up("edec"), 1)
            act.activation(cols(TOTAL), m.psum[:, 6, 96:192], ACT.Exp).then_inc(m.up("edec"), 1)

    def dve(dve):
        c = m.vchain
        split_xn(m, dve, xh, xl)
        taps = 0
        for unit in us[:6]:
            part = unit.u // 2
            dve.wait_ge(m.sem("done"), m.count("done", 2 * unit.u + 2))
            m.dve_unit(dve, unit)
            taps += 2 * len(spans(part))
            dve.wait_ge(m.sem("tapped"), m.count("tapped", taps))
            for t in range(2):
                h = 2 * (unit.u % 2) + t
                w = part * 8 + GH * group + h
                for i in (0, 1, 3, 4):
                    s = i - 2
                    for j, span in enumerate(spans(part)):
                        n = span.stop - span.start
                        a, b = max(0, -s), n - max(0, s)
                        o = outs[part][:, h, span.start + a:span.start + b]
                        ins = dve.scalar_tensor_tensor(o, banks(unit, t)[j][:, a + s:b + s],
                                                       col(v["conv_qkv"], i * 24 + w), o, ALU.mult, ALU.add)
                        if i == 4 and j == len(spans(part)) - 1:
                            ins.then_inc(m.up("freed"), 1)
                        else:
                            ins.then_inc(c.up(), 1)
                    if i < 4:
                        dve.wait_ge(c.sem, c.now())
        if seg_bd:
            unit = us[6]
            dve.wait_ge(m.sem("done"), m.count("done", 13))
            m.dve_unit(dve, unit)
            dve.wait_ge(m.sem("expa"), m.count("expa", 1))
            x3 = n3(sp_t[0])
            dve.tensor_tensor(x3, bdb[:, :, 16:32], wide_of(v["gdn_dt_bias"]), ALU.add).then_inc(c.up(), 1)
            dve.wait_ge(c.sem, c.now())
            softplus_abs(m, dve, sp_t[0], sp_t[1])
            softplus_sum(m, dve, sp_t[0], sp_t[2], sp_t[3], sp_t[4], sp_t[5])
            dve.scalar_tensor_tensor(n3(cols(GG)), n3(sp_t[5]), -1.0, wide_of(ea),
                                                         ALU.mult, ALU.mult).then_inc(m.up("decays"), 1)
            dve.wait_ge(m.sem("gsums"), m.count("gsums", 1))
            g4 = cols(GC).rearrange("p (n d h) -> p n d h", d=2, h=8)
            for d in range(2):
                dve.tensor_copy(g4[:, :, d, :], m.psum[:, 6, 48 * d:48 * d + 48].rearrange(
                    "p (n h) -> p n h", h=8)).then_inc(c.up(), 1)
                dve.wait_ge(c.sem, c.now())
            dve.scalar_tensor_tensor(cols(REST), cols(GC), -1.0, m.psum[:, 6, 96:192],
                                                          ALU.mult, ALU.add).then_inc(m.up("restsum"), 1)
            dve.wait_ge(m.sem("edec"), m.count("edec", 3))
            dve.tensor_scalar(cols(NEG_EG), cols(NEG_EG), -1.0, None, ALU.mult).then_inc(c.up(), 1)
            dve.wait_ge(c.sem, c.now())

    run_stage(m, dict(sp=lambda sp: [m.sp_unit(sp, unit) for unit in us], pe=pe, act=act, dve=dve,
                      pool=lambda pool: [m.pool_unit(pool, unit) for unit in us]))


def gdn_token_stage(m):
    kt, qt, vt = m.at(KT_AT, GH, TA), m.at(QT_AT, GH, T), m.at(VT_AT, GH, TA)
    ktok, vtok = m.at(KTOK_AT, NA, GH, P), m.at(VTOK_AT, NA, GH, P)
    qtok, sq = m.at(WORK_AT, NT, GH, P), m.at(WORK_AT + NT * GH * P, 2, GH, P)
    N = NA + NT
    ss, root, tmp = [m.small[:, 40 * i + 24:40 * i + 64] for i in range(3)]
    jobs = [(kt, ktok, i) for i in range(NA)] + [(qt, qtok, i) for i in range(NT)] + [(vt, vtok, i) for i in range(NA)]

    def pe(pe):
        for n, (src, _, i) in enumerate(jobs):
            if n >= 4:
                pe.wait_ge(m.sem("tokcopied"), m.count("tokcopied", n - 3))
            for h in range(GH):
                last = pe.transpose(m.psum[:, n % 4, h * P:(h + 1) * P], src[:, h, i * P:(i + 1) * P], m.ident[:, :])
            last.then_inc(m.up("turned"), 1)
        for n in range(N):
            if n >= 4:
                pe.wait_ge(m.sem("backcopied"), m.count("backcopied", n - 3))
            pe.wait_ge(m.sem("toknormed"), m.count("toknormed", n + 1))
            src = jobs[n][1][:, jobs[n][2]]
            for h in range(GH):
                last = pe.transpose(m.psum[:, 4 + n % 4, h * P:(h + 1) * P], src[:, h, :], m.ident[:, :])
            last.then_inc(m.up("back"), 1)

    def act(act):
        for n, (_, dst, i) in enumerate(jobs):
            act.wait_ge(m.sem("turned"), m.count("turned", n + 1))
            act.activation(dst[:, i].rearrange("p a b -> p (a b)"), m.psum[:, n % 4, :], ACT.Copy).then_inc(m.up("tokcopied"), 1)
        act.wait_ge(m.sem("sums"), m.count("sums", 1))
        act.activation(root, ss, ACT.Sqrt).then_inc(m.up("roots"), 1)
        for n in range(N):
            act.wait_ge(m.sem("back"), m.count("back", n + 1))
            dst, i = jobs[n][0], jobs[n][2]
            act.activation(dst[:, :, i * P:(i + 1) * P], m.psum[:, 4 + n % 4, :].rearrange(
                "p (a b) -> p a b", b=P), ACT.Copy).then_inc(m.up("backcopied"), 1)

    def pool(pool):
        for n in range(N):
            pool.wait_ge(m.sem("tokcopied"), m.count("tokcopied", n + 1))
            if n >= 2:
                pool.wait_ge(m.sem("reduced"), m.count("reduced", n - 1))
            src = jobs[n][1][:, jobs[n][2]]
            pool.tensor_tensor(sq[:, n % 2], src, src, ALU.mult).then_inc(m.up("squared"), 1)

    def dve(dve):
        c = m.vchain
        for n in range(N):
            dve.wait_ge(m.sem("squared"), m.count("squared", n + 1))
            dve.tensor_reduce(ss[:, GH * n:GH * n + GH], sq[:, n % 2], AX.X, ALU.add).then_inc(m.up("reduced"), 1)
        dve.wait_ge(m.sem("reduced"), m.count("reduced", N))
        dve.tensor_scalar(ss, ss, EPS, None, ALU.add).then_inc(m.up("sums"), 1)
        dve.wait_ge(m.sem("roots"), m.count("roots", 1))
        dve.reciprocal(root, root).then_inc(c.up(), 1)
        dve.wait_ge(c.sem, c.now())
        rstd_newton(m, dve, ss, root, tmp, m.sig("rstd"))
        dve.wait_ge(m.sem("rstd"), m.count("rstd", 1))
        dve.tensor_scalar(root[:, GH * NA:GH * N], root[:, GH * NA:GH * N], DK ** -0.5, None, ALU.mult).then_inc(c.up(), 1)
        dve.wait_ge(c.sem, c.now())
        for n in range(N):
            x = jobs[n][1][:, jobs[n][2]]
            r = root[:, GH * n:GH * n + GH].rearrange("p (a b) -> p a b", b=1).broadcast_to([P, GH, P])
            dve.tensor_tensor(x, x, r, ALU.mult).then_inc(m.up("toknormed"), 1)

    run_stage(m, dict(sp=lambda e: None, pe=pe, act=act, dve=dve, pool=pool))


def gdn_scan_stage(m, group):
    kt, qt, o = m.at(KT_AT, GH, TA), m.at(QT_AT, GH, T), m.at(O_AT, 8, T)
    ktok, vtok = m.at(KTOK_AT, NA, GH, P), m.at(VTOK_AT, NA, GH, P)
    places = [WORK_AT + 512 * i for i in range(12)] + [VT_AT + 512 * i for i in range(6)] + [17408, 17920]
    B = [{name: m.at(places[10 * d + i], GH, P) for i, name in enumerate(
        ("E", "A", "Z", "X", "Y", "QK", "QE", "R", "VN", "KD"))} for d in range(2)]
    S = [m.at(S_AT + 512 * d, GH, P) for d in range(2)]
    tiles = [[4, 5, 0, 1, 2, 3], [5, 4, 3, 2, 1, 0]]
    LEVELS = 7
    bank = lambda d, i: m.psum[:, 4 * d + i, :].rearrange("p (h c) -> p h c", c=P)
    sig = lambda name, d: m.sig(f"{name}{d}")
    wide = lambda x: x.rearrange("p (a b) -> p a b", a=1).broadcast_to([P, GH, P])
    nt = lambda n: slice(n * P, (n + 1) * P)

    def gcol(which, n, d, h):
        c = n * 16 + d * 8 + GH * group + h
        return m.gcols[:, which, c:c + 1]

    def gcols(which, n, d):
        c = n * 16 + d * 8 + GH * group
        return m.gcols[:, which, c:c + GH].rearrange("p (a b) -> p a b", b=1).broadcast_to([P, GH, P])

    def pe(pe):
        def each(d, i, f, name):
            for h in range(GH):
                last = f(bank(d, i)[:, h, :], h)
            last.then_inc(sig(name, d).up(), 1)

        def row_sums(t, d):
            n = tiles[d][t]
            each(d, 0, lambda out, h: pe.matmul(out, gcol(GG, n, d, h).broadcast_to([P, P]), m.cum[:, d, :],
                                                start=True, stop=True), "rsum")

        def gram(t, d):
            n = tiles[d][t]
            if t:
                pe.wait_ge(sig("znew", d).sem, sig("znew", d).count(LEVELS * t))
            each(d, 1, lambda out, h: pe.matmul(out, kt[:, h, nt(n)], kt[:, h, nt(n)], start=True, stop=True), "gram")

        def query_gram(t, d):
            n = tiles[d][t]
            if t == 2:
                pe.wait_ge(sig("vnew", d).sem, sig("vnew", d).count(t))
            else:
                pe.wait_ge(sig("oadd", d).sem, sig("oadd", d).count(t - 2))
            each(d, 2, lambda out, h: pe.matmul(out, kt[:, h, nt(n)], qt[:, h, nt(n)], start=True, stop=True), "qgram")

        def level(t, s):
            for d in range(2):
                b = B[d]
                if s:
                    pe.wait_ge(sig("xcopy", d).sem, sig("xcopy", d).count(6 * t + s))
                    if s == 1 and t >= 2:
                        pe.wait_ge(sig("qexp", d).sem, sig("qexp", d).count(t - 1))
                    each(d, 0, lambda out, h: pe.matmul(out, b["A"][:, h, :], b["X"][:, h, :],
                                                        start=True, stop=True), "ymul")
            for d in range(2):
                b = B[d]
                if s:
                    pe.wait_ge(sig("ymask", d).sem, sig("ymask", d).count(6 * t + s))
                    each(d, 1, lambda out, h: pe.matmul(out, b["Y"][:, h, :], b["Z"][:, h, :],
                                                        start=True, stop=True), "zmul")
            if s < LEVELS - 1:
                for d in range(2):
                    pe.wait_ge(sig("znew", d).sem, sig("znew", d).count(LEVELS * t + s + 1))
                    if t and s == 0:
                        pe.wait_ge(sig("snew", d).sem, sig("snew", d).count(t))
                    each(d, 3, lambda out, h: pe.transpose(out, B[d]["Z"][:, h, :], m.ident[:, :]), "turn")

        def state_product(t, d):
            n = tiles[d][t]
            if t >= 2:
                pe.wait_ge(sig("qk", d).sem, sig("qk", d).count(t - 1))
            each(d, 2, lambda out, h: pe.matmul(out, kt[:, h, nt(n)], S[d][:, h, :], start=True, stop=True), "ks")

        def updates(t, d):
            pe.wait_ge(sig("znew", d).sem, sig("znew", d).count(LEVELS * (t + 1)))
            pe.wait_ge(sig("resid", d).sem, sig("resid", d).count(t + 1))
            each(d, 2, lambda out, h: pe.matmul(out, B[d]["Z"][:, h, :], B[d]["R"][:, h, :],
                                                start=True, stop=True), "tmul")

        def state_and_output(t, d):
            b = B[d]
            pe.wait_ge(sig("vnew", d).sem, sig("vnew", d).count(t + 1))
            if t < NA - 1:
                pe.wait_ge(sig("kdec", d).sem, sig("kdec", d).count(t + 1))
                each(d, 3, lambda out, h: pe.matmul(out, b["KD"][:, h, :], b["VN"][:, h, :],
                                                    start=True, stop=True), "smul")
            if t >= 2:
                pe.wait_ge(sig("qe", d).sem, sig("qe", d).count(t - 1))

                def output(out, h):
                    pe.matmul(out, S[d][:, h, :], b["QE"][:, h, :], start=True, stop=False)
                    return pe.matmul(out, b["VN"][:, h, :], b["QK"][:, h, :], start=False, stop=True)
                each(d, 2, output, "omul")

        for d in range(2):
            row_sums(0, d)
            gram(0, d)
        for t in range(NA):
            for s in range(LEVELS):
                level(t, s)
                if t and s == LEVELS - 2:
                    for d in range(2):
                        state_product(t, d)
            if t < NA - 1:
                row_sums(t + 1, 0)
                row_sums(t + 1, 1)
            updates(t, 0)
            updates(t, 1)
            if t < NA - 1:
                gram(t + 1, 0)
                gram(t + 1, 1)
            state_and_output(t, 0)
            state_and_output(t, 1)
            if 1 <= t < NA - 1:
                query_gram(t + 1, 0)
                query_gram(t + 1, 1)

    def act(act):
        for t in range(NA):
            for d in range(2):
                b = B[d]
                act.wait_ge(sig("esum", d).sem, sig("esum", d).count(t + 1))
                act.activation(b["E"], b["E"], ACT.Exp).then_inc(sig("eexp", d).up(), 1)
            for d in range(2):
                if t >= 2:
                    if t >= 3:
                        act.wait_ge(sig("omul", d).sem, sig("omul", d).count(t - 2))
                    act.activation(B[d]["QE"], bank(d, 0), ACT.Exp).then_inc(sig("qexp", d).up(), 1)
            for s in range(LEVELS - 1):
                for d in range(2):
                    act.wait_ge(sig("turn", d).sem, sig("turn", d).count(6 * t + s + 1))
                    act.activation(B[d]["X"], bank(d, 3), ACT.Copy).then_inc(sig("xcopy", d).up(), 1)

    def pool(pool):
        for t in range(NA):
            for d in range(2):
                n, b = tiles[d][t], B[d]
                if t < NA - 1:
                    if t:
                        pool.wait_ge(sig("smul", d).sem, sig("smul", d).count(t))
                    pool.tensor_tensor(b["KD"], ktok[:, n], gcols(REST, n, d), ALU.mult).then_inc(sig("kdec", d).up(), 1)
                if t >= 2:
                    pool.wait_ge(sig("qexp", d).sem, sig("qexp", d).count(t - 1))
                    pool.tensor_tensor(b["QE"], b["QE"], qt[:, :, nt(n)], ALU.mult).then_inc(sig("qe", d).up(), 1)

    def dve(dve):
        c = m.vchain

        def sums(t, d):
            n, b = tiles[d][t], B[d]
            dve.wait_ge(sig("rsum", d).sem, sig("rsum", d).count(t + 1))
            for h in range(GH):
                ins = dve.scalar_tensor_tensor(b["E"][:, h, :], bank(d, 0)[:, h, :], gcol(GC, n, d, h),
                                               m.bar[:, d, :], ALU.subtract, ALU.add)
            ins.then_inc(sig("esum", d).up(), 1)

        def triangle(t, d):
            n, b = tiles[d][t], B[d]
            dve.wait_ge(sig("eexp", d).sem, sig("eexp", d).count(t + 1))
            dve.wait_ge(sig("gram", d).sem, sig("gram", d).count(t + 1))
            for h in range(GH):
                ins = dve.scalar_tensor_tensor(b["A"][:, h, :], bank(d, 1)[:, h, :], gcol(BETA, n, d, h),
                                               b["E"][:, h, :], ALU.mult, ALU.mult)
            ins.then_inc(c.up(), 1)
            dve.wait_ge(c.sem, c.now())
            dve.tensor_tensor(b["Z"], b["A"], wide(m.lev[:, 1 - d, 0, :]), ALU.mult).then_inc(c.up(), 1)
            dve.wait_ge(c.sem, c.now())
            dve.tensor_tensor(b["Z"], wide(m.ident[:, :]), b["Z"], ALU.subtract).then_inc(sig("znew", d).up(), 1)

        def query_decay(t, d):
            b = B[d]
            dve.wait_ge(sig("qgram", d).sem, sig("qgram", d).count(t - 1))
            dve.tensor_tensor(b["QK"], b["E"], bank(d, 2), ALU.mult).then_inc(sig("qk", d).up(), 1)

        def level(t, s):
            for d in range(2):
                dve.wait_ge(sig("ymul", d).sem, sig("ymul", d).count(6 * t + s))
                dve.tensor_tensor(B[d]["Y"], bank(d, 0), wide(m.lev[:, d, s, :]), ALU.mult).then_inc(
                    sig("ymask", d).up(), 1)
            for d in range(2):
                dve.wait_ge(sig("zmul", d).sem, sig("zmul", d).count(6 * t + s))
                dve.tensor_tensor(B[d]["Z"], B[d]["Z"], bank(d, 1), ALU.subtract).then_inc(sig("znew", d).up(), 1)

        def residual(t, d):
            n, b = tiles[d][t], B[d]
            if t:
                dve.wait_ge(sig("ks", d).sem, sig("ks", d).count(t))
                for h in range(GH):
                    ins = dve.scalar_tensor_tensor(b["R"][:, h, :], bank(d, 2)[:, h, :], gcol(NEG_EG, n, d, h),
                                                   vtok[:, n, h, :], ALU.mult, ALU.add)
            else:
                ins = dve.tensor_copy(b["R"], vtok[:, n])
            ins.then_inc(sig("resid", d).up(), 1)

        def updates(t, d):
            n, b = tiles[d][t], B[d]
            dve.wait_ge(sig("tmul", d).sem, sig("tmul", d).count(t + 1))
            dve.tensor_tensor(b["VN"], bank(d, 2), gcols(BETA, n, d), ALU.mult).then_inc(sig("vnew", d).up(), 1)

        def output(t, d):
            n = tiles[d][t]
            dve.wait_ge(sig("omul", d).sem, sig("omul", d).count(t - 1))
            out = o[:, GH * group:GH * (group + 1), nt(n)]
            if (n < 2) == (d == 0):
                ins = dve.tensor_copy(out, bank(d, 2))
            else:
                ins = dve.tensor_tensor(out, out, bank(d, 2), ALU.add)
            ins.then_inc(sig("oadd", d).up(), 1)

        def state(t, d):
            n = tiles[d][t]
            dve.wait_ge(sig("smul", d).sem, sig("smul", d).count(t + 1))
            for h in range(GH):
                if t:
                    ins = dve.scalar_tensor_tensor(S[d][:, h, :], S[d][:, h, :], gcol(TOTAL, n, d, h),
                                                   bank(d, 3)[:, h, :], ALU.mult, ALU.add)
                else:
                    ins = dve.tensor_copy(S[d][:, h, :], bank(d, 3)[:, h, :])
            ins.then_inc(sig("snew", d).up(), 1)

        sums(0, 0), sums(0, 1)
        triangle(0, 0), triangle(0, 1)
        for t in range(NA):
            for s in range(1, LEVELS):
                level(t, s)
                if s == LEVELS - 2:
                    residual(t, 0), residual(t, 1)
            if t < NA - 1:
                sums(t + 1, 0), sums(t + 1, 1)
            updates(t, 0), updates(t, 1)
            if t < NA - 1:
                triangle(t + 1, 0), triangle(t + 1, 1)
            for d in range(2):
                if t >= 2:
                    output(t, d)
                if t < NA - 1:
                    state(t, d)
            if 1 <= t < NA - 1:
                query_decay(t + 1, 0), query_decay(t + 1, 1)

    run_stage(m, dict(sp=lambda e: None, pe=pe, act=act, dve=dve, pool=pool))


QK_N, ROPE = 128, 64
K_ALL, V_ALL, CQ_AT, CKV_AT, QR_AT, QN_AT = 0, 6144, 12288, 15360, 18432, 20480
KR_AT, COS_AT, SIN_AT, ROT_AT, SEL_AT, KROW_AT, QROW_AT = \
    28672, 29440, 29952, 30464, 30592, 31744, 31232
KRS_AT, PR_AT, PT_AT = 12288, 15360, 16896


def mla_in_stage(m, seg, v, loads):
    xh, xl = m.at(0, KD, TA), m.at(KD * TA, KD, TA)
    cqh, cql = m.at(CQ_AT, 3, T), m.at(CQ_AT + 3 * T, 3, T)
    ckh, ckl = m.at(CKV_AT, 2, TA), m.at(CKV_AT + 2 * TA, 2, TA)
    kr, krsq = m.at(KR_AT, TA), m.at(KROW_AT, TA)
    accs = [m.at(XN_AT, T), m.at(XN_AT + T, TA)]
    sq = m.at(XN_AT + T + TA, 2, TA)
    rot = m.at(XN_AT + T + 3 * TA, T)
    outs = [cql[:, 0, :], cql[:, 1, :], cql[:, 2, :], ckl[:, 0, :], ckl[:, 1, :], kr]
    wide = [False] * 3 + [True] * 3
    mean, root, tmp, half = [m.small[:, 24 + 10 * i:34 + 10 * i] for i in range(4)]
    us = unrolled(seg)

    def sp(sp):
        for view, src in loads:
            sp.dma_start(view, src).then_inc(m.up("loaded", 16), 16)
        for unit in us:
            m.sp_unit(sp, unit)
        sp.wait_ge(m.sem("loaded"), m.count("loaded", 16 * len(loads)))

    def pe(pe):
        for unit in us:
            if unit.u == 2:
                pe.wait_ge(m.sem("freed"), m.count("freed", 2))
            pe_wide_unit(m, pe, unit, lambda k: (xh[:, k, :], xl[:, k, :]), wide[2 * unit.u:2 * unit.u + 2],
                         unit.u == 0)
        pe.wait_ge(m.sem("summed"), m.count("summed", 3))
        for i in range(4):
            pe.matmul(m.psum[:, 7, i:i + 1], accs[0][:, i * P:(i + 1) * P], m.ones[:, 0:1], start=True, stop=True)
        for i in range(NA):
            last = pe.matmul(m.psum[:, 7, 4 + i:5 + i], accs[1][:, i * P:(i + 1) * P], m.ones[:, 0:1],
                             start=True, stop=True)
        last.then_inc(m.up("ssq"), 1)
        pe.wait_ge(m.sem("loaded"), m.count("loaded", 16 * len(loads)))
        pe.wait_ge(m.sem("krgain"), m.count("krgain", 1))
        pe.matmul(m.psum[:, 0, :], m.at(ROT_AT, P), kr[:, 0:T], start=True, stop=True).then_inc(m.up("rotated"), 1)
        pe.wait_ge(m.sem("rstd"), m.count("rstd", 1))
        rstd_pe_spread(m, pe, root, 4, lambda i: m.psum[:, 6, i * P:(i + 1) * P])
        rstd_pe_spread(m, pe, root[:, 4:10], 6, lambda i: m.psum[:, 4 + i // 4, (i % 4) * P:(i % 4 + 1) * P])

    def act(act):
        round_xn(m, act, xh)
        for t in range(6):
            act.wait_ge(m.sem("freed"), m.count("freed", t + 1))
            n = TA if wide[t] else T
            dst = {0: accs[0], 3: accs[1], 5: krsq}.get(t, sq[:, t % 2, 0:n])
            act.activation(dst, outs[t], ACT.Square).then_inc(m.up("square"), 1)

    def dve(dve):
        c = m.vchain
        dve.memset(half, -0.5).then_inc(c.up(), 1)
        dve.wait_ge(c.sem, c.now())
        split_xn(m, dve, xh, xl)
        for unit in us:
            dve.wait_ge(m.sem("done"), m.count("done", 2 * unit.u + 2))
            m.dve_unit(dve, unit)
            for t in range(2):
                n = 2 * unit.u + t
                ins = dve.tensor_copy(outs[n][:, 0:T], m.psum[:, 2 * unit.slot + t, :])
                if wide[n]:
                    ins.then_inc(c.up(), 1)
                    ins = dve.tensor_copy(outs[n][:, CTX], m.psum[:, 4 + unit.slot, t * TC:(t + 1) * TC])
                ins.then_inc(m.up("freed"), 1)
            for t in range(2):
                n = 2 * unit.u + t
                if n in (1, 2, 4):
                    dve.wait_ge(m.sem("square"), m.count("square", n + 1))
                    if n == 2:
                        dve.wait_ge(m.sem("summed"), m.count("summed", 1))
                    a = accs[n // 3]
                    dve.tensor_tensor(a, a, sq[:, n % 2, 0:TA if wide[n] else T], ALU.add).then_inc(m.up("summed"), 1)
        dve.wait_ge(m.sem("square"), m.count("square", 6))
        dve.tensor_scalar(kr, kr, v["k_norm_rope"], None, ALU.mult).then_inc(m.up("krgain"), 1)
        dve.wait_ge(m.sem("ssq"), m.count("ssq", 1))
        dve.tensor_scalar(mean[:, 0:4], m.psum[:, 7, 0:4], 1.0 / 384, EPS, ALU.mult, ALU.add).then_inc(c.up(), 1)
        dve.wait_ge(c.sem, c.now())
        dve.tensor_scalar(mean[:, 4:10], m.psum[:, 7, 4:10], 1.0 / 256, EPS, ALU.mult, ALU.add).then_inc(m.up("mean"), 1)
        dve.wait_ge(m.sem("rotated"), m.count("rotated", 1))
        dve.wait_ge(m.sem("loaded"), m.count("loaded", 16 * len(loads)))
        dve.tensor_tensor(rot, m.at(SIN_AT, T), m.psum[:, 0, :], ALU.mult).then_inc(c.up(), 1)
        dve.wait_ge(c.sem, c.now())
        dve.tensor_tensor(kr[:, 0:T], kr[:, 0:T], m.at(COS_AT, T), ALU.mult).then_inc(c.up(), 1)
        dve.wait_ge(c.sem, c.now())
        dve.tensor_tensor(kr[:, 0:T], kr[:, 0:T], rot, ALU.add).then_inc(c.up(), 1)
        dve.wait_ge(c.sem, c.now())
        dve.wait_ge(m.sem("root"), m.count("root", 1))
        rstd_newton(m, dve, mean, root, tmp, m.sig("rstd"))
        dve.wait_ge(m.sem("spread"), m.count("spread", 2))
        for k in range(3):
            dve.scalar_tensor_tensor(cql[:, k, :], cql[:, k, :], col(v["q_a_norm"], k),
                                                 m.psum[:, 6, :], ALU.mult, ALU.mult).then_inc(c.up(), 1)
            dve.wait_ge(c.sem, c.now())
            split_in_place(m, dve, cqh[:, k, :], cql[:, k, :], m.sig("lready"))
        for k in range(2):
            for cols, bank in ((slice(0, T), 4), (CTX, 5)):
                o = ckl[:, k, cols]
                dve.scalar_tensor_tensor(o, o, col(v["kv_a_norm"], k), m.psum[:, bank, 0:o.shape[1]],
                                                     ALU.mult, ALU.mult).then_inc(c.up(), 1)
                dve.wait_ge(c.sem, c.now())
            split_in_place(m, dve, ckh[:, k, :], ckl[:, k, :], m.sig("lready"))

    def pool(pool):
        for unit in us:
            m.pool_unit(pool, unit)
        rstd_pool(m, pool, mean, half, root, 1)

    run_stage(m, dict(sp=sp, pe=pe, act=act, dve=dve, pool=pool))


def mla_heads_stage(m, segs, v):
    qn, qr = m.at(QN_AT, 8, T), m.at(QR_AT, 4, T)
    ka, va = m.at(K_ALL, 8, TA), m.at(V_ALL, NA, 8 * P)
    cqh, cql = m.at(CQ_AT, 3, T), m.at(CQ_AT + 3 * T, 3, T)
    ckh, ckl = m.at(CKV_AT, 2, TA), m.at(CKV_AT + 2 * TA, 2, TA)
    sq, rot = m.at(V_ALL, 2, TA), m.at(V_ALL + 2 * TA, T)
    krsq, krow, qrow = m.at(KROW_AT, TA), m.at(KROW_AT, TA)[0:8, :], m.at(QROW_AT, T)[0:8, :]
    sel = m.at(SEL_AT, 13, 8)
    us = [u for s in segs for u in unrolled(s)]
    bank = lambda unit, t: m.psum[:, 2 * unit.slot + t, :]

    def kind(n):
        return "q" if n < 4 else "r" if n < 6 else "k" if n < 10 else "v"

    def pe(pe):
        def sums(i):
            pe.wait_ge(m.sem("square"), m.count("square", i + 1))
            if i < 12:
                last = pe.matmul(m.psum[0:8, 7, :], sel[:, i, :], sq[:, i % 2, 0:T], start=i == 0, stop=i == 11)
                last.then_inc(m.up("qsum" if i == 11 else "sqread"), 1)
            else:
                if i == 12:
                    pe.wait_ge(m.sem("qrow"), m.count("qrow", 1))
                    pe.wait_ge(m.sem("qturned"), m.count("qturned", 4))
                    pe.matmul(m.psum[0:8, 6, :], sel[:, 12, :], krsq[:, 0:T], start=True, stop=False)
                    pe.matmul(m.psum[0:8, 7, 0:TC], sel[:, 12, :], krsq[:, CTX], start=True, stop=False)
                pe.matmul(m.psum[0:8, 6, :], sel[:, i - 12, :], sq[:, i % 2, 0:T], start=False, stop=i == 19)
                last = pe.matmul(m.psum[0:8, 7, 0:TC], sel[:, i - 12, :], sq[:, i % 2, CTX], start=False, stop=i == 19)
                last.then_inc(m.up("sqread"), 1)

        def turn(j):
            pe.wait_ge(m.sem("freed"), m.count("freed", 9 + j))
            if j:
                pe.wait_ge(m.sem("qturned"), m.count("qturned", j))
            pe.matmul(m.psum[:, 6, :], m.at(ROT_AT, P), qr[:, j, :], start=True, stop=True).then_inc(m.up("rotated"), 1)

        qhalves = lambda k: (cqh[:, k, :], cql[:, k, :])
        khalves = lambda k: (ckh[:, k, :], ckl[:, k, :])
        for n, unit in enumerate(us):
            if n >= 2:
                pe.wait_ge(m.sem("freed"), m.count("freed", 2 * (n - 1)))
            if kind(n) in "qr":
                pe_wide_unit(m, pe, unit, qhalves, [False] * 2)
            elif kind(n) == "k":
                pe_wide_unit(m, pe, unit, khalves, [True] * 2)
            else:
                pe.wait_ge(m.lo_done, unit.g + 1)
                for i in range(NA):
                    out = m.psum[:, 2 * unit.slot + i // 2 if i < 4 else 4 + unit.slot, (i % 2) * 256:(i % 2 + 1) * 256]
                    for k in range(2):
                        wh, wl = [m.rounded(m.ring[:, part, unit.slot, k * 256:(k + 1) * 256]) for part in (1, 2)]
                        a, b = [m.rounded(x[:, i * P:(i + 1) * P]) for x in khalves(k)]
                        pe.matmul(out, a, wh, start=k == 0, stop=False)
                        pe.matmul(out, b, wh, start=False, stop=False)
                        last = pe.matmul(out, a, wl, start=False, stop=k == 1)
                    if i in (3, 5):
                        last.then_inc(m.up("done"), 1)
            if 1 <= n <= 10:
                for t in range(2):
                    i = 2 * (n - 1) + t
                    sums(i)
                    if 8 <= i < 12:
                        turn(i - 8)

    def act(act):
        for n, unit in enumerate(us[:10]):
            for t in range(2):
                i = 2 * n + t
                act.wait_ge(m.sem("done"), m.count("done", 2 * n + (2 if kind(n) == "k" else t + 1)))
                if i >= 2:
                    if i - 1 >= 12:
                        act.wait_ge(m.sem("qsum"), m.count("qsum", 1))
                    act.wait_ge(m.sem("sqread"), m.count("sqread", i - 1 if i <= 12 else i - 2))
                if kind(n) != "k":
                    act.activation(sq[:, i % 2, 0:T], bank(unit, t), ACT.Square).then_inc(m.up("square"), 1)
                else:
                    act.activation(sq[:, i % 2, 0:T], bank(unit, t), ACT.Square).then_inc(m.achain.up(), 1)
                    act.activation(sq[:, i % 2, CTX], m.psum[:, 4 + unit.slot, t * TC:(t + 1) * TC],
                                                       ACT.Square).then_inc(m.up("square"), 1)
        act.wait_ge(m.sem("sqread"), m.count("sqread", 19))
        act.activation(krow[:, 0:T], m.psum[0:8, 6, :], ACT.Copy).then_inc(m.achain.up(), 1)
        act.activation(krow[:, CTX], m.psum[0:8, 7, 0:TC], ACT.Copy).then_inc(m.achain.up(), 1)

    def dve(dve):
        c = m.vchain
        for n, unit in enumerate(us):
            dve.wait_ge(m.sem("done"), m.count("done", 2 * n + 2))
            m.dve_unit(dve, unit)
            k_ = kind(n)
            if k_ == "v":
                if n == 10:
                    dve.wait_ge(m.sem("sqread"), m.count("sqread", 19))
                o = (n - 10) * 256
                for t in range(2):
                    dve.tensor_copy(
                        va[:, 2 * t:2 * t + 2, o:o + 256], bank(unit, t).rearrange("p (a b) -> p a b", b=256)).then_inc(m.up("freed"), 1)
                    if t == 0:
                        dve.tensor_copy(va[:, 4:6, o:o + 256], m.psum[:, 4 + unit.slot, :].rearrange(
                            "p (a b) -> p a b", b=256)).then_inc(c.up(), 1)
                continue
            dve.wait_ge(m.sem("square"), m.count("square", 2 * n + 2))
            for t in range(2):
                i = 2 * n + t
                if k_ == "k":
                    dve.tensor_scalar(ka[:, i - 12, CTX], m.psum[:, 4 + unit.slot, t * TC:(t + 1) * TC],
                                             v["k_norm_nope"], None, ALU.mult).then_inc(c.up(), 1)
                    dve.tensor_scalar(ka[:, i - 12, 0:T], bank(unit, t), v["k_norm_nope"], None,
                                                         ALU.mult).then_inc(m.up("freed"), 1)
                elif k_ == "q":
                    dve.tensor_scalar(qn[:, i, :], bank(unit, t), v["q_norm_nope"], None, ALU.mult).then_inc(m.up("freed"), 1)
                else:
                    dve.tensor_scalar(qr[:, i - 8, :], bank(unit, t), v["q_norm_rope"], None,
                                                         ALU.mult).then_inc(m.up("freed"), 1)
            if k_ == "r":
                dve.wait_ge(m.sem("freed"), m.count("freed", 2 * n + 2))
            if n in (5, 6):
                for j in (2 * (n - 5), 2 * (n - 5) + 1):
                    dve.wait_ge(m.sem("rotated"), m.count("rotated", j + 1))
                    dve.tensor_tensor(rot, m.at(SIN_AT, T), m.psum[:, 6, :], ALU.mult).then_inc(c.up(), 1)
                    dve.wait_ge(c.sem, c.now())
                    dve.tensor_tensor(qr[:, j, :], qr[:, j, :], m.at(COS_AT, T), ALU.mult).then_inc(c.up(), 1)
                    dve.wait_ge(c.sem, c.now())
                    dve.tensor_tensor(qr[:, j, :], qr[:, j, :], rot, ALU.add).then_inc(m.up("qturned"), 1)
                    dve.wait_ge(m.sem("qturned"), m.count("qturned", j + 1))
            if n == 6:
                dve.wait_ge(m.sem("qsum"), m.count("qsum", 1))
                dve.tensor_copy(qrow, m.psum[0:8, 7, :]).then_inc(m.up("qrow"), 1)

    run_stage(m, dict(sp=lambda sp: [m.sp_unit(sp, unit) for unit in us], pe=pe, act=act, dve=dve,
                      pool=lambda pool: [m.pool_unit(pool, unit) for unit in us]))


def head_roots(m, pe=None, act=None, dve=None, rows=None, tiles=0, scale=1.0):
    w = 8 * tiles
    mean, root, tmp = [m.small[:, 24 + 80 * i:24 + 80 * i + w] for i in range(3)]
    if pe is not None:
        for i in range(tiles):
            src = rows(i)
            last = pe.transpose(m.psum[:, 0, 8 * i:8 * i + 8], src, m.ident[0:8, 0:8])
        last.then_inc(m.up("rcols"), 1)
        pe.wait_ge(m.sem("rstd"), m.count("rstd", 1))
    if act is not None:
        act.wait_ge(m.sem("mean"), m.count("mean", 1))
        act.activation(root, mean, ACT.Sqrt).then_inc(m.up("root"), 1)
    if dve is not None:
        dve.wait_ge(m.sem("rcols"), m.count("rcols", 1))
        dve.tensor_scalar(mean, m.psum[:, 0, 0:w], scale, EPS, ALU.mult, ALU.add).then_inc(m.up("mean"), 1)
        dve.wait_ge(m.sem("root"), m.count("root", 1))
        dve.reciprocal(root, root).then_inc(m.vchain.up(), 1)
        dve.wait_ge(m.vchain.sem, m.vchain.now())
        rstd_newton(m, dve, mean, root, tmp, m.sig("rstd"))
    return root


def mla_norm_stage(m):
    ka, krs, kr = m.at(K_ALL, 8, TA), m.at(KRS_AT, 4, TA), m.at(KR_AT, TA)
    krow, qrow = m.at(KROW_AT, TA)[0:8, :], m.at(QROW_AT, T)[0:8, :]
    rows = lambda i: qrow[:, i * P:(i + 1) * P] if i < NT else krow[:, (i - NT) * P:(i - NT + 1) * P]
    args = dict(rows=rows, tiles=NT + NA, scale=1.0 / (QK_N + ROPE))
    root = m.small[:, 24 + 80:24 + 160]

    def pe(pe):
        head_roots(m, pe=pe, **args)
        flat = m.psum[:, :, :].rearrange("p a b -> p (a b)")
        for i in range(8):
            if i >= 2:
                pe.wait_ge(m.sem("scaled"), m.count("scaled", 2 * (i - 1)))
            for j in range(NA):
                o = (4 + 2 * (i % 2)) * 512 + j * P
                last = pe.matmul(flat[:, o:o + P], col(root, 8 * (NT + j) + i).broadcast_to([P, P]), m.ident[:, :],
                                 start=True, stop=True)
            last.then_inc(m.up("spread"), 1)

    def dve(dve):
        head_roots(m, dve=dve, **args)
        dve.wait_ge(m.sem("rstd"), m.count("rstd", 1))
        dve.tensor_scalar(root[:, 0:32], root[:, 0:32], float(QK_N + ROPE) ** -0.5, None, ALU.mult).then_inc(m.vchain.up(), 1)
        dve.wait_ge(m.vchain.sem, m.vchain.now())
        flat = m.psum[:, :, :].rearrange("p a b -> p (a b)")
        for i in range(8):
            dve.wait_ge(m.sem("spread"), m.count("spread", i + 1))
            o = (4 + 2 * (i % 2)) * 512
            rs = slice(ROPE * (i % 2), ROPE * (i % 2) + ROPE)
            dve.tensor_tensor(ka[:, i, :], ka[:, i, :], flat[:, o:o + TA], ALU.mult).then_inc(m.up("scaled"), 1)
            dve.tensor_tensor(krs[rs, i // 2, :], kr[rs, :], flat[rs, o:o + TA], ALU.mult).then_inc(m.up("scaled"), 1)

    run_stage(m, dict(sp=lambda e: None, pe=pe, act=lambda act: head_roots(m, act=act, **args), dve=dve,
                      pool=lambda e: None))


def mla_attend_stage(m):
    qn, qr = m.at(QN_AT, 8, T), m.at(QR_AT, 4, T)
    ka, va, krs = m.at(K_ALL, 8, TA), m.at(V_ALL, NA, 8 * P), m.at(KRS_AT, 4, TA)
    pr = [m.at(a, TA) for a in (PR_AT, PR_AT + TA, COS_AT)]
    pt = m.at(PT_AT, 2, NA, P)
    root = m.small[:, 24 + 80:24 + 160]
    negmax, total = m.small[:, 184:216], m.small[:, 216:248]
    flat = m.psum[:, :, :].rearrange("p a b -> p (a b)")
    steps = [(h, b) for h in range(8) for b in range(NT)]
    n = len(steps)
    scale = lambda i: col(root, 8 * steps[i][1] + steps[i][0])

    def pe(pe):
        def scores(i):
            h, b = steps[i]
            o, qs = ROPE * (h % 2), slice(b * P, (b + 1) * P)
            if i >= 2:
                pe.wait_ge(m.sem("exped"), m.count("exped", i - 1))
            for cols, bank in ((slice(0, T), 2 * (i % 2)), (CTX, 2 * (i % 2) + 1)):
                out = m.psum[:, bank, 0:cols.stop - cols.start]
                pe.matmul(out, qn[:, h, qs], ka[:, h, cols], start=True, stop=False)
                last = pe.matmul(out, qr[o:o + ROPE, h // 2, qs], krs[o:o + ROPE, h // 2, cols], start=False, stop=True)
            last.then_inc(m.up("scored"), 1)

        def turn(i):
            pe.wait_ge(m.sem("normed"), m.count("normed", i + 1))
            if i:
                pe.wait_ge(m.sem("ptcopied"), m.count("ptcopied", i))
            for j in range(NA):
                last = pe.transpose(flat[:, 2048 + j * P:2048 + (j + 1) * P], pr[i % 3][:, j * P:(j + 1) * P],
                                    m.ident[:, :])
            last.then_inc(m.up("turned"), 1)

        def values(i):
            h, b = steps[i]
            pe.wait_ge(m.sem("ptcopied"), m.count("ptcopied", i + 1))
            if b == 0 and h >= 2:
                pe.wait_ge(m.sem("attended"), m.count("attended", h - 1))
            for j in range(NA):
                last = pe.matmul(m.psum[:, 6 + h % 2, b * P:(b + 1) * P], va[:, j, h * P:(h + 1) * P],
                                 pt[:, i % 2, j, :], start=j == 0, stop=j == NA - 1)
            last.then_inc(m.up("valued"), 1)

        for i in range(n + 3):
            if i < n:
                scores(i)
            if 2 <= i <= n + 1:
                turn(i - 2)
            if i >= 3:
                values(i - 3)

    def act(act):
        for i in range(n + 2):
            if i < n:
                act.wait_ge(m.sem("biased"), m.count("biased", i + 1))
                if i >= 3:
                    act.wait_ge(m.sem("turned"), m.count("turned", i - 2))
                act.activation(pr[i % 3], flat[:, 1024 * (i % 2):1024 * (i % 2) + TA], ACT.Exp,
                                                  bias=col(negmax, i), scale=scale(i), accum_out=col(total, i)).then_inc(m.up("exped"), 1)
            if i >= 2:
                act.wait_ge(m.sem("turned"), m.count("turned", i - 1))
                if i >= 4:
                    act.wait_ge(m.sem("valued"), m.count("valued", i - 3))
                act.activation(pt[:, i % 2].rearrange("p a b -> p (a b)"),
                                                     flat[:, 2048:2048 + TA], ACT.Copy).then_inc(m.up("ptcopied"), 1)

    def dve(dve):
        c = m.vchain
        for i in range(n + 4):
            if i < n:
                dve.wait_ge(m.sem("scored"), m.count("scored", i + 1))
                dve.tensor_reduce(col(negmax, i), flat[:, 1024 * (i % 2):1024 * (i % 2) + TA], AX.X,
                                              ALU.max, negate=True).then_inc(c.up(), 1)
                dve.wait_ge(c.sem, c.now())
                dve.tensor_tensor(col(negmax, i), col(negmax, i), scale(i), ALU.mult).then_inc(m.up("biased"), 1)
            if 1 <= i <= n:
                dve.wait_ge(m.sem("exped"), m.count("exped", i))
                dve.reciprocal(col(total, i - 1), col(total, i - 1)).then_inc(c.up(), 1)
                dve.wait_ge(c.sem, c.now())
                dve.tensor_scalar(pr[(i - 1) % 3], pr[(i - 1) % 3], col(total, i - 1),
                                                      None, ALU.mult).then_inc(m.up("normed"), 1)
            if i >= 7 and (i - 7) % 4 == 0:
                h = (i - 7) // 4
                dve.wait_ge(m.sem("valued"), m.count("valued", 4 * (h + 1)))
                dve.tensor_copy(qn[:, h, :], m.psum[:, 6 + h % 2, :]).then_inc(m.up("attended"), 1)

    run_stage(m, dict(sp=lambda e: None, pe=pe, act=act, dve=dve, pool=lambda e: None))


OGH_AT, OGL_AT, OMH_AT, OML_AT, GATE_AT = 8192, 12288, 16384, 20480, 24576


def branch_stage(m, v):
    o, og = m.at(O_AT, 8, T), m.at(OGL_AT, 8, T)
    sq, row = m.at(0, 2, T), m.at(2048, T)[0:8, :]
    omh, oml = m.at(OMH_AT, 8, T), m.at(OML_AT, 8, T)
    sel = m.at(SEL_AT, 13, 8)
    rows = lambda i: row[:, i * P:(i + 1) * P]
    args = dict(rows=rows, tiles=NT, scale=1.0 / DK)
    root = m.small[:, 24 + 80:24 + 160]

    def pe(pe):
        for h in range(8):
            pe.wait_ge(m.sem("square"), m.count("square", h + 1))
            pe.matmul(m.psum[0:8, 7, :], sel[:, h, :], sq[:, h % 2, :], start=h == 0, stop=h == 7).then_inc(m.up("sqread"), 1)
        pe.wait_ge(m.sem("rowed"), m.count("rowed", 1))
        head_roots(m, pe=pe, **args)
        for h in range(8):
            if h >= 2:
                pe.wait_ge(m.sem("scaled"), m.count("scaled", h - 1))
            for j in range(NT):
                last = pe.matmul(m.psum[:, 3 + h % 2, j * P:(j + 1) * P], col(root, 8 * j + h).broadcast_to([P, P]),
                                 m.ident[:, :], start=True, stop=True)
            last.then_inc(m.up("spread"), 1)

    def act(act):
        for h in range(8):
            if h >= 2:
                act.wait_ge(m.sem("sqread"), m.count("sqread", h - 1))
            act.activation(sq[:, h % 2, :], o[:, h, :], ACT.Square).then_inc(m.up("square"), 1)
        act.wait_ge(m.sem("sqread"), m.count("sqread", 8))
        act.activation(row, m.psum[0:8, 7, :], ACT.Copy).then_inc(m.up("rowed"), 1)
        head_roots(m, act=act, **args)

    def dve(dve):
        for h in range(8):
            dve.tensor_copy(m.rounded(omh[:, h, :]), oml[:, h, :]).then_inc(m.up("omhi"), 1)
        head_roots(m, dve=dve, **args)
        for h in range(8):
            dve.wait_ge(m.sem("spread"), m.count("spread", h + 1))
            dve.scalar_tensor_tensor(og[:, h, :], o[:, h, :], v["out_norm"], m.psum[:, 3 + h % 2, :],
                                                         ALU.mult, ALU.mult).then_inc(m.up("scaled"), 1)

    def pool(pool):
        for h in range(8):
            pool.wait_ge(m.sem("omhi"), m.count("omhi", h + 1))
            pool.tensor_tensor(m.rounded(oml[:, h, :]), oml[:, h, :],
                                                 m.rounded(omh[:, h, :]).bitcast(F32), ALU.subtract).then_inc(m.up("omlo"), 1)

    run_stage(m, dict(sp=lambda e: None, pe=pe, act=act, dve=dve, pool=pool))


def merge_stage(m, segs, v):
    sz, sg, sb, so = segs
    xh, xl = m.at(0, KD, T), m.at(4096, KD, T)
    ogh, ogl, omh, oml = [m.at(a, 8, T) for a in (OGH_AT, OGL_AT, OMH_AT, OML_AT)]
    zt = m.at(GATE_AT + 8 * T, 2, T)
    gate = lambda i: m.at(GATE_AT + i * T, T) if isinstance(i, int) else pick(m.at(GATE_AT, 14, T), i)
    gain = m.small[:, 240:248]
    npe, nact, ndve, npool = norm_stage_parts(m, m.at(ACC_AT, T), gain, xh, xl, shift=m.mods[:, 0:KD, 0])
    bank = lambda unit, t: m.psum[:, 2 * unit.slot + t, :]
    res = Residual(m, so, 0, 40, 24, True, sq_at=8192, scale=m.mods[:, 2 * KD:3 * KD, 0])
    x = lambda k: (xh[:, k, :], xl[:, k, :])
    dz, dg, do = [Dense(m, s, x, s is sz, ("yready" if s is so else None, 8)) for s in (sz, sg, so)]

    def sp(sp):
        for s in segs:
            m.walk(sp, s, lambda unit: m.sp_unit(sp, unit))

    def pool(pool):
        npool(pool)
        for s in segs:
            m.walk(pool, s, lambda unit: m.pool_unit(pool, unit))

    def pe(pe):
        npe(pe)
        freed, gated = m.sig("freed"), m.sig("gated")
        for unit in unrolled(sz):
            if unit.u >= 2:
                pe.wait_ge(freed.sem, freed.count(2 * (unit.u - 1)))
            dz.pe_unit(pe, unit)

        def g_unit(unit):
            if isinstance(unit.u, int) and unit.u < 2:
                pe.wait_ge(freed.sem, freed.count(4 + 2 * (unit.u + 1)))
            else:
                pe.wait_ge(gated.sem, gated.count(2 * (unit.u - 1)))
            dg.pe_unit(pe, unit)

        def b_unit(unit):
            pe.wait_ge(m.lo_done, unit.g + 1)
            if isinstance(unit.u, int) and unit.u < 2:
                pe.wait_ge(gated.sem, gated.count(14 + 2 * unit.u))
            else:
                pe.wait_ge(freed.sem, freed.count(8 + 2 * (unit.u - 1)))
            if isinstance(unit.u, int) and unit.u == 0:
                pe.wait_ge(m.sem("ogready"), m.count("ogready", 8))
            for t, (hi, lo) in enumerate(((ogh, ogl), (omh, oml))):
                for k in range(KD):
                    o = k * sb.cols + t * P
                    w = [m.ring[:, part, unit.slot, o:o + P] for part in (1, 2)]
                    last = m.product(pe, bank(unit, t), w, (hi[:, k, :], lo[:, k, :]), k == 0, k == KD - 1)
                last.then_inc(m.up("done", unit.turns), 1)

        m.walk(pe, sg, g_unit)
        m.walk(pe, sb, b_unit)
        for unit in unrolled(so):
            pe.wait_ge(freed.sem, freed.count(22 + 2 * unit.u))
            if unit.u == 0:
                pe.wait_ge(m.sem("yready"), m.count("yready", 7))
            do.pe_unit(pe, unit)

    def act(act):
        nact(act)
        for unit in unrolled(sz):
            for t in range(2):
                h = 2 * unit.u + t
                act.wait_ge(m.sem("done"), m.count("done", h + 1))
                if h >= 2:
                    act.wait_ge(m.sem("ogready"), m.count("ogready", h - 1))
                act.activation(zt[:, t, :], bank(unit, t), ACT.Silu).then_inc(m.up("silu"), 1)
        act.wait_ge(m.sem("ogready"), m.count("ogready", 8))

        def g_unit(unit):
            for t in range(2):
                act.wait_ge(m.sem("done"), m.count("done", 8 + 2 * unit.u + (t + 1)))
                act.activation(gate(unit.u * 2 + t), bank(unit, t), ACT.Sigmoid).then_inc(m.up("gated", unit.turns), 1)

        m.walk(act, sg, g_unit)
        for unit in unrolled(so):
            res.act_unit(act, unit)

    def dve(dve):
        c = m.vchain
        dve.scalar_tensor_tensor(gain, m.mods[:, KD:2 * KD, 0], 1.0, v["norm_attn"], ALU.add, ALU.mult).then_inc(c.up(), 1)
        dve.wait_ge(c.sem, c.now())
        ndve(dve)
        for unit in unrolled(sz):
            dve.wait_ge(m.sem("done"), m.count("done", 2 * unit.u + 2))
            m.dve_unit(dve, unit)
            for t in range(2):
                h = 2 * unit.u + t
                dve.wait_ge(m.sem("silu"), m.count("silu", h + 1))
                dve.tensor_tensor(ogl[:, h, :], ogl[:, h, :], zt[:, t, :], ALU.mult).then_inc(m.up("freed"), 1)
                dve.wait_ge(m.sem("freed"), m.count("freed", h + 1))
                split_in_place(m, dve, ogh[:, h, :], ogl[:, h, :], m.sig("ogready"))

        def g_unit(unit):
            dve.wait_ge(m.sem("done"), m.count("done", 8 + 2 * unit.u + 2))
            m.dve_unit(dve, unit)

        def b_unit(unit):
            dve.wait_ge(m.sem("done"), m.count("done", 24 + 2 * unit.u + 2))
            m.dve_unit(dve, unit)
            for t in range(2):
                g = gate(unit.u * 2 + t)
                dve.tensor_tensor(g, g, bank(unit, t), ALU.mult).then_inc(m.up("freed", unit.turns), 1)
            dve.wait_ge(m.sem("freed"), m.count("freed", 8 + 2 * unit.u + 2))
            hi, lo = pick(xh, unit.u), pick(xl, unit.u)
            dve.tensor_tensor(lo, gate(unit.u * 2), gate(unit.u * 2 + 1), ALU.add).then_inc(c.up(), 1)
            dve.wait_ge(c.sem, c.now())
            split_in_place(m, dve, hi, lo, m.sig("yready"), unit.turns)

        m.walk(dve, sg, g_unit)
        dve.wait_ge(m.sem("gated"), m.count("gated", 16))
        m.walk(dve, sb, b_unit, c, 4)
        for unit in unrolled(so):
            res.dve_unit(dve, unit)
        res.dve_end(dve)

    run_stage(m, dict(sp=sp, pe=pe, act=act, dve=dve, pool=pool))


def mlp_stage(m, segs, v):
    NU = 8
    KT_ = 2 * NU
    xh, xl = m.at(0, KD, T), m.at(4096, KD, T)
    ah, al = m.at(8192, KT_, T), m.at(8192 + KT_ * T, KT_, T)
    gain = m.small[:, 240:248]
    npe, nact, ndve, npool = norm_stage_parts(m, m.at(ACC_AT, T), gain, xh, xl, shift=m.mods[:, 3 * KD:4 * KD, 0])
    per_half = 2 * NU + KD
    up = [Dense(m, segs[2 * i], lambda k: (xh[:, k, :], xl[:, k, :]), i == 0)
          for i in range(2)]
    down = [Dense(m, segs[2 * i + 1], lambda k: (ah[:, k, :], al[:, k, :]), last=("actready", (i + 1) * KT_))
            for i in range(2)]
    res = [Residual(m, segs[2 * i + 1], 0, i * per_half + 2 * NU, 0, False, scale=m.mods[:, 5 * KD:6 * KD, 0])
           for i in range(2)]
    bank = lambda unit, t: m.psum[:, 2 * unit.slot + t, :]

    def sp(sp):
        for s in segs:
            m.walk(sp, s, lambda unit: m.sp_unit(sp, unit))

    def pool(pool):
        npool(pool)
        for s in segs:
            m.walk(pool, s, lambda unit: m.pool_unit(pool, unit))

    def pe(pe):
        npe(pe)
        freed = m.sig("freed")
        for half in range(2):
            f0 = half * per_half

            def up_unit(unit):
                if not isinstance(unit.u, int) or unit.u >= 2:
                    pe.wait_ge(freed.sem, freed.count(f0 + (unit.u - 1) * 2))
                elif half:
                    pe.wait_ge(freed.sem, freed.count(f0 - 1 + unit.u))
                up[half].pe_unit(pe, unit)

            def down_unit(unit):
                if not isinstance(unit.u, int) or unit.u >= 2:
                    pe.wait_ge(freed.sem, freed.count(f0 + 2 * NU + unit.u - 1))
                else:
                    pe.wait_ge(freed.sem, freed.count(f0 + 2 * NU - 2 + 2 * unit.u))
                if isinstance(unit.u, int) and unit.u == 0:
                    pe.wait_ge(m.sem("actready"), m.count("actready", (half + 1) * KT_ - 1))
                down[half].pe_unit(pe, unit)

            m.walk(pe, segs[2 * half], up_unit)
            m.walk(pe, segs[2 * half + 1], down_unit)

    def act(act):
        nact(act)
        for half in range(2):
            f0 = half * per_half

            def up_unit(unit):
                for t in range(2):
                    act.wait_ge(m.sem("done"), m.count("done", f0 + 2 * unit.u + (t + 1)))
                    act.activation(pick(al, unit.u * 2 + t), bank(unit, t), ACT.Relu).then_inc(m.up("relu", unit.turns), 1)

            m.walk(act, segs[2 * half], up_unit)

    def dve(dve):
        c = m.vchain
        dve.scalar_tensor_tensor(gain, m.mods[:, 4 * KD:5 * KD, 0], 1.0, v["norm_mlp"], ALU.add, ALU.mult).then_inc(c.up(), 1)
        dve.wait_ge(c.sem, c.now())
        ndve(dve)
        for half in range(2):
            f0 = half * per_half

            def up_unit(unit):
                dve.wait_ge(m.sem("done"), m.count("done", f0 + 2 * unit.u + 2))
                m.dve_unit(dve, unit)
                for t in range(2):
                    hi, lo = pick(ah, unit.u * 2 + t), pick(al, unit.u * 2 + t)
                    dve.wait_ge(m.sem("relu"), m.count("relu", half * KT_ + 2 * unit.u + (t + 1)))
                    dve.scalar_tensor_tensor(lo, bank(unit, t), 0.0, lo, ALU.max, ALU.mult).then_inc(m.up("freed", unit.turns), 1)
                    dve.wait_ge(m.sem("freed"), m.count("freed", f0 + 2 * unit.u + (t + 1)))
                    split_in_place(m, dve, hi, lo, m.sig("actready"), unit.turns)

            m.walk(dve, segs[2 * half], up_unit, c, 4)
            m.walk(dve, segs[2 * half + 1], lambda unit: res[half].dve_unit(dve, unit))

    run_stage(m, dict(sp=sp, pe=pe, act=act, dve=dve, pool=pool))


def program(nc, d, vcols, nvec):
    ctx = ExitStack()
    with ctx:
        m = Machine(nc, ctx)
        vectors = ctx.enter_context(nc.sbuf_tensor("vectors", [P, nvec], F32))
        v = {n: vectors[:, o:o + c] for n, (o, c) in vcols.items()}
        S = {"lru_in": Segment(d["w_lru_in"], 10, 8, 2), "lru_out": Segment(d["w_lru_out"], 4, 8, 2)}
        for l in range(2):
            for half in range(2):
                S[f"up{l}{half}"] = Segment(d[f"w_up{l}{half}"], FF_HALF, 8, 2)
                S[f"down{l}{half}"] = Segment(d[f"w_down{l}{half}"], 8, FF_HALF, 1)
        ffn = lambda l: [S[f"{n}{l}{h}"] for h in range(2) for n in ("up", "down")]
        S["odd_in"], S["odd_f"] = Segment(d["w_odd_in"], 10, 8, 2), Segment(d["w_odd_f"], 1, 8, 1)
        S["odd_out"] = Segment(d["w_odd_out"], 4, 8, 2)
        order = [S["lru_in"], S["lru_out"]] + ffn(0) + [S["odd_in"], S["odd_f"], S["odd_out"]] + ffn(1)
        for g in range(2):
            S[f"gdn{g}"] = Segment(d[f"w_gdn{g}"], 6, 8, 2)
        S["bd"] = Segment(d["w_bd"], 1, 8, 1, cols=32)
        S["lat"] = Segment(d["w_lat"], 3, 8, 2)
        S["uqn"], S["uqr"] = Segment(d["w_uqn"], 4, 3, 2), Segment(d["w_uqr"], 2, 3, 2)
        S["ukn"], S["uv"] = Segment(d["w_ukn"], 4, 2, 2), Segment(d["w_uv"], 4, 2, 2)
        S["z"], S["gates"] = Segment(d["w_z"], 4, 8, 2), Segment(d["w_gates"], 8, 8, 2)
        S["branch"], S["out"] = Segment(d["w_branch"], 8, 8, 2), Segment(d["w_out"], 4, 8, 2)
        for half in range(2):
            S[f"mup{half}"] = Segment(d[f"w_mup{half}"], 8, 8, 2)
            S[f"mdown{half}"] = Segment(d[f"w_mdown{half}"], 8, 16, 1)
        two = [S[n] for n in ("gdn0", "bd", "gdn1", "lat", "uqn", "uqr", "ukn", "uv", "z", "gates", "branch",
                              "out", "mup0", "mdown0", "mup1", "mdown1")]
        order += two
        m.plan(order)
        gates_w = m.at(GATES_AT, 8, P)
        consts = [(m.ident[:, :], d["ident"]), (m.cum[:, :, :].rearrange("p a b -> p (a b)"), d["cum"]),
                  (m.bar[:, :, :].rearrange("p a b -> p (a b)"), d["bar"]),
                  (m.lev[:, :, :, :].rearrange("p a b c -> p (a b c)").bitcast(mybir.dt.uint16), d["lev"]),
                  (m.ones[:, :], d["ones"]), (vectors[:, :], d["vec"]),
                  (gates_w[:, :, :].rearrange("p a b -> p (a b)"), d["lru_gates"])]
        begin_stage(m, consts + [(m.h[:, :, :], d["xT"].rearrange("(k p) t -> p k t", p=P))])
        lru_stage(m, S["lru_in"], S["lru_out"], v, gates_w)
        ffn_stage(m, ffn(0), v["ffn_norm0"], v["ffn_taps0"], Modulation(m, d["w_mod"], d["cond"], 0))
        odd_in_stage(m, S["odd_in"], S["odd_f"], v,
                     [(m.at(SGU_W_AT, 1024), d["sgu_w"]), (m.at(SGU_B_AT, 512), d["sgu_b"]),
                      (m.at(SGU_N_AT, 512), d["sgu_n"])])
        fox_stage(m, v)
        out_stage(m, S["odd_out"], Y_AT)
        ffn_stage(m, ffn(1), v["ffn_norm1"], v["ffn_taps1"], Modulation(m, d["w_mod"], d["cond"], 1))
        renorm_stage(m, v["final_norm"], v["b_mod"])
        second(m, S, v, d)
        store_stage(m, d["out"])


def second(m, S, v, d):
    norm2_stage(m, v, d["ctxT"])
    for g in range(2):
        gdn_in_stage(m, S[f"gdn{g}"], S["bd"] if g == 0 else None, v, g)
        gdn_token_stage(m)
        gdn_scan_stage(m, g)
    mla_in_stage(m, S["lat"], v, [(m.at(COS_AT, 1280), d["rope"])])
    mla_heads_stage(m, [S["uqn"], S["uqr"], S["ukn"], S["uv"]], v)
    mla_norm_stage(m)
    mla_attend_stage(m)
    branch_stage(m, v)
    merge_stage(m, [S[n] for n in ("z", "gates", "branch", "out")], v)
    mlp_stage(m, [S[n] for n in ("mup0", "mdown0", "mup1", "mdown1")], v)


def columns(a):
    a = np.asarray(a)
    a = a.reshape(-1, a.shape[-1])
    return a.reshape(a.shape[0] * (a.shape[1] // P), P).T


def units_of(w, tile_order, k_tiles, tiles):
    w = np.asarray(w).reshape(k_tiles, P, -1, P)[:, :, tile_order]
    w = w.reshape(k_tiles, P, len(tile_order) // tiles, tiles, P)
    return np.ascontiguousarray(w.transpose(2, 1, 0, 3, 4)).reshape(len(tile_order) // tiles, P, -1)


def lay_out(a):
    f = {}
    vec = {}
    f["xT"] = np.ascontiguousarray(a["x"][0].T)
    xa, ga, c, b, vb = [list(range(4 * i, 4 * i + 4)) for i in range(5)]
    order = xa + ga + [t for pair in zip(c, vb) for t in pair] + b
    f["w_lru_in"] = units_of(a["mix0_w_in"][0], order, 8, 2)
    f["w_lru_out"] = units_of(a["mix0_w_out"][0], list(range(8)), 8, 2)
    bd = np.zeros((P, 8, P), a["lru_wa"].dtype)
    for g, w in enumerate(("lru_wa", "lru_wx")):
        for head in range(8):
            o = 64 * (head % 2)
            bd[o:o + 64, g * 4 + head // 2, o:o + 64] = a[w][0, head]
    f["lru_gates"] = bd.reshape(P, -1)
    for n in ("mix0_norm", "lru_conv_w", "lru_conv_b", "lru_ba", "lru_bx", "lru_lambda", "sconv_w", "sconv_b",
              "mix1_norm"):
        vec[n] = columns(a[n])
    nf = 2 * FF_HALF
    for l in range(2):
        order = [t for j in range(nf) for t in (j, nf + j)]
        up = units_of(a["ffn_up"][l], order, 8, 2)
        down = a["ffn_down"][l]
        for half in range(2):
            f[f"w_up{l}{half}"] = up[half * FF_HALF:(half + 1) * FF_HALF]
            f[f"w_down{l}{half}"] = units_of(down[half * FF_HALF * P:(half + 1) * FF_HALF * P], list(range(8)),
                                             FF_HALF, 1)
        taps = np.concatenate([a["ffn_conv_w"][l], a["ffn_conv_b"][l][None]]).reshape(4, 2 * nf, P)[:, order]
        vec[f"ffn_taps{l}"] = taps.transpose(2, 1, 0).reshape(P, -1)
        vec[f"ffn_norm{l}"] = columns(a["ffn_norm"][l])
    vec["final_norm"] = columns(a["final_norm"])
    w = a["mix1_w_in"][0]
    f["w_odd_in"] = units_of(w[:, :20 * P], [8, 9, 10, 11, 12, 13, 14, 15, 16, 17, 18, 19, 0, 1, 2, 3, 4, 5, 6, 7], 8, 2)
    gates = np.zeros((D, P), w.dtype)
    for o in (0, 8, 64, 72):
        gates[:, o:o + 8] = w[:, 20 * P:]
    f["w_odd_f"] = units_of(gates, [0], 8, 1)
    f["w_odd_out"] = units_of(a["mix1_w_out"][0], list(range(8)), 8, 2)
    bf = np.zeros((P, 1), w.dtype)
    for o in (0, 8, 64, 72):
        bf[o:o + 8, 0] = a["fox_bf"][0]
    vec["fox_bf"] = bf
    sel = np.zeros((P, 18), np.float32)
    sel[0:8, 0] = 1
    sel[8:16, 1] = -1
    for h in range(8):
        sel[8 + h, 2 + h] = 1
        sel[h, 10 + h] = 1
    sel[64:80] = sel[0:16]
    vec["fox_select"] = sel
    f["sgu_w"] = np.ascontiguousarray(a["sgu_w"][0].transpose(2, 0, 1)).reshape(P, -1)
    f["sgu_b"] = np.repeat(a["sgu_b"][0].reshape(4, 2, 1, P), 64, axis=2).reshape(4, P, P).transpose(1, 0, 2).reshape(P, -1)
    f["sgu_n"] = np.repeat(a["sgu_norm"][0][None], P, axis=0)
    f["ctxT"] = np.ascontiguousarray(a["ctx_2"][0].T)
    f["cond"] = np.repeat(np.concatenate([a["c_2"][0], a["c_ctx_2"]])[None], P, axis=0)
    f["w_mod"] = np.ascontiguousarray(a["w_mod_2"][0].T).reshape(48, P, D)
    vec["b_mod"] = columns(a["b_mod_2"])
    vec["norm_attn"], vec["norm_mlp"] = columns(a["norm_attn_2"]), columns(a["norm_mlp_2"])
    vec["conv_qkv"] = columns(a["conv_qkv_2"])
    vec["gdn_a_log"] = np.repeat(a["gdn_a_log_2"].reshape(1, 16), P, axis=0)
    vec["gdn_dt_bias"] = np.repeat(a["gdn_dt_bias_2"].reshape(1, 16), P, axis=0)
    w = a["w_in_2"][0]
    qkv, rest = w[:, :3072], w[:, 3072:]
    for g in range(2):
        f[f"w_gdn{g}"] = units_of(qkv, [8 * part + 4 * g + h for part in range(3) for h in range(4)], 8, 2)
    bd = rest[:, 1024:1056]
    lat = np.concatenate([rest[:, 1056:1696], rest[:, 1696:1760], rest[:, 1696:1760]], 1)
    f["w_lat"] = units_of(lat, list(range(6)), 8, 2)
    uq = a["w_uq_2"][0].reshape(384, 8, 192)
    f["w_uqn"] = units_of(uq[:, :, :128].reshape(384, 1024), list(range(8)), 3, 2)
    f["w_uqr"] = units_of(uq[:, :, 128:].reshape(384, 512), list(range(4)), 3, 2)
    ukv = a["w_ukv_2"][0].reshape(256, 8, 256)
    f["w_ukn"] = units_of(ukv[:, :, :128].reshape(256, 1024), list(range(8)), 2, 2)
    f["w_uv"] = units_of(ukv[:, :, 128:].reshape(256, 1024), list(range(8)), 2, 2)
    vec["q_a_norm"], vec["kv_a_norm"] = columns(a["mla_q_a_norm_2"]), columns(a["mla_kv_a_norm_2"])
    vec["out_norm"] = columns(a["gdn_out_norm_2"])
    for n in ("q_norm", "k_norm"):
        w2 = a[n + "_2"][0]
        vec[n + "_nope"] = w2[:128, None]
        vec[n + "_rope"] = np.concatenate([w2[128:], w2[128:]])[:, None]
    f["w_z"] = units_of(rest[:, 0:1024], list(range(8)), 8, 2)
    pairs = [t for i in range(8) for t in (i, 8 + i)]
    f["w_gates"] = units_of(rest[:, 1760:], pairs, 8, 2)
    f["w_branch"] = units_of(np.concatenate([a["w_branch_gdn_2"][0], a["w_branch_mla_2"][0]], 1), pairs, 8, 2)
    f["w_out"] = units_of(a["w_out_2"][0], list(range(8)), 8, 2)
    up, down = units_of(a["w_mlp_in_2"][0], list(range(32)), 8, 2), a["w_mlp_out_2"][0]
    for half in range(2):
        f[f"w_mup{half}"] = up[8 * half:8 * half + 8]
        f[f"w_mdown{half}"] = units_of(down[2048 * half:2048 * (half + 1)], list(range(8)), 16, 1)
    f["w_bd"] = np.ascontiguousarray(bd.reshape(8, P, 32).transpose(1, 0, 2)).reshape(1, P, 256)
    return f, vec


def shape_constants():
    i, j = np.arange(P)[:, None], np.arange(P)[None, :]
    f = {"ident": np.eye(P, dtype=np.float32)}
    f["cum"] = np.stack([i <= j, i >= j], 1).astype(np.float32).reshape(P, -1)
    f["bar"] = np.where(np.stack([i <= j, i >= j], 1), 0, -1e30).astype(np.float32).reshape(P, -1)
    lev = []
    for s in (1, 2, 4, 8, 16, 32, 64):
        lev.append((i // (2 * s) == j // (2 * s)) & (i // s > j // s))
    lev = np.stack(lev, 1)
    pos = np.arange(T)
    inv = 10000.0 ** (-np.arange(16, dtype=np.float32) / np.float32(16))
    ang = np.concatenate([(pos // 64)[None] * inv[:, None]] * 2 + [(pos % 64)[None] * inv[:, None]] * 2)
    ang = np.concatenate([ang, ang]).astype(np.float32)
    rot = np.zeros((P, P), np.float32)
    for b in range(0, P, 32):
        for r in range(16):
            rot[b + 16 + r, b + r] = -1
            rot[b + r, b + 16 + r] = 1
    sel = np.zeros((P, 16, 8), np.float32)
    for h in range(8):
        sel[:, h, h] = 1
        sel[64 * (h % 2):64 * (h % 2) + 64, 8 + h // 2, h] = 1
    sel[0:64, 12, :] = 1
    f["rope"] = np.concatenate([np.cos(ang), np.sin(ang), rot, sel.reshape(P, -1)], 1).astype(np.float32)
    f["lev"] = (np.stack([lev, np.transpose(lev, (2, 1, 0))], 1) * 0x3F80).astype(np.uint16).reshape(P, -1)
    return f


def kernel(**inputs):
    import concourse.bacc as bacc
    from concourse.bass_utils import run_bass_kernel_spmd

    f, vec = lay_out({name: np.asarray(value) for name, value in inputs.items()})
    f.update(shape_constants())
    f["ones"] = np.ones((P, 1), np.float32)
    vcols, n = {}, 0
    for name, value in vec.items():
        vcols[name] = (n, value.shape[1])
        n += value.shape[1]
    f["vec"] = np.concatenate(list(vec.values()), axis=1)
    nc = bacc.Bacc("TRN2", target_bir_lowering=False, num_devices=1)
    arrays, d = {}, {}
    for name, value in f.items():
        arrays["in_" + name] = value = np.ascontiguousarray(value)
        d[name] = nc.dram_tensor("in_" + name, value.shape, mybir.dt.from_np(value.dtype), kind="ExternalInput").ap()
    d["out"] = nc.dram_tensor("out", (D, T), F32, kind="ExternalOutput").ap()
    program(nc, d, vcols, n)
    result = run_bass_kernel_spmd(nc, [arrays], core_ids=[0])
    return np.ascontiguousarray(result.results[0]["out"].T)[None]
```
